# Optimizing a Trainium2 kernel written in Bass

```python
import jax, jax.numpy as jnp
from jax import lax
import numpy as np
import math

D_MODEL = 1024
BATCH = 1
SEQ = 512
DEPTH = 1

CHUNK = 64
SGU_BLOCK = 128
D_A = 1024
A_GROUPS = 8
A_GROUP_DIM = D_A // A_GROUPS
D_B = 1024
POOL_WINDOWS = (2, 4, 8, 16)
B_GROUPS = len(POOL_WINDOWS)
B_GROUP_DIM = D_B // B_GROUPS
D_C = 1024
CONV_WIDTH = 3
N_BRANCH = 3
SPLIT_SIZES = (D_A, D_A, D_A, D_B, D_B, D_C, D_C, D_C, D_C, N_BRANCH * D_MODEL)
N_IN = sum(SPLIT_SIZES)
SPLIT_OFFSETS = tuple(int(o) for o in np.cumsum(SPLIT_SIZES)[:-1])
RMS_EPS = 1e-6
LN_EPS = 1e-5


def rmsnorm(x, g):
    xf = x.astype(jnp.float32)
    y = xf * lax.rsqrt(jnp.mean(xf * xf, axis=-1, keepdims=True) + RMS_EPS)
    return (y * g.astype(jnp.float32)).astype(x.dtype)

def layernorm(x, g, b):
    xf = x.astype(jnp.float32)
    mu = jnp.mean(xf, axis=-1, keepdims=True)
    var = jnp.mean(jnp.square(xf - mu), axis=-1, keepdims=True)
    y = (xf - mu) * lax.rsqrt(var + LN_EPS)
    return (y * g.astype(jnp.float32) + b.astype(jnp.float32)).astype(x.dtype)

def chunk_causal_mask():
    c = jnp.arange(SGU_BLOCK) // CHUNK
    return c[None, :] <= c[:, None]

def spatial_gating(u, v, w_s, b_s, ln_g, ln_b):
    bsz, s, _ = v.shape
    v = layernorm(v, ln_g, ln_b)
    vb = v.reshape(bsz, s // SGU_BLOCK, SGU_BLOCK, A_GROUPS, A_GROUP_DIM)
    w = jnp.where(chunk_causal_mask()[None], w_s, jnp.zeros_like(w_s))
    mixed = jnp.einsum('gij,bnjgc->bnigc', w, vb) + b_s.T[:, :, None]
    return u * mixed.reshape(bsz, s, D_A)

def multiscale_pool(p, w_g, b_g, scale):
    bsz, s, _ = p.shape
    pf = p.astype(jnp.float32)
    csum = jnp.cumsum(pf, axis=1)
    pos1 = jnp.arange(1, s + 1, dtype=jnp.int32)
    outs = []
    for k, win in enumerate(POOL_WINDOWS):
        sl = slice(k * B_GROUP_DIM, (k + 1) * B_GROUP_DIM)
        cg = csum[..., sl]
        shifted = jnp.pad(cg, ((0, 0), (win, 0), (0, 0)))[:, :s]
        count = jnp.minimum(pos1, win).astype(jnp.float32)[:, None]
        outs.append((cg - shifted) / count - pf[..., sl])
    d = jnp.concatenate(outs, axis=-1).astype(p.dtype)
    d = d.reshape(bsz, s, B_GROUPS, B_GROUP_DIM)
    y = jnp.einsum('bsgc,gcd->bsgd', d, w_g).reshape(bsz, s, D_B) + b_g
    return y * scale

def causal_depthwise_conv(h, w, b):
    s = h.shape[1]
    hp = jnp.pad(h, ((0, 0), (CONV_WIDTH - 1, 0), (0, 0)))
    y = sum(w[k] * hp[:, k:k + s] for k in range(CONV_WIDTH))
    return y + b

def first_inputs(seed: int = 0) -> dict:
    key = jax.random.key(seed)
    ks = jax.random.split(key, 20)

    def nrm(k, shape, scale):
        return jax.random.normal(k, shape, jnp.float32) * scale

    L = DEPTH
    return {
        "x": nrm(ks[0], (BATCH, SEQ, D_MODEL), 1.0),
        "norm_g": 1.0 + nrm(ks[1], (L, D_MODEL), 0.05),
        "w_in": nrm(ks[2], (L, D_MODEL, N_IN), D_MODEL ** -0.5),
        "sgu_ln_g": 1.0 + nrm(ks[3], (L, D_A), 0.05),
        "sgu_ln_b": nrm(ks[4], (L, D_A), 0.02),
        "sgu_w": nrm(ks[5], (L, A_GROUPS, SGU_BLOCK, SGU_BLOCK), SGU_BLOCK ** -0.5),
        "sgu_b": 1.0 + nrm(ks[6], (L, A_GROUPS, SGU_BLOCK), 0.05),
        "pool_w": nrm(ks[7], (L, B_GROUPS, B_GROUP_DIM, B_GROUP_DIM), B_GROUP_DIM ** -0.5),
        "pool_b": nrm(ks[8], (L, D_B), 0.01),
        "pool_scale": 1.0 + nrm(ks[9], (L, D_B), 0.1),
        "conv_w": nrm(ks[10], (L, CONV_WIDTH, D_C), CONV_WIDTH ** -0.5),
        "conv_b": nrm(ks[11], (L, D_C), 0.01),
        "w_branch_a": nrm(ks[12], (L, D_A, D_MODEL), D_A ** -0.5),
        "w_branch_b": nrm(ks[13], (L, D_B, D_MODEL), D_B ** -0.5),
        "w_branch_c": nrm(ks[14], (L, D_C, D_MODEL), D_C ** -0.5),
        "w_out": nrm(ks[15], (L, D_MODEL, D_MODEL), D_MODEL ** -0.5),
        "final_g": 1.0 + nrm(ks[16], (D_MODEL,), 0.05),
    }

def first_block(x, norm_g, w_in, sgu_ln_g, sgu_ln_b, sgu_w, sgu_b, pool_w, pool_b,
              pool_scale, conv_w, conv_b, w_branch_a, w_branch_b, w_branch_c,
              w_out, final_g):
    bsz, s, _ = x.shape
    for l in range(DEPTH):
        h = rmsnorm(x, norm_g[l])
        proj = jnp.einsum('bsd,dn->bsn', h, w_in[l])
        a_u, a_v, a_z, b_p, b_z, c_h, c_b, c_c, c_z, gate_logits = jnp.split(
            proj, SPLIT_OFFSETS, axis=-1)

        ya = spatial_gating(jax.nn.gelu(a_u), jax.nn.gelu(a_v), sgu_w[l], sgu_b[l],
                            sgu_ln_g[l], sgu_ln_b[l]) * jax.nn.silu(a_z)
        yb = multiscale_pool(b_p, pool_w[l], pool_b[l], pool_scale[l]) * jax.nn.silu(b_z)
        yc = c_b * causal_depthwise_conv(c_c * c_h, conv_w[l], conv_b[l]) * jax.nn.silu(c_z)

        gates = jax.nn.sigmoid(gate_logits.reshape(bsz, s, N_BRANCH, D_MODEL))
        merged = (gates[:, :, 0] * jnp.einsum('bsc,cd->bsd', ya, w_branch_a[l])
                  + gates[:, :, 1] * jnp.einsum('bsc,cd->bsd', yb, w_branch_b[l])
                  + gates[:, :, 2] * jnp.einsum('bsc,cd->bsd', yc, w_branch_c[l]))
        x = x + jnp.einsum('bsd,de->bse', merged, w_out[l])
    return rmsnorm(x, final_g)


DEPTH_2 = 2

N_EVEN = (DEPTH_2 + 1) // 2
N_ODD = DEPTH_2 // 2
EPS = 1e-6

W_A = 1024
S5_GROUP = 16
S5_GROUPS = W_A // S5_GROUP
S5_STATE = 64
S5_DT_MIN = 1e-3
S5_DT_MAX = 1e-1
W_B = 1024
CONV_K = 31
EV_INNER = W_A + W_B
EV_IN = 2 * W_A + 3 * W_B

GLA_HEADS = 4
GLA_DV = 2048
GLA_DK = GLA_DV // 2
GLA_HK = GLA_DK // GLA_HEADS
GLA_HV = GLA_DV // GLA_HEADS
GLA_LOWRANK = 16
GLA_TAU = 16.0
GLA_CHUNK = 64
OD_IN = 2 * GLA_DK + 2 * GLA_DV + GLA_LOWRANK


def rms_norm(x, g):
    xf = x.astype(jnp.float32)
    y = xf * lax.rsqrt(jnp.mean(xf * xf, axis=-1, keepdims=True) + EPS)
    return (y * g.astype(jnp.float32)).astype(x.dtype)

def layer_norm(x, g, b):
    xf = x.astype(jnp.float32)
    mu = jnp.mean(xf, axis=-1, keepdims=True)
    xc = xf - mu
    y = xc * lax.rsqrt(jnp.mean(xc * xc, axis=-1, keepdims=True) + EPS)
    return (y * g.astype(jnp.float32) + b.astype(jnp.float32)).astype(x.dtype)

def s5_layer(u, lam_re, lam_im, log_dt, b_re, b_im, c_re, c_im, d):
    f32 = jnp.float32
    bsz, seq, _ = u.shape
    uf = u.astype(f32).reshape(bsz, seq, S5_GROUPS, S5_GROUP)
    lam = lax.complex(lam_re.astype(f32), lam_im.astype(f32))
    dt = jnp.exp(log_dt.astype(f32))[:, None]
    lam_bar = jnp.exp(lam * dt)
    b_mat = lax.complex(b_re.astype(f32), b_im.astype(f32))
    b_bar = ((lam_bar - 1.0) / lam)[..., None] * b_mat
    bu = jnp.einsum('gnp,blgp->blgn', b_bar, uf)
    a = jnp.broadcast_to(lam_bar, (1, seq) + lam_bar.shape)

    def combine(e1, e2):
        a1, b1 = e1
        a2, b2 = e2
        return a2 * a1, a2 * b1 + b2

    _, states = lax.associative_scan(combine, (a, bu), axis=1)
    c_mat = lax.complex(c_re.astype(f32), c_im.astype(f32))
    y = jnp.einsum('gpn,blgn->blgp', c_mat, states).real
    y = y + d.astype(f32).reshape(S5_GROUPS, S5_GROUP) * uf
    return y.reshape(bsz, seq, W_A).astype(u.dtype)

def conformer_conv(val, gate, w_dw, b_dw, ln_g, ln_b, w_pw, b_pw):
    h = val * jax.nn.sigmoid(gate)
    h = lax.conv_general_dilated(
        h, w_dw[:, None, :].astype(h.dtype), window_strides=(1,),
        padding=((CONV_K - 1, 0),), dimension_numbers=('NWC', 'WIO', 'NWC'),
        feature_group_count=W_B) + b_dw
    h = jax.nn.silu(layer_norm(h, ln_g, ln_b))
    return h @ w_pw + b_pw

def gla_chunked(q, k, v, g):
    bsz, seq, nh, dk = q.shape
    dv = v.shape[-1]
    nc = seq // GLA_CHUNK

    def chunks(t):
        return t.reshape(bsz, nc, GLA_CHUNK, nh, t.shape[-1]).transpose(1, 0, 3, 2, 4)

    qc, kc, vc = chunks(q), chunks(k), chunks(v)
    bc = jnp.cumsum(chunks(g), axis=3)
    causal = jnp.tril(jnp.ones((GLA_CHUNK, GLA_CHUNK), dtype=bool))

    def step(state, inp):
        qi, ki, vi, bi = inp
        b_last = bi[:, :, -1:, :]
        q_dec = qi * jnp.exp(bi)
        attn = jnp.einsum('bhik,bhjk->bhij', q_dec, ki * jnp.exp(-bi))
        attn = jnp.where(causal, attn, 0.0)
        o = (jnp.einsum('bhij,bhjv->bhiv', attn, vi)
             + jnp.einsum('bhik,bhkv->bhiv', q_dec, state))
        state = (jnp.exp(b_last[:, :, 0, :, None]) * state
                 + jnp.einsum('bhjk,bhjv->bhkv', ki * jnp.exp(b_last - bi), vi))
        return state, o

    s0 = jnp.zeros((bsz, nh, dk, dv), jnp.float32)
    _, o = lax.scan(step, s0, (qc, kc, vc, bc))
    return o.transpose(1, 0, 3, 2, 4).reshape(bsz, seq, nh, dv)

def gla_branch(p, w_gate_up, b_gate, norm_g):
    f32 = jnp.float32
    bsz, seq, _ = p.shape
    q, k, v, r, lr = jnp.split(
        p, [GLA_DK, 2 * GLA_DK, 2 * GLA_DK + GLA_DV, 2 * GLA_DK + 2 * GLA_DV], axis=-1)
    g = jax.nn.log_sigmoid((lr @ w_gate_up + b_gate).astype(f32)) / GLA_TAU

    def heads(t, dh):
        return t.astype(f32).reshape(bsz, seq, GLA_HEADS, dh)

    o = gla_chunked(heads(q, GLA_HK) * (GLA_HK ** -0.5), heads(k, GLA_HK),
                    heads(v, GLA_HV), heads(g, GLA_HK))
    o = rms_norm(o, norm_g)
    return o.reshape(bsz, seq, GLA_DV).astype(p.dtype) * jax.nn.silu(r)

def second_inputs(seed: int = 0) -> dict:
    key = jax.random.key(seed)
    ks = jax.random.split(key, 28)
    f32 = jnp.float32

    def nrm(k, shape, scale):
        return jax.random.normal(k, shape, f32) * scale

    NE, NO = N_EVEN, N_ODD
    n_idx = jnp.arange(S5_STATE, dtype=f32)
    return {
        "x": nrm(ks[0], (BATCH, SEQ, D_MODEL), 1.0),
        "norm_pre": 1.0 + nrm(ks[1], (DEPTH_2, D_MODEL), 0.05),
        "norm_post": 1.0 + nrm(ks[2], (DEPTH_2, D_MODEL), 0.05),
        "ev_w_in": nrm(ks[3], (NE, D_MODEL, EV_IN), D_MODEL ** -0.5),
        "s5_lambda_re": -0.5 + nrm(ks[4], (NE, S5_GROUPS, S5_STATE), 0.01),
        "s5_lambda_im": jnp.pi * n_idx + nrm(ks[5], (NE, S5_GROUPS, S5_STATE), 0.01),
        "s5_log_dt": jax.random.uniform(ks[6], (NE, S5_GROUPS), f32,
                                        minval=math.log(S5_DT_MIN), maxval=math.log(S5_DT_MAX)),
        "s5_b_re": nrm(ks[7], (NE, S5_GROUPS, S5_STATE, S5_GROUP), (2 * S5_GROUP) ** -0.5),
        "s5_b_im": nrm(ks[8], (NE, S5_GROUPS, S5_STATE, S5_GROUP), (2 * S5_GROUP) ** -0.5),
        "s5_c_re": nrm(ks[9], (NE, S5_GROUPS, S5_GROUP, S5_STATE), S5_STATE ** -0.5),
        "s5_c_im": nrm(ks[10], (NE, S5_GROUPS, S5_GROUP, S5_STATE), S5_STATE ** -0.5),
        "s5_d": nrm(ks[11], (NE, W_A), 1.0),
        "s5_w_glu": nrm(ks[12], (NE, W_A, W_A), W_A ** -0.5),
        "s5_b_glu": nrm(ks[13], (NE, W_A), 0.02),
        "conv_w": nrm(ks[14], (NE, CONV_K, W_B), CONV_K ** -0.5),
        "conv_b": nrm(ks[15], (NE, W_B), 0.02),
        "conv_ln_g": 1.0 + nrm(ks[16], (NE, W_B), 0.05),
        "conv_ln_b": nrm(ks[17], (NE, W_B), 0.02),
        "conv_w_pw": nrm(ks[18], (NE, W_B, W_B), W_B ** -0.5),
        "conv_b_pw": nrm(ks[19], (NE, W_B), 0.02),
        "ev_w_out": nrm(ks[20], (NE, EV_INNER, D_MODEL), EV_INNER ** -0.5),
        "od_w_in": nrm(ks[21], (NO, D_MODEL, OD_IN), D_MODEL ** -0.5),
        "gla_w_gate_up": nrm(ks[22], (NO, GLA_LOWRANK, GLA_DK), GLA_LOWRANK ** -0.5),
        "gla_b_gate": nrm(ks[23], (NO, GLA_DK), 0.1),
        "gla_norm_g": 1.0 + nrm(ks[24], (NO, GLA_HV), 0.05),
        "od_w_out": nrm(ks[25], (NO, GLA_DV, D_MODEL), GLA_DV ** -0.5),
    }

def second_block(x, norm_pre, norm_post, ev_w_in, s5_lambda_re, s5_lambda_im, s5_log_dt,
              s5_b_re, s5_b_im, s5_c_re, s5_c_im, s5_d, s5_w_glu, s5_b_glu,
              conv_w, conv_b, conv_ln_g, conv_ln_b, conv_w_pw, conv_b_pw, ev_w_out,
              od_w_in, gla_w_gate_up, gla_b_gate, gla_norm_g, od_w_out):
    for i in range(DEPTH_2):
        u = rms_norm(x, norm_pre[i])
        if i % 2 == 0:
            j = i // 2
            p = u @ ev_w_in[j]
            a_in, a_z, b_val, b_gate, b_z = jnp.split(
                p, [W_A, 2 * W_A, 2 * W_A + W_B, 2 * W_A + 2 * W_B], axis=-1)
            ya = s5_layer(a_in, s5_lambda_re[j], s5_lambda_im[j], s5_log_dt[j],
                          s5_b_re[j], s5_b_im[j], s5_c_re[j], s5_c_im[j], s5_d[j])
            ya = jax.nn.gelu(ya)
            ya = ya * jax.nn.sigmoid(ya @ s5_w_glu[j] + s5_b_glu[j])
            ya = ya * jax.nn.silu(a_z)
            yb = conformer_conv(b_val, b_gate, conv_w[j], conv_b[j], conv_ln_g[j],
                                conv_ln_b[j], conv_w_pw[j], conv_b_pw[j])
            yb = yb * jax.nn.silu(b_z)
            y = jnp.concatenate([ya, yb], axis=-1) @ ev_w_out[j]
        else:
            j = i // 2
            p = u @ od_w_in[j]
            y = gla_branch(p, gla_w_gate_up[j], gla_b_gate[j], gla_norm_g[j]) @ od_w_out[j]
        x = x + rms_norm(y, norm_post[i])
    return x


def setup_inputs(seed=0):
    out = dict(first_inputs(seed))
    for name, value in second_inputs(seed + 1).items():
        if name != "x":
            out[name + "_2"] = value
    return out


def reference(
    x, norm_g, w_in, sgu_ln_g, sgu_ln_b, sgu_w, sgu_b, pool_w, pool_b, pool_scale, conv_w,
    conv_b, w_branch_a, w_branch_b, w_branch_c, w_out, final_g, norm_pre_2, norm_post_2,
    ev_w_in_2, s5_lambda_re_2, s5_lambda_im_2, s5_log_dt_2, s5_b_re_2, s5_b_im_2, s5_c_re_2,
    s5_c_im_2, s5_d_2, s5_w_glu_2, s5_b_glu_2, conv_w_2, conv_b_2, conv_ln_g_2, conv_ln_b_2,
    conv_w_pw_2, conv_b_pw_2, ev_w_out_2, od_w_in_2, gla_w_gate_up_2, gla_b_gate_2,
    gla_norm_g_2, od_w_out_2,
):
    x = first_block(
        x, norm_g, w_in, sgu_ln_g, sgu_ln_b, sgu_w, sgu_b, pool_w, pool_b, pool_scale, conv_w,
        conv_b, w_branch_a, w_branch_b, w_branch_c, w_out, final_g,
    )
    return second_block(
        x, norm_pre_2, norm_post_2, ev_w_in_2, s5_lambda_re_2, s5_lambda_im_2, s5_log_dt_2,
        s5_b_re_2, s5_b_im_2, s5_c_re_2, s5_c_im_2, s5_d_2, s5_w_glu_2, s5_b_glu_2, conv_w_2,
        conv_b_2, conv_ln_g_2, conv_ln_b_2, conv_w_pw_2, conv_b_pw_2, ev_w_out_2, od_w_in_2,
        gla_w_gate_up_2, gla_b_gate_2, gla_norm_g_2, od_w_out_2,
    )


_drawn_inputs = setup_inputs


def setup_inputs(seed=0):
    import zlib

    import numpy as np

    out = dict(_drawn_inputs(seed))
    spreads = {}
    factors = {'sgu_ln_g': 4.017,
     'sgu_ln_b': 8.0,
     'sgu_b': 3.22,
     'pool_b': 8.0,
     'conv_b': 8.0,
     's5_lambda_re_2': 200.0,
     's5_b_glu_2': 8.0,
     'conv_ln_b_2': 3.204,
     's5_lambda_im_2': 28.376,
     's5_log_dt_2': 30.528,
     's5_b_re_2': 38.88,
     's5_b_im_2': 39.656,
     's5_c_re_2': 39.024,
     's5_c_im_2': 38.84}
    for name, (base, spread) in spreads.items():
        noise = np.random.default_rng([zlib.crc32(name.encode()), seed]).standard_normal(out[name].shape)
        drawn = base * np.exp(spread * noise) if base else spread * noise
        out[name] = __import__('jax').numpy.asarray(drawn.astype(out[name].dtype))
    for name, factor in factors.items():
        out[name] = (out[name] * factor).astype(out[name].dtype)
    return out
```

```python
from contextlib import ExitStack

import numpy as np
import concourse.bass as bass
from concourse import mybir

F32 = mybir.dt.float32
F32R = mybir.dt.float32r
U32 = mybir.dt.uint32
ALU = mybir.AluOpType
ACT = mybir.ActivationFunctionType

P = 128
SEQ = 512
D = 1024
KT = D // P
TT = SEQ // P
NC = 512
RING = 4
SGU_GROUPS = 8
CHUNK = 64
POOL_WINDOWS = (2, 4, 8, 16)
PPAD = 16
CONV_K = 31
CPAD = CONV_K - 1
RMS_EPS = 1e-6
LN_EPS = 1e-5
S5_GROUP = 16
S5_STATE = 64
T4 = 4
NCH = SEQ // T4
PAIRS = D // (2 * S5_GROUP)
HEADS = 4
HK = 256
HV = 512
LOWRANK = 16
GLA_TAU = 16.0
GCH = SEQ // CHUNK

TWO_PI = 2.0 * np.pi
PI_A = 6.28125
PI_B = float(np.float32(np.floor((TWO_PI - PI_A) * 2 ** 21) / 2 ** 21))
PI_C = float(np.float32(TWO_PI - PI_A - PI_B))
ROUND = 12582912.0

VEC = {n: i for i, n in enumerate(
    ["norm_g", "pool_b", "pool_scale", "conv_w0", "conv_w1", "conv_w2", "conv_b", "norm_pre0", "norm_pre1",
     "b_glu", "conv_b_2", "ln_g2", "ln_b2", "b_pw", "gla_norm_g"])}
VEC_CONV = 16
N_VEC = VEC_CONV + CONV_K

JOBS = []


def _add(name, chunks=0, side=0, a=0, d=0, lo=None):
    JOBS.append((name, chunks, side, a, d, lo))


def _section(name, a=0, d=0, chunks=4):
    for u in range(2):
        _add(f"{name}.{u}", chunks, 0, a, d)


_add("params", side=1, a=3)
_add("h_t.0", side=4, lo=("h", 4))
_add("h_t.1", side=4, lo=("h", 8))
_section("a_v", a=4)
_section("a_u", a=4)
_add("c_t", side=1, a=2)
_section("a_z", a=4)
for _i in range(4):
    _add(f"w_t.{_i}", side=1, a=2, d=2)
_add("sgu_t", side=1, a=2)
for _i in range(2):
    _add(f"k.{_i}", side=1, d=4)
_section("g0", a=4)
for _i in range(2):
    _add(f"sgu.{_i}", side=1, d=4)
_section("b_p", a=4)
_section("w_a", d=4)
_section("b_z", a=4)
for _i in range(2):
    _add(f"pool.{_i}", side=1, d=4)
_section("g1", a=4)
_section("c_h", a=4)
_section("w_b", d=4)
_section("c_c", d=4)
_section("g2", a=4)
_section("c_b", d=4)
_section("c_z", a=4)
_section("w_c", d=4)
_section("w_out", d=4)
_add("u_t.0", side=4, lo=("h", 20))
_add("u_t.1", side=4, lo=("h", 24))
_section("b_val", a=4)
_section("b_gate", a=4)
for _u in range(2):
    _add(f"a_in.{_u}", 4, 0, 4, 0)
for _u in range(2):
    _add(f"s5_t.{_u}", side=1, a=4)
for _i in range(8):
    _add(f"s5_z.{_i}", side=1, a=4)
_section("a_z2", a=4)
_section("b_z2", a=4)
for _i in range(2):
    _add(f"s5_y.{_i}", side=1, a=4)
for _i in range(2):
    _add(f"y_t.{_i}", side=4, lo=("y", 8 * 3 + 4 * (_i + 1)))
_add("mean", side=1, d=1)
_section("glu", a=4)
_add("var", a=1)
_section("pw", d=4)
_section("ev_out", a=4, chunks=8)
_add("u2_t.0", side=4, lo=("h", 36))
_add("u2_t.1", side=4, lo=("h", 40))
_add("lr", a=1)
NAMES = [j[0] for j in JOBS]


def _sum(column, upto):
    return sum(j[column] for j in JOBS[:upto])


def chunks_before(name):
    return _sum(1, NAMES.index(name))


def used_after(name):
    return _sum(1, NAMES.index(name) + 1)


def side_after(name, k=0):
    i = NAMES.index(name)
    return _sum(2, i) + (k if k else JOBS[i][2])


def act_after(name, k=0):
    i = NAMES.index(name)
    return _sum(3, i) + (k if k else JOBS[i][3])


def dve_after(name, k=0):
    i = NAMES.index(name)
    return _sum(4, i) + (k if k else JOBS[i][4])


UNITS = [j[0] for j in JOBS if j[1]]
N_STATIC = _sum(1, len(JOBS))
HEAD_CHUNKS = 16

HDVE, HACT, HST, HD0, HS0 = 18, 14, 13, 5, 1
HSEQ_ACT, HSEQ_DVE = 4, 1
HS_D, HS_I = {0: HS0 + 4}, {}
_n = HS0 + 4
for _c in range(GCH):
    if _c + 1 < GCH - 1:
        _n += 1
        HS_D[_c + 1] = _n
    if _c:
        _n += 1
        HS_I[_c] = _n
HS_O = [HS_I[2 * _t + 1] for _t in range(TT)]
HS_OT = [_n + _m + 1 for _m in range(4)]
HSIDE = _n + 4 - HS0


def st_after(c):
    return 1 + 2 * c


W_IN = {n: i * D for i, n in enumerate(
    ["a_u", "a_v", "a_z", "b_p", "b_z", "c_h", "c_b", "c_c", "c_z", "g0", "g1", "g2"])}
EV_IN = {n: i * D for i, n in enumerate(["a_in", "a_z2", "b_val", "b_gate", "b_z2"])}


class Order:

    def __init__(self, eng, sem):
        self.eng, self.sem, self.n, self.base = eng, sem, 0, 0

    def inc(self, instruction):
        instruction.then_inc(self.sem, 1)
        self.n += 1
        return self.n

    def wait(self, n=None):
        self.eng.wait_ge(self.sem, self.base + (self.n if n is None else n))


def three_branch_s5_gla_kernel(nc, a, out):
    ctx = ExitStack()
    with ctx:
        def sem(name):
            return ctx.enter_context(nc.semaphore(name))

        at = {}
        start = nc.sbuf_base + -nc.sbuf_base % 32

        def region(name, size):
            at[name] = region.top
            region.top += size
        region.top = start
        for name, size in (("WR", 16384), ("WH", 16384), ("WL", 16384), ("HH", 16384), ("HL", 16384),
                           ("YH", 16384), ("YL", 16384), ("R1", 17344), ("R2", 16384), ("R3", 16384),
                           ("R4", 16384), ("R5", 16384), ("R6", 8192), ("ident", 512), ("PRM", 4 * 8 * N_VEC),
                           ("TMP", 4096), ("LAM", 384), ("SMALL", 376)):
            region(name, size)
        ctx.enter_context(nc.sbuf_tensor("arena", [P, (region.top - nc.sbuf_base + 3) // 4], F32))

        def put(name, where, shape, dt=F32, skip=0):
            return nc.alloc_sbuf_tensor_at(name, [P, *shape], dt, offset=at[where] + skip, align_bytes=4)

        WR = put("WR", "WR", [RING, 2, NC])
        WH = put("WH", "WH", [RING, 2, NC], F32R)
        WL = put("WL", "WL", [RING, 2, NC], F32R)
        HH = put("HH", "HH", [KT, SEQ], F32R)
        HL = put("HL", "HL", [KT, SEQ], F32R)
        YH = put("YH", "YH", [KT, SEQ], F32R)
        YL = put("YL", "YL", [KT, SEQ], F32R)
        ident = put("ident", "ident", [P])
        PRM = put("PRM", "PRM", [8 * N_VEC])
        TMP = put("TMP", "TMP", [2, NC])
        XN0 = put("XN0", "R1", [TT, D])
        V = put("V", "R1", [TT, D])
        CH = put("CH", "R1", [KT, PPAD + SEQ])
        U = put("U", "R2", [KT, SEQ])
        X = put("X", "R3", [TT, D])
        WIN = put("WIN", "R3", [3, PPAD + SEQ])
        M = put("M", "R4", [KT, SEQ])
        XN1 = put("XN1", "R4", [TT, D])
        G = put("G", "R5", [KT, SEQ])
        LNROWS = put("LNROWS", "R5", [2, D])
        SGW = put("SGW", "R5", [SGU_GROUPS, P], skip=8192)
        SGWT = put("SGWT", "R6", [SGU_GROUPS, P])
        SGB = put("SGB", "R6", [SGU_GROUPS, P], skip=4096)
        PW = put("PW", "R6", [4, 2, 256])
        FROW = put("FROW", "R6", [D])
        PR = put("PR", "R6", [3, P])
        GRE = put("GRE", "YH", [PAIRS, 5, S5_GROUP])
        GNI = put("GNI", "YH", [PAIRS, 5, S5_GROUP], skip=10240)
        TM = put("TM", "YH", [PAIRS, 64], skip=20480)
        CRAW = put("CRAW", "YH", [2, 4, P], skip=28672)
        WST = put("WST", "R4", [2, PAIRS, T4, S5_GROUP])
        BRAW = put("BRAW", "R5", [2, PAIRS, S5_GROUP], skip=12288)
        WTS = put("WTS", "R3", [2, PAIRS, 64])
        PT = put("PT", "R3", [2, PAIRS, S5_GROUP])
        DT2 = put("DT2", "R3", [PAIRS, 64], skip=4096)
        LS = put("LS", "R6", [20, PAIRS], skip=1536)
        LAM = put("LAM", "LAM", [3, PAIRS])
        DCOL = put("DCOL", "SMALL", [PAIRS])
        INVC = put("INVC", "SMALL", [PPAD], skip=128)
        MJ = put("MJ", "SMALL", [4], skip=192)
        MJ8 = put("MJ8", "SMALL", [2, 4], skip=208)
        ST1 = put("ST1", "SMALL", [2, PAIRS])
        ST2 = put("ST2", "PRM", [2, PAIRS])
        STAT = put("STAT", "SMALL", [4, 4], skip=272)
        BNA = put("BNA", "SMALL", [4, 2], skip=336)
        EPS = put("EPS", "SMALL", [2], skip=368)
        BNS = put("BNS", "TMP", [TT, 2, 6])
        CP = put("CP", "R1", [KT, CPAD + SEQ])
        UT = put("UT", "R2", [PAIRS, NCH])
        YA = put("YA", "R2", [KT, SEQ])
        WT = put("WT", "R3", [2, PAIRS, 64])
        VT = put("VT", "R3", [2, PAIRS, 64])
        X1 = put("X1", "R3", [TT, D])
        AS = put("AS", "R4", [2, 32, T4, S5_GROUP])
        AZ = put("AZ", "R4", [KT, SEQ])
        BZ = put("BZ", "R5", [KT, SEQ])
        XN2 = put("XN2", "R5", [TT, D])
        T6 = put("T6", "R6", [PAIRS, 64])
        MU = put("MU", "R6", [SEQ])
        RS = put("RS", "R6", [SEQ], skip=2048)
        ONES = put("ONES", "R6", [P], skip=4096)
        PROW0 = put("PROW0", "R6", [D], skip=4096)
        S = put("S", "YH", [2, PAIRS, NCH])
        YT = put("YT", "HH", [T4, D])
        YO = put("YO", "R1", [TT, D])
        YO2 = put("YO2", "R2", [TT, D])
        QK = put("QK", "R1", [4, SEQ])
        BC = put("BC", "R1", [2, SEQ], skip=8192)
        ET = put("ET", "R1", [2, SEQ], skip=12288)
        LWR = put("LWR", "R4", [KT, LOWRANK], skip=8192)
        LWH = put("LWH", "R4", [KT, P], F32R)
        LWL = put("LWL", "R4", [KT, P], F32R, skip=4096)
        QD = put("QD", "R4", [2, SEQ])
        KE = put("KE", "R4", [2, SEQ], skip=4096)
        KDC = put("KDC", "R4", [2, SEQ], skip=8192)
        KTK = put("KTK", "R4", [TT, 2, P], skip=12288)
        PROW1 = put("PROW1", "R4", [D])
        V2 = put("V2", "R5", [TT, HV])
        RR = put("RR", "R5", [4, SEQ], skip=8192)
        ATS = put("ATS", "R6", [TT, P])
        CMASK = put("CMASK", "R6", [P], skip=2048)
        SMASK = put("SMASK", "R6", [2 * SEQ], skip=2560)
        GU = put("GU", "R6", [HK], skip=6656)
        LR = put("LR", "TMP", [SEQ])
        DEC = put("DEC", "TMP", [2, GCH], skip=2048)
        OH = put("OH", "YH", [4, SEQ], F32R)
        OL = put("OL", "YH", [4, SEQ], F32R, skip=8192)
        ST = put("ST", "YL", [2, 2, HV])
        ON = put("ON", "YL", [TT, HV], skip=8192)

        PS = ctx.enter_context(nc.psum_tensor("PS", [P, 8, NC], F32))

        def bank(name, m):
            return PS[:, 4 * (NAMES.index(name) % 2) + m, :]

        d_wt = nc.dram_tensor("d_wt", [P, 2 * PAIRS * 64], F32, kind="Internal").ap()
        d_g = nc.dram_tensor("d_g", [P, 2, PAIRS, 64], F32, kind="Internal").ap()
        d_tm = nc.dram_tensor("d_tm", [P, PAIRS * 64], F32, kind="Internal").ap()
        d_x1 = nc.dram_tensor("d_x1", [SEQ, D], F32, kind="Internal").ap()

        w_loaded = [sem(f"w_loaded{i}") for i in range(RING)]
        w_hi, w_lo, weights_used = sem("w_hi"), sem("w_lo"), sem("weights_used")
        banks_act, banks_dve, side_done = sem("banks_act"), sem("banks_dve"), sem("side_done")
        act_seq, dve_seq, pool_seq = sem("act_seq"), sem("dve_seq"), sem("pool_seq")
        h_hi, h_lo, y_hi, y_lo = sem("h_hi"), sem("h_lo"), sem("y_hi"), sem("y_lo")
        x_in, prm_in, lam_in, c_in, b_in, sg_in, ln_in, d_in, bs_in = (sem(n) for n in (
            "x_in", "prm_in", "lam_in", "c_in", "b_in", "sg_in", "ln_in", "d_in", "bs_in"))
        pw_in, x_again, frow_in, wt_in, vt_in, t6_in, x1_out, x1_in, prow0_in = (sem(n) for n in (
            "pw_in", "x_again", "frow_in", "wt_in", "vt_in", "t6_in", "x1_out", "x1_in", "prow0_in"))
        s5_out = sem("s5_out")
        consts = sem("consts")
        sq0, std0, xn0 = sem("sq0"), sem("std0"), sem("xn0")
        v_std, v_done = sem("v_std"), sem("v_done")
        m_acc, sq_used, ke_done = sem("m_acc"), sem("sq_used"), sem("ke_done")
        lam_exp, lam_ang, lam_sin, lam_den, lam_rec = (sem(n) for n in (
            "lam_exp", "lam_ang", "lam_sin", "lam_den", "lam_rec"))
        pool_g, pool_w, pool_t = sem("pool_g"), sem("pool_w"), sem("pool_t")
        pool_rep = sem("pool_rep")
        sgw_masked = sem("sgw_masked")
        tmp_free = sem("tmp_free")
        ya_ready, d_ready, yb_ready, pads = sem("ya_ready"), sem("d_ready"), sem("yb_ready"), sem("pads")
        cpads = sem("cpads")
        x1_done, xn1, sq1, std1, sq2, std2 = (sem(n) for n in (
            "x1_done", "xn1", "sq1", "std1", "sq2", "std2"))
        states, conv_done = sem("states"), sem("conv_done")
        ya_final, z_cent, z_sq, z_norm, z_act, ones_in = (sem(n) for n in (
            "ya_final", "z_cent", "z_sq", "z_norm", "z_act", "ones_in"))
        sq3, std3, x2_done, sq4, std4, xn2 = (sem(n) for n in ("sq3", "std3", "x2_done", "sq4", "std4", "xn2"))
        lw_in, lw_zero, lw_hi, lw_lo, gla_consts, y2_zero = (sem(n) for n in (
            "lw_in", "lw_zero", "lw_hi", "lw_lo", "gla_consts", "y2_zero"))
        gu_in = sem("gu_in")
        e_abs, g_scan, e_q, e_ke, e_d, dec_in, qd_done, kd_done = (sem(n) for n in (
            "e_abs", "g_scan", "e_q", "e_ke", "e_d", "dec_in", "qd_done", "kd_done"))
        hd_side, hd_act, hd_dve = sem("hd_side"), sem("hd_act"), sem("hd_dve")
        o_sq, o_std, o_f, o_hi, o_lo, rr_in, st_done = (sem(n) for n in (
            "o_sq", "o_std", "o_f", "o_hi", "o_lo", "rr_in", "st_done"))
        sq5, std5, fin, fin_out, prow1_in = sem("sq5"), sem("std5"), sem("fin"), sem("fin_out"), sem("prow1_in")

        def col(name, kt, n=1):
            c = 8 * VEC[name] + kt
            return PRM[:, c:c + n]

        def tokens(dram):
            return dram.rearrange("(t p) d -> p t d", p=P)

        x_d = tokens(a["x"][0])
        ctx.enter_context(nc.allow_non_contiguous_dma(reason="small S5 tables, loaded once"))
        block = ctx.enter_context(nc.Block())

        @block.sync
        def _(sp):
            sp.dma_start(X[:, :, :], x_d).then_inc(x_in, 16)

            def chunk(n, src, first=False):
                slot = n % RING
                if n >= RING:
                    sp.wait_ge(w_lo, n - RING + 1)
                sp.dma_start(WR[:, slot, :, :], src.rearrange("(k p) n -> p k n", p=P)).then_inc(w_loaded[slot], 16)

            def section(name, src, col0, rows=D):
                n0 = chunks_before(name + ".0")
                per = rows // (2 * P)
                if n0 < RING:
                    for u in range(2):
                        for q in range(per):
                            chunk(n0 + u * per + q, src[q * 2 * P:(q + 1) * 2 * P, col0 + u * NC:col0 + (u + 1) * NC])
                    return
                with sp.Fori(0, 2) as u:
                    for q in range(per):
                        slot = q % RING
                        sp.wait_ge(w_lo, u * per + (n0 + q - RING + 1))
                        sp.dma_start(WR[:, slot, :, :],
                                     src[q * 2 * P:(q + 1) * 2 * P, bass.ds(u * NC + col0, NC)]
                                     .rearrange("(k p) n -> p k n", p=P)).then_inc(w_loaded[slot], 16)

            w_in, ev_in = a["w_in"][0], a["ev_w_in_2"][0]
            section("a_v", w_in, W_IN["a_v"])
            for i, name in enumerate(("s5_c_re_2", "s5_c_im_2")):
                for t in range(4):
                    for r in range(8):
                        sp.dma_start(CRAW[16 * r:16 * r + 16, i, t, :].rearrange("p (g n) -> p g n", g=2),
                                     a[name][0, 16 * t + 2 * r:16 * t + 2 * r + 2].rearrange("g p n -> p g n")).then_inc(c_in, 16)
            section("a_u", w_in, W_IN["a_u"])
            section("a_z", w_in, W_IN["a_z"])
            sp.wait_ge(pool_g, 1)
            sp.dma_start(d_g[:, 0, :, :], GRE[:, :, 1:5, :].rearrange("p r t q -> p r (t q)")).then_inc(s5_out, 16)
            sp.dma_start(d_g[:, 1, :, :], GNI[:, :, 1:5, :].rearrange("p r t q -> p r (t q)")).then_inc(s5_out, 16)
            section("g0", w_in, W_IN["g0"])
            sp.wait_ge(banks_act, act_after("w_t.3"))
            sp.wait_ge(banks_dve, dve_after("w_t.3"))
            sp.dma_start(d_wt, WTS[:, :, :, :].rearrange("p r g n -> p (r g n)")).then_inc(s5_out, 16)
            sp.wait_ge(banks_dve, dve_after("k.1"))
            sp.dma_start(d_tm, TM[:, :, :].rearrange("p g n -> p (g n)")).then_inc(s5_out, 16)
            section("b_p", w_in, W_IN["b_p"])
            sp.wait_ge(side_done, side_after("sgu.1"))
            sp.wait_ge(ya_ready, 8)
            sp.dma_start(PW[:, :, :, :], a["pool_w"][0].rearrange("g (k p) d -> p g k d", p=P)).then_inc(pw_in, 16)
            section("w_a", a["w_branch_a"][0], 0)
            section("b_z", w_in, W_IN["b_z"])
            section("g1", w_in, W_IN["g1"])
            sp.wait_ge(d_ready, 4)
            sp.wait_ge(s5_out, 64)
            sp.dma_start(X[:, :, :], x_d).then_inc(x_again, 16)
            section("c_h", w_in, W_IN["c_h"])
            sp.wait_ge(side_done, side_after("pool.1"))
            sp.dma_start(FROW[:, :], a["final_g"].rearrange("(o n) -> o n", o=1).broadcast_to([P, D])).then_inc(frow_in, 16)
            section("w_b", a["w_branch_b"][0], 0)
            for name in ("c_c", "g2", "c_b", "c_z"):
                section(name, w_in, W_IN[name])
            section("w_c", a["w_branch_c"][0], 0)
            section("w_out", a["w_out"][0], 0)
            section("b_val", ev_in, EV_IN["b_val"])
            sp.wait_ge(x1_done, 4)
            sp.dma_start(tokens(d_x1), X[:, :, :]).then_inc(x1_out, 16)
            sp.dma_start(T6[:, :, :].rearrange("p g n -> p (g n)"), d_tm).then_inc(t6_in, 16)
            sp.wait_ge(x1_out, 16)
            sp.wait_ge(xn1, 4)
            sp.dma_start(WT[:, :, :, :].rearrange("p r g n -> p (r g n)"), d_wt).then_inc(wt_in, 16)
            section("b_gate", ev_in, EV_IN["b_gate"])
            section("a_in", ev_in, EV_IN["a_in"])
            section("a_z2", ev_in, EV_IN["a_z2"])
            sp.wait_ge(side_done, side_after("s5_z.7"))
            sp.dma_start(VT[:, :, :, :].rearrange("p r g n -> p r (g n)"),
                         d_g.rearrange("p r g n -> p r (g n)")).then_inc(vt_in, 16)
            section("b_z2", ev_in, EV_IN["b_z2"])
            section("glu", a["s5_w_glu_2"][0], 0)
            sp.wait_ge(side_done, side_after("s5_y.1"))
            sp.dma_start(X1[:, :, :], tokens(d_x1)).then_inc(x1_in, 16)
            section("pw", a["conv_w_pw_2"][0], 0)
            sp.wait_ge(sq_used, KT)
            sp.dma_start(PROW0[:, :], a["norm_post_2"][0:1, :].broadcast_to([P, D])).then_inc(prow0_in, 16)
            section("ev_out", a["ev_w_out_2"][0], 0, 2 * D)
            od_in, od_out = a["od_w_in_2"][0], a["od_w_out_2"][0]
            with sp.Fori(0, HEADS) as h:
                def head_chunk(j, pieces):
                    slot = j % RING
                    sp.wait_ge(w_lo, h * HEAD_CHUNKS + (N_STATIC + j - RING + 1))
                    for c0, width, src in pieces:
                        sp.dma_start(WR[:, slot, :, c0:c0 + width],
                                     src.rearrange("(k p) n -> p k n", p=P)).then_inc(w_loaded[slot], 16)
                for q in range(4):
                    rows = od_in[q * 2 * P:(q + 1) * 2 * P, :]
                    head_chunk(q, [(0, HK, rows[:, bass.ds(h * HK, HK)]),
                                   (HK, HK, rows[:, bass.ds(h * HK + HEADS * HK, HK)])])
                for q in range(4):
                    rows = od_in[q * 2 * P:(q + 1) * 2 * P, :]
                    head_chunk(4 + q, [(0, HV, rows[:, bass.ds(h * HV + 2 * HEADS * HK, HV)])])
                for q in range(4):
                    rows = od_in[q * 2 * P:(q + 1) * 2 * P, :]
                    head_chunk(8 + q, [(0, HV, rows[:, bass.ds(h * HV + 2 * HEADS * HK + HEADS * HV, HV)])])
                for u in range(2):
                    for q in range(2):
                        head_chunk(12 + 2 * u + q,
                                   [(0, NC, od_out[bass.ds(h * HV + q * 2 * P, 2 * P), u * NC:(u + 1) * NC])])
            sp.wait_ge(hd_side, HS0 + HEADS * HSIDE)
            sp.dma_start(PROW1[:, :], a["norm_post_2"][1:2, :].broadcast_to([P, D])).then_inc(prow1_in, 16)
            sp.wait_ge(fin, 4)
            sp.dma_start(tokens(out[0]), YO2[:, :, :]).then_inc(fin_out, 16)
            sp.wait_ge(fin_out, 16)

        @block.gpsimd
        def _(pool):
            seq = Order(pool, pool_seq)
            seq.inc(pool.memset(ident[:, :], 0.0))
            seq.inc(pool.memset(MJ8[:, :, :], 1.0))
            pool.memset(EPS[:, 0:1], RMS_EPS).then_inc(consts, 1)
            pool.memset(EPS[:, 1:2], LN_EPS).then_inc(consts, 1)
            seq.wait()
            pool.affine_select(out=ident[:, :], in_=ident[:, :], compare_op=ALU.not_equal, fill=1.0, base=0,
                               pattern=[[-1, P]], channel_multiplier=1).then_inc(consts, 1)
            seq.inc(pool.affine_select(out=MJ8[:, :, :], in_=MJ8[:, :, :], compare_op=ALU.is_ge, fill=0.0, base=0,
                                       pattern=[[-64, 2], [-16, 4]], channel_multiplier=1))
            seq.wait()
            seq.inc(pool.affine_select(out=MJ8[:, :, :], in_=MJ8[:, :, :], compare_op=ALU.is_ge, fill=0.0, base=15,
                                       pattern=[[64, 2], [16, 4]], channel_multiplier=-1))
            seq.wait()
            pool.tensor_tensor(MJ[:, :], MJ8[:, 0, :], MJ8[:, 1, :], ALU.add).then_inc(consts, 1)
            for c in range(PPAD):
                pool.memset(INVC[:, c:c + 1], 1.0 / (c + 1)).then_inc(consts, 1)

            def tt(o, x, y, op):
                seq.wait()
                return seq.inc(pool.tensor_tensor(o, x, y, op))

            def ts(o, x, s1, s2, op0, op1):
                seq.wait()
                return seq.inc(pool.tensor_scalar(o, x, s1, s2, op0, op1))

            LRE, LIM, DTL, DT, RE, IM, K, RED, HALF, EX, SN, SH, LR_, LI_, NR, T1, T2, DEN, REC, F0 = range(20)
            l = [LS[:, i, :] for i in range(20)]
            F1 = K
            pool.wait_ge(lam_in, 64)
            pool.wait_ge(lam_exp, 1)
            tt(l[RE], l[LRE], l[DT], ALU.mult)
            tt(l[IM], l[LIM], l[DT], ALU.mult)
            tt(l[T1], l[LRE], l[LRE], ALU.mult)
            tt(l[T2], l[LIM], l[LIM], ALU.mult)
            tt(l[DEN], l[T1], l[T2], ALU.add)
            ts(l[K], l[IM], 1.0 / TWO_PI, ROUND, ALU.mult, ALU.add)
            ts(l[K], l[K], ROUND, -1.0, ALU.subtract, ALU.mult)
            seq.wait()
            pool.tensor_scalar(l[T1], l[K], PI_A, None, ALU.mult).then_inc(lam_den, 1)
            pool.wait_ge(lam_den, 1)
            tt(l[RED], l[IM], l[T1], ALU.add)
            ts(l[T2], l[K], PI_B, None, ALU.mult, ALU.bypass)
            tt(l[RED], l[RED], l[T2], ALU.add)
            ts(l[T1], l[K], PI_C, None, ALU.mult, ALU.bypass)
            tt(l[RED], l[RED], l[T1], ALU.add)
            ts(l[RED], l[RED], 3.1415925, -3.1415925, ALU.min, ALU.max)
            seq.wait()
            pool.tensor_scalar(l[HALF], l[RED], 0.5, None, ALU.mult).then_inc(lam_ang, 1)
            pool.wait_ge(lam_sin, 3)
            tt(l[T1], l[SH], l[SH], ALU.mult)
            tt(l[LI_], l[EX], l[SN], ALU.mult)
            ts(l[T1], l[T1], -2.0, 1.0, ALU.mult, ALU.add)
            tt(l[LR_], l[EX], l[T1], ALU.mult)
            ts(l[NR], l[LR_], -1.0, None, ALU.add, ALU.bypass)
            tt(l[T1], l[NR], l[LRE], ALU.mult)
            tt(l[T2], l[LI_], l[LIM], ALU.mult)
            tt(l[F0], l[T1], l[T2], ALU.add)
            tt(l[T1], l[LI_], l[LRE], ALU.mult)
            tt(l[T2], l[NR], l[LIM], ALU.mult)
            tt(l[F1], l[T1], l[T2], ALU.subtract)
            pool.wait_ge(lam_rec, 1)
            tt(l[F0], l[F0], l[REC], ALU.mult)
            tt(l[F1], l[F1], l[REC], ALU.mult)

            def wide(row):
                return row.unsqueeze(2).to_broadcast([P, PAIRS, S5_GROUP])

            pool.wait_ge(b_in, 32)
            pool.wait_ge(xn0, 4)
            P0, P1 = PT[:, 0, :, :], PT[:, 1, :, :]

            def cmul(ore, oim, xre, xim, yre, yim, signs=(ALU.subtract, ALU.add)):
                tt(P0, xre, yre, ALU.mult)
                tt(P1, xim, yim, ALU.mult)
                tt(ore, P0, P1, signs[0])
                tt(P0, xim, yre, ALU.mult)
                tt(P1, xre, yim, ALU.mult)
                tt(oim, P0, P1, signs[1])

            cmul(WST[:, 0, :, 3, :], WST[:, 1, :, 3, :], BRAW[:, 0, :, :], BRAW[:, 1, :, :], wide(l[F0]), wide(l[F1]))
            for j in (2, 1, 0):
                cmul(WST[:, 0, :, j, :], WST[:, 1, :, j, :], WST[:, 0, :, j + 1, :], WST[:, 1, :, j + 1, :],
                     wide(l[LR_]), wide(l[LI_]))
            seq.wait()
            pool.memset(MJ8[:, 0, 0:1], 0.0).then_inc(pool_w, 1)
            tt(l[T1], l[LR_], l[LR_], ALU.mult)
            tt(l[T2], l[LI_], l[LI_], ALU.mult)
            tt(l[NR], l[LR_], l[LI_], ALU.mult)
            tt(l[T1], l[T1], l[T2], ALU.subtract)
            ts(l[NR], l[NR], 2.0, None, ALU.mult, ALU.bypass)
            tt(l[T2], l[T1], l[T1], ALU.mult)
            tt(l[DEN], l[NR], l[NR], ALU.mult)
            tt(l[IM], l[T1], l[NR], ALU.mult)
            tt(LAM[:, 0, :], l[T2], l[DEN], ALU.subtract)
            ts(LAM[:, 1, :], l[IM], 2.0, None, ALU.mult, ALU.bypass)
            ts(LAM[:, 2, :], l[IM], -2.0, None, ALU.mult, ALU.bypass)
            pool.wait_ge(banks_act, act_after("c_t"))
            for k in range(4):
                cmul(GRE[:, :, k + 1, :], GNI[:, :, k + 1, :], GRE[:, :, k, :], GNI[:, :, k, :],
                     wide(l[LR_]), wide(l[LI_]), signs=(ALU.add, ALU.subtract))
            seq.wait()
            pool.memset(MJ8[:, 0, 1:2], 0.0).then_inc(pool_g, 1)
            pool.wait_ge(d_in, 128)
            pool.wait_ge(consts, 3)

            def dcol():
                return DCOL[:, :].unsqueeze(2).to_broadcast([P, PAIRS, 64])

            def eye(half):
                return ident[:, 64 * half:64 * half + 64].unsqueeze(1).to_broadcast([P, PAIRS, 64])

            tt(TM[:, :, :], dcol(), eye(0), ALU.mult)
            tt(DT2[:, :, :], dcol(), eye(1), ALU.mult)
            seq.wait()
            pool.tensor_tensor(TM[:, :, :], TM[:, :, :], DT2[:, :, :], ALU.add).then_inc(pool_t, 1)
            pool.wait_ge(sg_in, 16)
            pool.memset(SGW[0:CHUNK, :, CHUNK:P], 0.0).then_inc(sgw_masked, 1)
            pool.wait_ge(side_done, side_after("w_t.3"))
            for ri in range(2):
                pool.tensor_copy(WST[:, ri, :, 0:T4 - 1, :],
                                 WST[:, ri, :, T4 - 1:T4, :].to_broadcast([P, PAIRS, T4 - 1, S5_GROUP])).then_inc(pool_rep, 1)
            pool.wait_ge(side_done, side_after("sgu.1"))
            pool.memset(CH[:, :, 0:PPAD], 0.0).then_inc(pads, 1)
            pool.wait_ge(s5_out, 64)
            pool.memset(WIN[:, :, 0:PPAD], 0.0).then_inc(pads, 1)
            pool.wait_ge(tmp_free, 16)
            pool.memset(CP[:, :, 0:CPAD], 0.0).then_inc(cpads, 1)
            pool.wait_ge(weights_used, used_after("w_c.1"))
            pool.memset(S[:, :, :, 0:1], 0.0).then_inc(states, 1)
            pool.wait_ge(banks_act, act_after("s5_z.7"))
            per_step = 4
            first = seq.n
            with pool.Fori(0, NCH - 1) as c:
                seq.base, seq.n = c * per_step, first
                now, nxt = S[:, :, :, bass.ds(c, 1)], S[:, :, :, bass.ds(c + 1, 1)]
                nre, nim = S[:, 0:1, :, bass.ds(c + 1, 1)], S[:, 1:2, :, bass.ds(c + 1, 1)]
                pool.wait_ge(states, c + 1)
                seq.inc(pool.tensor_tensor(ST1[:, :, :].unsqueeze(3), LAM[:, 0:1, :].to_broadcast([P, 2, PAIRS]).unsqueeze(3), now, ALU.mult))
                seq.inc(pool.tensor_tensor(ST2[:, :, :].unsqueeze(3), LAM[:, 1:3, :].unsqueeze(3), now, ALU.mult))
                seq.wait()
                seq.inc(pool.tensor_tensor(nxt, nxt, ST1[:, :, :].unsqueeze(3), ALU.add))
                seq.wait()
                seq.inc(pool.tensor_tensor(nim, nim, ST2[:, 0:1, :].unsqueeze(3), ALU.add))
                pool.tensor_tensor(nre, nre, ST2[:, 1:2, :].unsqueeze(3), ALU.add).then_inc(states, 1)
                assert seq.n - first == per_step
            seq.base, seq.n = 0, first + per_step * (NCH - 1)
            pool.wait_ge(x2_done, 4)
            seq.inc(pool.memset(CMASK[:, :], 1.0))
            seq.inc(pool.memset(ATS[:, :, :], 0.0))
            seq.inc(pool.memset(SMASK[:, :], 1.0))
            seq.inc(pool.memset(LR[0:32, :], 1.0))
            seq.wait()
            seq.inc(pool.affine_select(out=CMASK[:, :], in_=CMASK[:, :], compare_op=ALU.is_ge, fill=0.0, base=0,
                                       pattern=[[1, P]], channel_multiplier=-1))
            seq.inc(pool.memset(SMASK[:, :].rearrange("p (c t) -> p c t", t=CHUNK)[:, :, 0:1], 0.0))
            seq.wait()
            pool.memset(CMASK[0:CHUNK, CHUNK:P], 0.0).then_inc(gla_consts, 1)
            pool.wait_ge(xn2, 4)
            pool.memset(YO2[:, :, :], 0.0).then_inc(y2_zero, 1)

        @block.scalar
        def _(act):
            seq = Order(act, act_seq)
            state = {"unit": 0, "hi": 0, "y": 0}

            lam = LS
            act.dma_start(lam[:, 0, :], a["s5_lambda_re_2"][0].rearrange("(r g) n -> (g n) r", g=2)).then_inc(lam_in, 16)
            act.dma_start(lam[:, 1, :], a["s5_lambda_im_2"][0].rearrange("(r g) n -> (g n) r", g=2)).then_inc(lam_in, 16)
            for g in range(2):
                act.dma_start(lam[64 * g:64 * g + 64, 2, :],
                              a["s5_log_dt_2"].rearrange("o (r g) -> g o r", g=2)[g].broadcast_to([64, PAIRS])).then_inc(lam_in, 16)
            act.dma_start(PR[0:8, 0, :], a["norm_g"].rearrange("o (r p) -> (o r) p", p=P)).then_inc(prm_in, 16)
            rows = [("pool_b", 1), ("pool_scale", 1), ("conv_w", 3), ("conv_b", 1), ("norm_pre_2", 2), ("s5_b_glu_2", 1),
                    ("conv_b_2", 1), ("conv_ln_g_2", 1), ("conv_ln_b_2", 1), ("conv_b_pw_2", 1)]
            r0 = 8
            for name, n in rows:
                src = a[name][0] if name == "conv_w" else a[name]
                act.dma_start(PR[r0:r0 + 8 * n, 0, :], src.rearrange("k (r p) -> (k r) p", p=P)).then_inc(prm_in, 16)
                r0 += 8 * n
            act.dma_start(PR[r0:r0 + 4, 0, :], a["gla_norm_g_2"].rearrange("o (r p) -> (o r) p", p=P)).then_inc(prm_in, 16)
            taps = a["conv_w_2"][0].rearrange("k (r p) -> (k r) p", p=P)
            act.dma_start(PR[:, 1, :], taps[0:P, :]).then_inc(prm_in, 16)
            act.dma_start(PR[0:8 * CONV_K - P, 2, :], taps[P:8 * CONV_K, :]).then_inc(prm_in, 16)
            for i, name in enumerate(("s5_b_re_2", "s5_b_im_2")):
                act.dma_start(BRAW[:, i, :, :], a[name][0].rearrange("(r g) n q -> (g n) r q", g=2)).then_inc(b_in, 16)
            for i, name in enumerate(("sgu_ln_g", "sgu_ln_b")):
                act.dma_start(LNROWS[:, i, :], a[name].broadcast_to([P, D])).then_inc(ln_in, 16)
            act.dma_start(SGW[:, :, :], a["sgu_w"][0].rearrange("g i j -> i g j")).then_inc(sg_in, 16)
            act.dma_start(SGB[:, :, :].rearrange("p g i -> p (g i)"),
                          a["sgu_b"].rearrange("o g i -> o (g i)").broadcast_to([P, D])).then_inc(bs_in, 16)
            for g in range(2):
                for j in range(T4):
                    act.dma_start(DCOL[64 * g + 16 * j:64 * g + 16 * j + 16, :],
                                  a["s5_d_2"][0].rearrange("(r g q) -> g q r", g=2, q=S5_GROUP)[g]).then_inc(d_in, 16)

            def split(units=1):
                for _u in range(units):
                    if state["unit"] >= len(UNITS):
                        return
                    name = UNITS[state["unit"]]
                    for n in range(chunks_before(name), used_after(name)):
                        act.wait_ge(w_loaded[n % RING], 16 * (n // RING + 1))
                        if n >= RING:
                            act.wait_ge(weights_used, n - RING + 1)
                        act.activation(WH[:, n % RING, :, :], WR[:, n % RING, :, :], ACT.Copy).then_inc(w_hi, 1)
                    state["unit"] += 1

            def rms(src, n, junk, waits, sq, std):
                for t in range(n):
                    waits(t)
                    act.activation(junk(t), src(t), ACT.Square, accum_out=STAT[:, 0, t:t + 1]).then_inc(sq, 1)
                act.wait_ge(sq, n)
                act.activation(STAT[:, 1, 0:n], STAT[:, 0, 0:n], ACT.Sqrt, scale=1.0 / D, bias=EPS[:, 0:1]).then_inc(std, 1)

            def turned(job, kt0, vec, before=None):
                for m in range(4):
                    act.wait_ge(side_done, side_after(job, m + 1))
                    act.activation(HH[:, kt0 + m, :], bank(job, m), ACT.Copy, scale=col(vec, kt0 + m)).then_inc(h_hi, 1)

            def evac(job, outs, func, waits=None, inc=banks_act, **kw):
                act.wait_ge(weights_used if job in UNITS else side_done,
                            used_after(job) if job in UNITS else side_after(job))
                for m, o in enumerate(outs):
                    if waits:
                        waits(m)
                    extra = {k: v(m) for k, v in kw.items()}
                    act.activation(o, bank(job, m), func, **extra).then_inc(inc, 1)

            def via_tmp(job, func, **kw):
                act.wait_ge(weights_used, used_after(job))
                for m in range(4):
                    if state["hi"] >= 2:
                        act.wait_ge(tmp_free, state["hi"] - 1)
                    extra = {k: v(m) for k, v in kw.items()}
                    act.activation(TMP[:, state["hi"] % 2, :], bank(job, m), func, **extra).then_inc(banks_act, 1)
                    state["hi"] += 1

            def y_halves(ready, count, src, kts):
                for kt in kts:
                    act.wait_ge(ready, count(kt))
                    act.activation(YH[:, kt, :], src(kt), ACT.Copy).then_inc(y_hi, 1)

            act.wait_ge(consts, 2)
            act.wait_ge(x_in, 16)
            rms(lambda t: X[:, t, :], TT, lambda t: XN0[:, t, :], lambda t: None, sq0, std0)
            act.wait_ge(side_done, side_after("params"))
            for i, n in enumerate((116, 128, 120)):
                act.activation(PRM[:, 128 * i:128 * i + n], bank("params", i)[:, 0:n], ACT.Copy).then_inc(banks_act, 1)
            act.wait_ge(banks_act, act_after("params"))
            turned("h_t.0", 0, "norm_g")
            turned("h_t.1", 4, "norm_g")
            split()
            act.wait_ge(lam_in, 64)
            act.activation(LS[:, 3, :], LS[:, 2, :], ACT.Exp).then_inc(lam_exp, 1)
            act.wait_ge(lam_ang, 1)
            act.activation(LS[:, 9, :], LS[:, 4, :], ACT.Exp).then_inc(lam_sin, 1)
            act.activation(LS[:, 10, :], LS[:, 7, :], ACT.Sin).then_inc(lam_sin, 1)
            act.activation(LS[:, 11, :], LS[:, 8, :], ACT.Sin).then_inc(lam_sin, 1)

            def v_free(m):
                act.wait_ge(side_done, side_after("h_t.1"))

            split()
            evac("a_v.0", [V[:, m, 0:NC] for m in range(4)], ACT.Gelu_apprx_tanh, waits=v_free)
            split()
            evac("a_v.1", [V[:, m, NC:D] for m in range(4)], ACT.Gelu_apprx_tanh)
            split()
            evac("a_u.0", [U[:, m, :] for m in range(4)], ACT.Gelu_apprx_tanh)
            split()
            evac("a_u.1", [U[:, 4 + m, :] for m in range(4)], ACT.Gelu_apprx_tanh)
            act.wait_ge(v_std, 4)
            act.activation(STAT[:, 2, :], BNA[:, :, 1], ACT.Sqrt, bias=EPS[:, 1:2]).then_inc(v_std, 1)
            split()
            act.wait_ge(side_done, side_after("c_t"))
            act.activation(GRE[:, :, 0, :], bank("c_t", 0).rearrange("p (r q) -> p r q", q=S5_GROUP), ACT.Copy).then_inc(banks_act, 1)
            act.activation(GNI[:, :, 0, :], bank("c_t", 1).rearrange("p (r q) -> p r q", q=S5_GROUP), ACT.Copy,
                           scale=-1.0).then_inc(banks_act, 1)
            via_tmp("a_z.0", ACT.Silu)
            split()
            via_tmp("a_z.1", ACT.Silu)
            act.wait_ge(pool_t, 1)
            for i in range(4):
                act.wait_ge(side_done, side_after(f"w_t.{i}"))
                for ri in range(2):
                    act.activation(WTS[0:64, ri, 8 * i:8 * i + 8, :],
                                   bank(f"w_t.{i}", 2 * ri)[0:64, :].rearrange("p (r n) -> p r n", r=8),
                                   ACT.Copy).then_inc(banks_act, 1)
            for m in range(2):
                if not m:
                    act.wait_ge(side_done, side_after("sgu_t"))
                act.activation(SGWT[:, 4 * m:4 * m + 4, :], bank("sgu_t", m).rearrange("p (g i) -> p g i", g=4),
                               ACT.Copy).then_inc(banks_act, 1)
            split()
            act.wait_ge(v_done, 4)
            evac("g0.0", [G[:, m, :] for m in range(4)], ACT.Sigmoid)
            split()
            evac("g0.1", [G[:, 4 + m, :] for m in range(4)], ACT.Sigmoid)
            act.wait_ge(s5_out, 64)
            y_halves(ya_ready, lambda kt: kt + 1, lambda kt: U[:, kt, :], range(4))
            split()
            y_halves(ya_ready, lambda kt: kt + 1, lambda kt: U[:, kt, :], range(4, 8))
            act.wait_ge(pads, 1)
            evac("b_p.0", [CH[:, m, PPAD:] for m in range(4)], ACT.Copy)
            split()
            evac("b_p.1", [CH[:, 4 + m, PPAD:] for m in range(4)], ACT.Copy)
            split()
            split()
            split()
            act.wait_ge(d_ready, 4)
            evac("b_z.0", [CH[:, m, PPAD:] for m in range(4)], ACT.Silu)
            split()
            evac("b_z.1", [CH[:, 4 + m, PPAD:] for m in range(4)], ACT.Silu)
            act.wait_ge(weights_used, used_after("w_a.1"))
            y_halves(yb_ready, lambda kt: kt + 1, lambda kt: CH[:, kt, PPAD:], range(8))
            split()
            act.wait_ge(banks_dve, dve_after("w_a.1"))
            evac("g1.0", [G[:, m, :] for m in range(4)], ACT.Sigmoid)
            split()
            evac("g1.1", [G[:, 4 + m, :] for m in range(4)], ACT.Sigmoid)
            split()
            act.wait_ge(y_lo, 16)
            evac("c_h.0", [CH[:, m, PPAD:] for m in range(4)], ACT.Copy)
            split()
            evac("c_h.1", [CH[:, 4 + m, PPAD:] for m in range(4)], ACT.Copy)
            split()
            split()
            split()
            split()
            split()
            act.wait_ge(banks_dve, dve_after("w_b.1"))
            evac("g2.0", [G[:, m, :] for m in range(4)], ACT.Sigmoid)
            split()
            evac("g2.1", [G[:, 4 + m, :] for m in range(4)], ACT.Sigmoid)
            split()
            split()
            split()
            act.wait_ge(weights_used, used_after("w_b.1"))
            act.wait_ge(banks_dve, dve_after("c_b.1"))
            via_tmp("c_z.0", ACT.Silu)
            y_halves(tmp_free, lambda kt: 8 + kt + 1, lambda kt: U[:, kt, :], range(4))
            split()
            via_tmp("c_z.1", ACT.Silu)
            y_halves(tmp_free, lambda kt: 8 + kt + 1, lambda kt: U[:, kt, :], range(4, 8))
            split()
            split()
            act.wait_ge(weights_used, used_after("c_z.1"))
            for kt in range(KT):
                act.wait_ge(m_acc, 8 + kt + 1)
                act.activation(HH[:, kt, :], M[:, kt, :], ACT.Copy).then_inc(h_hi, 1)
            split()
            split()

            act.wait_ge(h_lo, 16)
            rms(lambda t: X[:, t, :], TT, lambda t: XN1[:, t, :], 
                lambda t: act.wait_ge(banks_dve, dve_after("w_out.1", t + 1)), sq1, std1)
            rms(lambda t: X[:, t, :], TT, lambda t: XN1[:, t, :], lambda t: act.wait_ge(x1_done, t + 1), sq2, std2)
            turned("u_t.0", 0, "norm_pre0")
            turned("u_t.1", 4, "norm_pre0")

            split()
            act.wait_ge(cpads, 1)
            evac("b_val.0", [CP[:, m, CPAD:] for m in range(4)], ACT.Copy)
            split()
            evac("b_val.1", [CP[:, 4 + m, CPAD:] for m in range(4)], ACT.Copy)
            split()
            via_tmp("b_gate.0", ACT.Sigmoid)
            split()
            via_tmp("b_gate.1", ACT.Sigmoid)
            for u in range(2):
                split()
                act.wait_ge(weights_used, used_after(f"a_in.{u}"))
                for j in range(T4):
                    act.activation(AS[:, u, :, j, :], bank(f"a_in.{u}", j).rearrange("p (g q) -> p g q", q=S5_GROUP),
                                   ACT.Copy).then_inc(banks_act, 1)
            for u in range(2):
                evac(f"s5_t.{u}", [UT[:, 16 * u + 4 * m:16 * u + 4 * m + 4, :].rearrange("p r c -> p (r c)")
                                   for m in range(4)], ACT.Copy)
            for i in range(8):
                act.wait_ge(side_done, side_after(f"s5_z.{i}"))
                for m in range(4):
                    ri, g = m // 2, m % 2
                    act.activation(S[64 * g:64 * g + 64, ri, 4 * i:4 * i + 4, 1:NCH],
                                   bank(f"s5_z.{i}", m)[64 * g:64 * g + 64, :].rearrange("p (r c) -> p r c", c=NCH)[:, :, 0:NCH - 1],
                                   ACT.Copy).then_inc(banks_act, 1)
            split()
            evac("a_z2.0", [AZ[:, m, :] for m in range(4)], ACT.Silu)
            split()
            evac("a_z2.1", [AZ[:, 4 + m, :] for m in range(4)], ACT.Silu)
            split()
            evac("b_z2.0", [BZ[:, m, :] for m in range(4)], ACT.Silu)
            split()
            evac("b_z2.1", [BZ[:, 4 + m, :] for m in range(4)], ACT.Silu)
            for i in range(2):
                act.wait_ge(side_done, side_after(f"s5_y.{i}"))
                for m in range(4):
                    oc, g = 2 * i + m // 2, m % 2
                    dst = YT[:, :, :].rearrange("c t (r g q) -> c g r t q", g=2, q=S5_GROUP)[:, g, 8 * oc:8 * oc + 8, :, :]
                    act.activation(dst, bank(f"s5_y.{i}", m).rearrange("p (r t q) -> p r t q", r=8, t=T4),
                                   ACT.Gelu_apprx_tanh).then_inc(banks_act, 1)
            for i in range(2):
                for m in range(4):
                    act.wait_ge(side_done, side_after(f"y_t.{i}", m + 1))
                    act.activation(YH[:, 4 * i + m, :].rearrange("p (c t) -> p t c", t=T4),
                                   bank(f"y_t.{i}", m).rearrange("p (t c) -> p t c", t=T4), ACT.Copy).then_inc(y_hi, 1)
            split()
            act.wait_ge(conv_done, 8)
            via_tmp("glu.0", ACT.Sigmoid, bias=lambda m: col("b_glu", m))
            split()
            via_tmp("glu.1", ACT.Sigmoid, bias=lambda m: col("b_glu", 4 + m))
            for kt in range(KT):
                act.wait_ge(z_cent, kt + 1)
                if kt >= 2:
                    act.wait_ge(sq_used, kt - 1)
                else:
                    act.wait_ge(tmp_free, state["hi"])
                act.activation(TMP[:, kt % 2, :], CP[:, kt, CPAD:], ACT.Square).then_inc(z_sq, 1)
            act.wait_ge(sq_used, KT)
            act.activation(RS[:, :], bank("var", 0), ACT.Sqrt, bias=EPS[:, 0:1]).then_inc(banks_act, 1)
            for kt in range(KT):
                act.wait_ge(z_norm, kt + 1)
                act.activation(CP[:, kt, CPAD:], CP[:, kt, CPAD:], ACT.Silu, scale=col("ln_g2", kt),
                               bias=col("ln_b2", kt)).then_inc(z_act, 1)
                if kt == 0:
                    act.wait_ge(weights_used, used_after("glu.1"))
                act.wait_ge(z_act, kt + 1)
                act.activation(YH[:, kt, :], CP[:, kt, CPAD:], ACT.Copy).then_inc(y_hi, 1)
            for kt in range(KT):
                act.wait_ge(ya_final, kt + 1)
                act.activation(HH[:, kt, :], YA[:, kt, :], ACT.Copy).then_inc(h_hi, 1)
            split()
            split()
            act.wait_ge(weights_used, used_after("pw.1"))
            y_halves(banks_dve, lambda kt: dve_after(f"pw.{kt // 4}", kt % 4 + 1), lambda kt: BZ[:, kt, :], range(8))
            split()
            evac("ev_out.0", [YO[:, m, 0:NC] for m in range(4)], ACT.Copy)
            evac("ev_out.1", [YO[:, m, NC:D] for m in range(4)], ACT.Copy)
            act.wait_ge(banks_act, act_after("ev_out.1"))
            act.wait_ge(y_lo, 48)
            rms(lambda t: YO[:, t, :], TT, lambda t: XN2[:, t, :], lambda t: None, sq3, std3)
            rms(lambda t: X1[:, t, :], TT, lambda t: XN2[:, t, :], lambda t: act.wait_ge(x2_done, t + 1), sq4, std4)
            turned("u2_t.0", 0, "norm_pre1")
            turned("u2_t.1", 4, "norm_pre1")

            act.wait_ge(h_lo, 32)
            act.dma_start(LWR[:, :, :], a["od_w_in_2"][0][:, 6 * D:6 * D + LOWRANK].rearrange("(k p) n -> p k n", p=P)).then_inc(lw_in, 16)
            act.wait_ge(lw_in, 16)
            act.wait_ge(lw_zero, 2)
            act.activation(LWH[:, :, 0:LOWRANK], LWR[:, :, :], ACT.Copy).then_inc(lw_hi, 1)
            act.wait_ge(gla_consts, 1)
            act.wait_ge(hd_side, HS0)
            act.activation(LR[0:LOWRANK, :], bank("lr", 0)[0:LOWRANK, :], ACT.Copy).then_inc(banks_act, 1)

            with act.Fori(0, HEADS) as h:
                def hsplit(j0, n):
                    for j in range(j0, j0 + n):
                        slot = j % RING
                        act.wait_ge(w_loaded[slot], h * 80 + (16 * (N_STATIC // RING) + 32 + 16 * (j // RING)))
                        act.wait_ge(weights_used, h * HEAD_CHUNKS + (N_STATIC + j - RING + 1))
                        act.activation(WH[:, slot, :, :], WR[:, slot, :, :], ACT.Copy).then_inc(w_hi, 1)

                def used(j):
                    return h * HEAD_CHUNKS + (N_STATIC + j)

                def aside(k):
                    return h * HSIDE + k

                seq.base, seq.n = h * HSEQ_ACT, 0
                act.wait_ge(hd_side, h * HSIDE + HS0)
                act.dma_start(GU[0:LOWRANK, :], a["gla_w_gate_up_2"][0][:, bass.ds(h * HK, HK)]).then_inc(gu_in, 16)
                act.dma_start(GU[LOWRANK:LOWRANK + 1, :], a["gla_b_gate_2"][0:1, bass.ds(h * HK, HK)]).then_inc(gu_in, 16)
                hsplit(0, 4)
                hsplit(4, 4)
                act.wait_ge(weights_used, used(4))
                act.wait_ge(hd_dve, h * HDVE + HD0)
                for m in range(4):
                    act.activation(QK[:, m, :], PS[:, m, :], ACT.Copy).then_inc(hd_act, 1)
                act.wait_ge(hd_side, aside(HS0 + 1))
                for m in range(2):
                    seq.inc(act.activation(ET[:, m, :], PS[:, 4 + m, :], ACT.Abs))
                for m in range(2):
                    seq.wait(m + 1)
                    seq.inc(act.activation(ET[:, m, :], ET[:, m, :], ACT.Exp, scale=-1.0))
                for m in range(2):
                    seq.wait(m + 3)
                    act.activation(ET[:, m, :], ET[:, m, :], ACT.Ln, bias=1.0).then_inc(e_abs, 1)
                act.wait_ge(g_scan, h * 2 + 1)
                act.activation(ET[:, :, :], BC[:, :, :], ACT.Exp, scale=1.0 / GLA_TAU).then_inc(e_q, 1)
                act.activation(DEC[:, :, :], BC[:, :, :].rearrange("p k (c t) -> p k c t", t=CHUNK)[:, :, :, CHUNK - 1],
                               ACT.Exp, scale=1.0 / GLA_TAU).then_inc(dec_in, 1)
                act.wait_ge(qd_done, h + 1)
                act.activation(ET[:, :, :], BC[:, :, :], ACT.Exp, scale=-1.0 / GLA_TAU).then_inc(e_ke, 1)
                act.wait_ge(g_scan, h * 2 + 2)
                act.wait_ge(ke_done, h + 1)
                act.activation(ET[:, :, :], KDC[:, :, :], ACT.Exp, scale=1.0 / GLA_TAU).then_inc(e_d, 1)
                hsplit(8, 4)
                act.wait_ge(weights_used, used(8))
                for m in range(4):
                    act.activation(V2[:, m, :], PS[:, m, :], ACT.Copy).then_inc(hd_act, 1)
                hsplit(12, 4)
                act.wait_ge(weights_used, used(12))
                for m in range(4):
                    act.activation(RR[:, m, :], PS[:, 4 + m, :], ACT.Silu).then_inc(hd_act, 1)
                act.wait_ge(hd_side, aside(HS0 + 2))
                for m in range(2):
                    act.activation(KTK[:, 2 * m:2 * m + 2, :, :].rearrange("p t k n -> p (t k n)"),
                                   PS[:, m, :], ACT.Copy).then_inc(hd_act, 1)
                for m in range(4):
                    act.wait_ge(hd_side, aside(HS_O[m]))
                    act.activation(ON[:, m, :], PS[:, m, :], ACT.Square, accum_out=STAT[:, 0, m:m + 1]).then_inc(o_sq, 1)
                act.wait_ge(o_sq, h * 4 + 4)
                act.activation(STAT[:, 1, :], STAT[:, 0, :], ACT.Sqrt, scale=1.0 / HV, bias=EPS[:, 0:1]).then_inc(o_std, 1)
                for m in range(4):
                    act.wait_ge(o_f, h * 4 + m + 1)
                    act.activation(OH[:, m, :], RR[:, m, :], ACT.Copy).then_inc(o_hi, 1)

            act.wait_ge(hd_dve, HD0 + HEADS * HDVE)
            rms(lambda t: YO2[:, t, :], TT, lambda t: XN2[:, t, :], lambda t: None, sq5, std5)

        @block.vector
        def _(dve):
            seq = Order(dve, dve_seq)
            state = {"unit": 0, "via": 0}

            def split(units=1):
                for _u in range(units):
                    if state["unit"] >= len(UNITS):
                        return
                    name = UNITS[state["unit"]]
                    for n in range(chunks_before(name), used_after(name)):
                        s = n % RING
                        dve.wait_ge(w_hi, n + 1)
                        dve.tensor_tensor(WL[:, s, :, :], WR[:, s, :, :], WH[:, s, :, :].bitcast(F32),
                                          ALU.subtract).then_inc(w_lo, 1)
                    state["unit"] += 1

            def done(job):
                dve.wait_ge(weights_used if job in UNITS else side_done,
                            used_after(job) if job in UNITS else side_after(job))

            def rstd(k):
                seq.inc(dve.reciprocal(STAT[:, 3, :], STAT[:, k, :]))
                seq.wait()

            def turned(job, kt0, vec, version):
                for m in range(4):
                    kt = kt0 + m
                    dve.wait_ge(h_hi, 8 * version + kt + 1)
                    dve.scalar_tensor_tensor(HL[:, kt, :], bank(job, m), col(vec, kt), HH[:, kt, :].bitcast(F32),
                                             ALU.mult, ALU.subtract).then_inc(h_lo, 1)

            def y_low(version, src, kts):
                for kt in kts:
                    dve.wait_ge(y_hi, 8 * version + kt + 1)
                    dve.tensor_tensor(YL[:, kt, :], src(kt), YH[:, kt, :].bitcast(F32), ALU.subtract).then_inc(y_lo, 1)

            def h_low(version, src, kts):
                for kt in kts:
                    dve.wait_ge(h_hi, 8 * version + kt + 1)
                    dve.tensor_tensor(HL[:, kt, :], src(kt), HH[:, kt, :].bitcast(F32), ALU.subtract).then_inc(h_lo, 1)

            def times_tmp(dsts, sems=None):
                for i, (job, m, d) in enumerate(dsts):
                    dve.wait_ge(banks_act, act_after(job, m + 1))
                    dve.tensor_tensor(d, d, TMP[:, state["via"] % 2, :], ALU.mult).then_inc(tmp_free, 1)
                    state["via"] += 1

            dve.wait_ge(std0, 1)
            rstd(1)
            for t in range(TT):
                dve.tensor_scalar(XN0[:, t, :], X[:, t, :], STAT[:, 3, t:t + 1], None, ALU.mult).then_inc(xn0, 1)
            dve.wait_ge(banks_act, act_after("params"))
            turned("h_t.0", 0, "norm_g", 0)
            turned("h_t.1", 4, "norm_g", 0)
            split()
            dve.wait_ge(lam_den, 1)
            dve.reciprocal(LS[:, 18, :], LS[:, 17, :]).then_inc(lam_rec, 1)
            split()
            split()
            split()
            for t in range(TT):
                dve.wait_ge(banks_act, act_after("a_v.1", t + 1))
                for u in range(2):
                    seq.inc(dve.bn_stats(BNS[:, t, u, :], V[:, t, u * NC:(u + 1) * NC]))
                seq.wait()
                dve.bn_aggr(BNA[:, t, :], BNS[:, t, :, :]).then_inc(v_std, 1)
            split()
            dve.wait_ge(v_std, 5)
            rstd(2)
            dve.wait_ge(ln_in, 32)
            n = [seq.inc(dve.tensor_scalar(V[:, t, :], V[:, t, :], BNA[:, t, 0:1], STAT[:, 3, t:t + 1],
                                           ALU.subtract, ALU.mult)) for t in range(TT)]
            for t in range(TT):
                seq.wait(n[t])
                n[t] = seq.inc(dve.tensor_tensor(V[:, t, :], V[:, t, :], LNROWS[:, 0, :], ALU.mult))
            split()
            for t in range(TT):
                seq.wait(n[t])
                dve.tensor_tensor(V[:, t, :], V[:, t, :], LNROWS[:, 1, :], ALU.add).then_inc(v_done, 1)
            times_tmp([("a_z.0", m, U[:, m, :]) for m in range(4)])
            split()
            times_tmp([("a_z.1", m, U[:, 4 + m, :]) for m in range(4)])
            dve.wait_ge(pool_t, 1)
            dve.wait_ge(consts, 4)
            for i in range(4):
                done(f"w_t.{i}")
                for ri in range(2):
                    dve.tensor_copy(WTS[64:P, ri, 8 * i:8 * i + 8, :],
                                    bank(f"w_t.{i}", 2 * ri + 1)[64:P, :].rearrange("p (r n) -> p r n", r=8)).then_inc(banks_dve, 1)
            for i in range(2):
                done(f"k.{i}")
                for m in range(4):
                    oc, g = 2 * i + m // 2, m % 2
                    lags = bank(f"k.{i}", m)[64 * g:64 * g + 64, :].rearrange("p (r l q) -> p r l q", r=8, l=T4)
                    tm = TM[64 * g:64 * g + 64, 8 * oc:8 * oc + 8, :].rearrange("p r (t q) -> p r t q", q=S5_GROUP)
                    for lag in range(T4):
                        if lag:
                            seq.wait()
                        for t in range(lag, T4):
                            o = dve.scalar_tensor_tensor(tm[:, :, t, :], lags[:, :, lag, :], MJ[64 * g:64 * g + 64, t - lag:t - lag + 1],
                                                         tm[:, :, t, :], ALU.mult, ALU.add)
                            if lag == T4 - 1:
                                o.then_inc(banks_dve, 1)
                            else:
                                seq.inc(o)
            split()
            dve.wait_ge(bs_in, 16)
            dve.wait_ge(tmp_free, 8)

            def sgu_out(i):
                done(f"sgu.{i}")
                for m in range(4):
                    g = 4 * i + m
                    dve.tensor_tensor(TMP[:, m % 2, :].rearrange("p (n i) -> p n i", i=P),
                                      bank(f"sgu.{i}", m).rearrange("p (n i) -> p n i", i=P),
                                      SGB[:, g, :].unsqueeze(1).to_broadcast([P, TT, P]), ALU.add).then_inc(banks_dve, 1)
                    dve.wait_ge(banks_dve, dve_after(f"sgu.{i}", m + 1))
                    dve.tensor_tensor(U[:, g, :], U[:, g, :], TMP[:, m % 2, :], ALU.mult).then_inc(ya_ready, 1)

            split()
            sgu_out(0)
            sgu_out(1)
            dve.wait_ge(ya_ready, 8)
            y_low(0, lambda kt: U[:, kt, :], range(8))
            split()
            split()
            dve.wait_ge(pads, 2)
            dve.wait_ge(consts, 4 + PPAD)

            def windows(k):
                w = POOL_WINDOWS[k]
                for kt in (2 * k, 2 * k + 1):
                    dve.wait_ge(banks_act, act_after(f"b_p.{kt // 4}", kt % 4 + 1))
                    src, step = CH[:, kt, :], 1
                    slot = 0
                    while step < w:
                        seq.inc(dve.tensor_tensor(WIN[:, slot, PPAD:], src[:, PPAD:], src[:, PPAD - step:PPAD - step + SEQ], ALU.add))
                        src, slot, step = WIN[:, slot, :], slot ^ 1, 2 * step
                        seq.wait()
                    seq.inc(dve.tensor_tensor(WIN[:, 2, PPAD:PPAD + w], src[:, PPAD:PPAD + w], INVC[:, 0:w], ALU.mult))
                    seq.inc(dve.scalar_tensor_tensor(U[:, kt, w:], src[:, PPAD + w:], 1.0 / w, CH[:, kt, PPAD + w:],
                                                     ALU.mult, ALU.subtract))
                    seq.wait()
                    o = dve.tensor_tensor(U[:, kt, 0:w], WIN[:, 2, PPAD:PPAD + w], CH[:, kt, PPAD:PPAD + w], ALU.subtract)
                    if kt % 2:
                        o.then_inc(d_ready, 1)
                    else:
                        seq.inc(o)

            windows(0)
            windows(1)
            split()
            done("w_a.0")
            for m in range(4):
                dve.tensor_tensor(M[:, m, :], bank("w_a.0", m), G[:, m, :], ALU.mult).then_inc(banks_dve, 1)
            split()
            windows(2)
            done("w_a.1")
            for m in range(4):
                dve.tensor_tensor(M[:, 4 + m, :], bank("w_a.1", m), G[:, 4 + m, :], ALU.mult).then_inc(banks_dve, 1)
            windows(3)
            split()
            split()
            for i in range(2):
                done(f"pool.{i}")
                for m in range(4):
                    kt = 4 * i + m
                    if kt >= 2:
                        dve.wait_ge(yb_ready, kt - 1)
                    dve.tensor_scalar(TMP[:, m % 2, :], bank(f"pool.{i}", m), col("pool_b", kt), col("pool_scale", kt),
                                      ALU.add, ALU.mult).then_inc(banks_dve, 1)
                    dve.wait_ge(banks_dve, dve_after(f"pool.{i}", m + 1))
                    if m == 0:
                        dve.wait_ge(banks_act, act_after(f"b_z.{i}"))
                    dve.tensor_tensor(CH[:, kt, PPAD:], CH[:, kt, PPAD:], TMP[:, m % 2, :], ALU.mult).then_inc(yb_ready, 1)
            dve.wait_ge(yb_ready, 8)
            y_low(1, lambda kt: CH[:, kt, PPAD:], range(8))
            split()
            split()
            split()
            split()

            def merge(job, u, version=None):
                done(job)
                for m in range(4):
                    kt = 4 * u + m
                    dve.tensor_tensor(TMP[:, m % 2, :], bank(job, m), G[:, kt, :], ALU.mult).then_inc(banks_dve, 1)
                    dve.wait_ge(banks_dve, dve_after(job, m + 1))
                    dve.tensor_tensor(M[:, kt, :], M[:, kt, :], TMP[:, m % 2, :], ALU.add).then_inc(m_acc, 1)

            split()
            dve.wait_ge(banks_act, act_after("g1.1"))
            dve.wait_ge(banks_dve, dve_after("w_a.1"))
            merge("w_b.0", 0)
            split()
            merge("w_b.1", 1)
            for u in range(2):
                split()
                done(f"c_c.{u}")
                dve.wait_ge(banks_act, act_after(f"c_h.{u}"))
                for m in range(4):
                    kt = 4 * u + m
                    dve.tensor_tensor(CH[:, kt, PPAD:], bank(f"c_c.{u}", m), CH[:, kt, PPAD:], ALU.mult).then_inc(banks_dve, 1)
                dve.wait_ge(side_done, side_after("pool.1"))
                for m in range(4):
                    kt = 4 * u + m
                    dve.wait_ge(banks_dve, dve_after(f"c_c.{u}", m + 1))
                    seq.inc(dve.tensor_scalar(U[:, kt, :], CH[:, kt, PPAD:], col("conv_w2", kt), col("conv_b", kt), ALU.mult, ALU.add))
                for k, s in ((1, 1), (0, 2)):
                    first = seq.n - 3
                    for m in range(4):
                        kt = 4 * u + m
                        seq.wait(first + m)
                        seq.inc(dve.scalar_tensor_tensor(U[:, kt, :], CH[:, kt, PPAD - s:PPAD - s + SEQ], col(f"conv_w{k}", kt),
                                                         U[:, kt, :], ALU.mult, ALU.add))
            split()
            split()
            split()
            seq.wait()
            for u in range(2):
                done(f"c_b.{u}")
                for m in range(4):
                    kt = 4 * u + m
                    dve.tensor_tensor(U[:, kt, :], bank(f"c_b.{u}", m), U[:, kt, :], ALU.mult).then_inc(banks_dve, 1)
                split()
            for u in range(2):
                dve.wait_ge(banks_dve, dve_after(f"c_b.{u}"))
                times_tmp([(f"c_z.{u}", m, U[:, 4 * u + m, :]) for m in range(4)])
                y_low(2, lambda kt: U[:, kt, :], range(4 * u, 4 * u + 4))
                split()
            dve.wait_ge(banks_act, act_after("g2.1"))
            dve.wait_ge(m_acc, 8)
            merge("w_c.0", 0)
            split()
            merge("w_c.1", 1)
            h_low(1, lambda kt: M[:, kt, :], range(8))
            split()
            dve.wait_ge(x_again, 16)
            for u in range(2):
                done(f"w_out.{u}")
                for t in range(TT):
                    dve.tensor_tensor(X[:, t, u * NC:(u + 1) * NC], bank(f"w_out.{u}", t), X[:, t, u * NC:(u + 1) * NC],
                                      ALU.add).then_inc(banks_dve, 1)
                if u == 0:
                    split()
            dve.wait_ge(std1, 1)
            rstd(1)
            dve.wait_ge(frow_in, 16)
            for t in range(TT):
                dve.scalar_tensor_tensor(X[:, t, :], X[:, t, :], STAT[:, 3, t:t + 1], FROW[:, :], ALU.mult, ALU.mult).then_inc(x1_done, 1)
            dve.wait_ge(std2, 1)
            rstd(1)
            for t in range(TT):
                dve.tensor_scalar(XN1[:, t, :], X[:, t, :], STAT[:, 3, t:t + 1], None, ALU.mult).then_inc(xn1, 1)
            turned("u_t.0", 0, "norm_pre0", 2)
            turned("u_t.1", 4, "norm_pre0", 2)

            split()
            split()
            split()
            for u in range(2):
                times_tmp([(f"b_gate.{u}", m, CP[:, 4 * u + m, CPAD:]) for m in range(4)])
                split()
            dve.wait_ge(cpads, 1)

            def taps():
                for kt0 in range(0, KT, 2):
                    for k in range(CONV_K):
                        for s in range(2):
                            yield kt0 + s, k, s

            todo = list(taps())
            conv = {"i": 0}

            def convolve(n):
                for kt, k, s in todo[conv["i"]:conv["i"] + n]:
                    w = PRM[:, 8 * (VEC_CONV + k) + kt:8 * (VEC_CONV + k) + kt + 1]
                    if k == 0:
                        if kt >= 2:
                            dve.wait_ge(conv_done, kt - 1)
                        conv[s] = seq.inc(dve.tensor_scalar(TMP[:, s, :], CP[:, kt, 0:SEQ], w, col("conv_b_2", kt), ALU.mult, ALU.add))
                    else:
                        seq.wait(conv[s])
                        last = k == CONV_K - 1
                        o = dve.scalar_tensor_tensor(CP[:, kt, CPAD:] if last else TMP[:, s, :], CP[:, kt, k:k + SEQ], w,
                                                     TMP[:, s, :], ALU.mult, ALU.add)
                        if last:
                            o.then_inc(conv_done, 1)
                        else:
                            conv[s] = seq.inc(o)
                    conv["i"] += 1

            dve.wait_ge(tmp_free, 24)
            convolve(40)
            split()
            convolve(34)
            split()
            convolve(40)
            split()
            convolve(24)
            split()
            convolve(24)
            split()
            convolve(len(todo))

            for i in range(2):
                for m in range(4):
                    kt = 4 * i + m
                    dve.wait_ge(y_hi, 24 + kt + 1)
                    src = bank(f"y_t.{i}", m).rearrange("p (t c) -> p t c", t=T4)
                    seq.inc(dve.tensor_copy(YA[:, kt, :].rearrange("p (c t) -> p t c", t=T4), src))
                    dve.tensor_tensor(YL[:, kt, :].rearrange("p (c t) -> p t c", t=T4), src,
                                      YH[:, kt, :].bitcast(F32).rearrange("p (c t) -> p t c", t=T4), ALU.subtract).then_inc(y_lo, 1)
            dve.wait_ge(side_done, side_after("s5_y.1"))
            dve.memset(ONES[:, :], 1.0 / D).then_inc(ones_in, 1)
            done("mean")
            dve.tensor_copy(MU[:, :], bank("mean", 0)).then_inc(banks_dve, 1)
            split()
            dve.wait_ge(banks_dve, dve_after("mean"))
            dve.wait_ge(conv_done, 8)
            for kt in range(KT):
                dve.tensor_tensor(CP[:, kt, CPAD:], CP[:, kt, CPAD:], MU[:, :], ALU.subtract).then_inc(z_cent, 1)
            seq.wait()
            for u in range(2):
                if u:
                    split()
                times_tmp([(f"glu.{u}", m, YA[:, 4 * u + m, :]) for m in range(4)])
                for m in range(4):
                    dve.wait_ge(tmp_free, 24 + 4 * u + m + 1)
                    kt = 4 * u + m
                    if kt == 0:
                        dve.wait_ge(banks_act, act_after("a_z2.1"))
                    dve.tensor_tensor(YA[:, kt, :], YA[:, kt, :], AZ[:, kt, :], ALU.mult).then_inc(ya_final, 1)
            dve.wait_ge(banks_act, act_after("var"))
            seq.inc(dve.reciprocal(RS[:, :], RS[:, :]))
            seq.wait()
            dve.wait_ge(z_sq, 8)
            for kt in range(KT):
                dve.tensor_tensor(CP[:, kt, CPAD:], CP[:, kt, CPAD:], RS[:, :], ALU.mult).then_inc(z_norm, 1)
            y_low(4, lambda kt: CP[:, kt, CPAD:], range(8))
            split()
            dve.wait_ge(ya_final, 8)
            h_low(3, lambda kt: YA[:, kt, :], range(8))
            for u in range(2):
                if u:
                    split()
                done(f"pw.{u}")
                dve.wait_ge(banks_act, act_after("b_z2.1"))
                for m in range(4):
                    kt = 4 * u + m
                    dve.scalar_tensor_tensor(BZ[:, kt, :], bank(f"pw.{u}", m), col("b_pw", kt), BZ[:, kt, :],
                                             ALU.add, ALU.mult).then_inc(banks_dve, 1)
            for kt in range(8):
                dve.wait_ge(y_hi, 8 * 5 + kt + 1)
                dve.tensor_tensor(YL[:, kt, :], BZ[:, kt, :], YH[:, kt, :].bitcast(F32), ALU.subtract).then_inc(y_lo, 1)

            split()
            dve.wait_ge(std3, 1)
            rstd(1)
            dve.wait_ge(prow0_in, 16)
            dve.wait_ge(x1_in, 16)
            for t in range(TT):
                seq.inc(dve.scalar_tensor_tensor(YO[:, t, :], YO[:, t, :], STAT[:, 3, t:t + 1], PROW0[:, :], ALU.mult, ALU.mult))
            for t in range(TT):
                seq.wait(seq.n - TT + 1 + t)
                dve.tensor_tensor(X1[:, t, :], X1[:, t, :], YO[:, t, :], ALU.add).then_inc(x2_done, 1)
            dve.wait_ge(std4, 1)
            rstd(1)
            for t in range(TT):
                dve.tensor_scalar(XN2[:, t, :], X1[:, t, :], STAT[:, 3, t:t + 1], None, ALU.mult).then_inc(xn2, 1)
            dve.memset(LWH[:, :, :].bitcast(F32), 0.0).then_inc(lw_zero, 1)
            dve.memset(LWL[:, :, :].bitcast(F32), 0.0).then_inc(lw_zero, 1)
            turned("u2_t.0", 0, "norm_pre1", 4)
            turned("u2_t.1", 4, "norm_pre1", 4)
            dve.wait_ge(lw_hi, 1)
            dve.tensor_tensor(LWL[:, :, 0:LOWRANK], LWR[:, :, :], LWH[:, :, 0:LOWRANK].bitcast(F32), ALU.subtract).then_inc(lw_lo, 1)
            dve.memset(BNA[:, 0, 0:1], 0.0).then_inc(hd_dve, HD0)

            dve.wait_ge(gla_consts, 1)
            seq0 = seq.n
            with dve.Fori(0, HEADS) as h:
                seq.base, seq.n = h * HSEQ_DVE + seq0, 0

                def hsplit(j0, n):
                    for j in range(j0, j0 + n):
                        s = j % RING
                        dve.wait_ge(w_hi, h * HEAD_CHUNKS + (N_STATIC + j + 1))
                        dve.tensor_tensor(WL[:, s, :, :], WR[:, s, :, :], WH[:, s, :, :].bitcast(F32),
                                          ALU.subtract).then_inc(w_lo, 1)

                def ev(k):
                    return h * HDVE + (HD0 + k)

                hsplit(0, 4)
                hsplit(4, 4)
                for m in range(2):
                    dve.wait_ge(e_abs, h * 2 + (m + 1))
                    dve.scalar_tensor_tensor(ET[:, m, :], PS[:, 4 + m, :], 0.0, ET[:, m, :], ALU.min, ALU.subtract).then_inc(hd_dve, 1)
                dve.wait_ge(hd_dve, ev(2))
                dve.tensor_tensor_scan(BC[:, :, :].rearrange("p k t -> p (k t)"), SMASK[:, :],
                                       ET[:, :, :].rearrange("p k t -> p (k t)"), 0.0, ALU.mult, ALU.add).then_inc(g_scan, 1)
                dve.wait_ge(e_q, h + 1)
                dve.wait_ge(hd_act, h * HACT + 4)
                dve.scalar_tensor_tensor(QD[:, :, :], QK[:, 0:2, :], float(HK) ** -0.5, ET[:, :, :], ALU.mult, ALU.mult).then_inc(qd_done, 1)
                dve.wait_ge(e_ke, h + 1)
                dve.tensor_tensor(KE[:, :, :], QK[:, 2:4, :], ET[:, :, :], ALU.mult).then_inc(ke_done, 1)
                dve.wait_ge(g_scan, h * 2 + 1)
                b4 = BC[:, :, :].rearrange("p k (c t) -> p (k c) t", t=CHUNK)
                dve.tensor_tensor(KDC[:, :, :].rearrange("p k (c t) -> p (k c) t", t=CHUNK),
                                  b4[:, :, CHUNK - 1:CHUNK].to_broadcast([P, 2 * GCH, CHUNK]), b4, ALU.subtract).then_inc(g_scan, 1)
                dve.wait_ge(e_d, h + 1)
                dve.tensor_tensor(KDC[:, :, :], QK[:, 2:4, :], ET[:, :, :], ALU.mult).then_inc(kd_done, 1)
                hsplit(8, 4)
                hsplit(12, 4)
                for m in range(4):
                    dve.wait_ge(hd_act, h * HACT + (8 + m + 1))
                    if m == 3:
                        dve.wait_ge(hd_side, h * HSIDE + (HS0 + 3))
                    dve.tensor_scalar(RR[:, m, :], RR[:, m, :], col("gla_norm_g", m), None, ALU.mult).then_inc(rr_in, 1)
                for t in range(TT):
                    dve.copy_predicated(ATS[:, t, :], CMASK[:, :].bitcast(U32), PS[:, 4, t * P:(t + 1) * P]).then_inc(hd_dve, 1)
                for c in range(GCH - 1):
                    dve.wait_ge(hd_side, h * HSIDE + HS_D[c])
                    if c >= 2:
                        dve.wait_ge(hd_side, h * HSIDE + HS_I[c - 1])
                    delta = PS[:, 4 + 2 * (c % 2):6 + 2 * (c % 2), :]
                    if c == 0:
                        dve.tensor_copy(ST[:, 0, :, :], delta).then_inc(st_done, 1)
                        dve.wait_ge(dec_in, h + 1)
                        continue
                    dve.wait_ge(st_done, h * HST + st_after(c - 1))
                    for k in range(2):
                        dve.scalar_tensor_tensor(ST[:, c % 2, k, :], ST[:, (c - 1) % 2, k, :], DEC[:, k, c:c + 1], delta[:, k, :],
                                                 ALU.mult, ALU.add).then_inc(st_done, 1)
                dve.wait_ge(o_std, h + 1)
                seq.inc(dve.reciprocal(STAT[:, 3, :], STAT[:, 1, :]))
                seq.wait()
                for m in range(TT):
                    dve.tensor_scalar(ON[:, m, :], PS[:, m, :], STAT[:, 3, m:m + 1], None, ALU.mult).then_inc(hd_dve, 1)
                dve.wait_ge(rr_in, h * 4 + 4)
                for m in range(4):
                    dve.wait_ge(hd_side, h * HSIDE + HS_OT[m])
                    dve.tensor_tensor(RR[:, m, :], PS[:, 4 + m, :], RR[:, m, :], ALU.mult).then_inc(o_f, 1)
                for m in range(4):
                    dve.wait_ge(o_hi, h * 4 + (m + 1))
                    dve.tensor_tensor(OL[:, m, :], RR[:, m, :], OH[:, m, :].bitcast(F32), ALU.subtract).then_inc(o_lo, 1)
                dve.wait_ge(y2_zero, 1)
                for u in range(2):
                    dve.wait_ge(weights_used, h * HEAD_CHUNKS + (N_STATIC + 12 + 2 * (u + 1)))
                    for t in range(TT):
                        dve.tensor_tensor(YO2[:, t, u * NC:(u + 1) * NC], PS[:, 4 * u + t, :], YO2[:, t, u * NC:(u + 1) * NC],
                                          ALU.add).then_inc(hd_dve, 1)
                assert seq.n == HSEQ_DVE
            seq.base, seq.n = 0, seq0 + HEADS * HSEQ_DVE

            dve.wait_ge(std5, 1)
            rstd(1)
            dve.wait_ge(prow1_in, 16)
            for t in range(TT):
                seq.inc(dve.scalar_tensor_tensor(YO2[:, t, :], YO2[:, t, :], STAT[:, 3, t:t + 1], PROW1[:, :], ALU.mult, ALU.mult))
            for t in range(TT):
                seq.wait(seq.n - TT + 1 + t)
                dve.tensor_tensor(YO2[:, t, :], X1[:, t, :], YO2[:, t, :], ALU.add).then_inc(fin, 1)

        @block.tensor
        def _(pe):
            state = {"n": 0}

            def free(name, skip=True):
                i = NAMES.index(name)
                if i < 2:
                    return
                prev = JOBS[i - 2]
                if _sum(3, i - 1):
                    pe.wait_ge(banks_act, _sum(3, i - 1))
                if _sum(4, i - 1):
                    pe.wait_ge(banks_dve, _sum(4, i - 1))
                if prev[5]:
                    pe.wait_ge(h_lo if prev[5][0] == "h" else y_lo, prev[5][1])

            halves = ((0, 0), (0, 1), (1, 0))

            def unit(n0, out_banks, acts, kt_ready, rows, tok=None, slot0=0, per=4):
                for q in range(per):
                    s = (slot0 + q) % RING
                    pe.wait_ge(w_lo, n0 + (q + 1))
                    for kk in range(2):
                        kt = 2 * q + kk
                        kt_ready(kt)
                        for m in range(4):
                            for i, (wi, ai) in enumerate(halves):
                                w, x = (WH, WL)[wi], acts(kt)[ai]
                                if rows:
                                    st, mv = tok(x, m), w[:, s, kk, :]
                                else:
                                    st, mv = w[:, s, kk, m * P:(m + 1) * P], x
                                mm = pe.matmul(out_banks[m], st, mv, start=(kt == 0 and i == 0), stop=(kt == 2 * per - 1 and i == 2))
                    mm.then_inc(weights_used, 1)

            def tile(x, m):
                return x[:, m * P:(m + 1) * P]

            def strided(x, m):
                return x.rearrange("p (c j) -> p j c", j=T4)[:, m, :]

            def acts_of(hi, lo):
                return lambda kt: (hi[:, kt, :], lo[:, kt, :])

            def ready(s, version):
                return lambda kt: pe.wait_ge(s, 8 * version + min(kt, 7) + 1)

            H, Y = acts_of(HH, HL), acts_of(YH, YL)

            def section(name, acts, r, rows=False, tok=tile, per=4):
                for u in range(2):
                    job = f"{name}.{u}"
                    free(job)
                    unit(chunks_before(job), [bank(job, m) for m in range(4)], acts, r if u == 0 else (lambda kt: None),
                         rows, tok, per=per)

            def run(names, acts, r):
                first = NAMES.index(names[0] + ".0")
                need = [(_sum(3, first + i - 1), _sum(4, first + i - 1)) for i in range(2 * len(names))]
                r(7)
                n0 = chunks_before(names[0] + ".0")
                da, dd = need[2][0] - need[0][0], need[2][1] - need[0][1]
                assert all(need[i + 2] == (need[i][0] + da, need[i][1] + dd) for i in range(2 * len(names) - 2)), names
                prev = [JOBS[first + i - 2][5] for i in range(2)]
                for p in prev:
                    if p:
                        pe.wait_ge(h_lo if p[0] == "h" else y_lo, p[1])
                with pe.Fori(0, len(names)) as s:
                    for u in range(2):
                        if need[u][0]:
                            pe.wait_ge(banks_act, s * da + need[u][0])
                        if need[u][1]:
                            pe.wait_ge(banks_dve, s * dd + need[u][1])
                        job = f"{names[0]}.{u}"
                        unit(s * 8 + (n0 + 4 * u), [bank(job, m) for m in range(4)], acts, lambda kt: None, False)

            def turn(job, srcs, sem_=None):
                free(job)
                for m, four in enumerate(srcs):
                    for t, (src, wait) in enumerate(four):
                        if wait:
                            wait()
                        mm = pe.transpose(bank(job, m)[:, t * P:(t + 1) * P], src, ident[:, :])
                    mm.then_inc(side_done, 1)

            def turn_tokens(job, x, kt0, s):
                turn(job, [[(x[:, t, (kt0 + m) * P:(kt0 + m + 1) * P], lambda t=t: pe.wait_ge(s, t + 1)) for t in range(TT)]
                           for m in range(4)])

            pe.wait_ge(consts, 4)
            pe.wait_ge(prm_in, 16 * 14)
            for i, n in enumerate((116, P, 8 * CONV_K - P)):
                mm = pe.transpose(bank("params", i)[:, 0:n], PR[0:n, i, :], ident[0:n, 0:n])
            mm.then_inc(side_done, 1)
            turn_tokens("h_t.0", XN0, 0, xn0)
            turn_tokens("h_t.1", XN0, 4, xn0)
            section("a_v", H, ready(h_lo, 0), rows=True)
            section("a_u", H, ready(h_lo, 0))
            pe.wait_ge(c_in, 16 * 64)
            free("c_t")
            for i in range(2):
                for t in range(4):
                    mm = pe.transpose(bank("c_t", i)[:, t * P:(t + 1) * P], CRAW[:, i, t, :], ident[:, :])
            mm.then_inc(side_done, 1)
            section("a_z", H, ready(h_lo, 0))
            pe.wait_ge(pool_w, 1)
            for i in range(4):
                free(f"w_t.{i}")
                for r in range(8):
                    for m in range(4):
                        ri, g = m // 2, m % 2
                        half = slice(64 * g, 64 * g + 64)
                        mm = pe.matmul(bank(f"w_t.{i}", m)[half, r * 64:(r + 1) * 64],
                                       WST[half, ri, 8 * i + r, :, :].rearrange("p j q -> p (j q)"), ident[half, half],
                                       start=True, stop=True)
                mm.then_inc(side_done, 1)
            pe.wait_ge(sgw_masked, 1)
            free("sgu_t")
            for g in range(SGU_GROUPS):
                mm = pe.transpose(bank("sgu_t", g // 4)[:, (g % 4) * P:(g % 4 + 1) * P], SGW[:, g, :], ident[:, :])
            mm.then_inc(side_done, 1)
            pe.wait_ge(pool_g, 1)
            pe.wait_ge(pool_rep, 2)
            for i in range(2):
                free(f"k.{i}")
                for r in range(8):
                    for m in range(4):
                        oc, g = 2 * i + m // 2, m % 2
                        pr, half = 8 * oc + r, slice(64 * g, 64 * g + 64)
                        for ri, lags in enumerate((GRE, GNI)):
                            mm = pe.matmul(bank(f"k.{i}", m)[half, r * 64:(r + 1) * 64],
                                           WST[half, ri, pr, :, :].rearrange("p j q -> p (j q)"),
                                           lags[half, pr, 0:T4, :].rearrange("p l q -> p (l q)"),
                                           start=(ri == 0), stop=(ri == 1))
                mm.then_inc(side_done, 1)
            section("g0", H, ready(h_lo, 0))
            pe.wait_ge(v_done, 4)
            for i in range(2):
                free(f"sgu.{i}")
                if i == 0:
                    pe.wait_ge(banks_act, act_after("sgu_t"))
                for m in range(4):
                    g = 4 * i + m
                    for t in range(TT):
                        mm = pe.matmul(bank(f"sgu.{i}", m)[:, t * P:(t + 1) * P], V[:, t, g * P:(g + 1) * P], SGWT[:, g, :],
                                       start=True, stop=True)
                mm.then_inc(side_done, 1)
            section("b_p", H, ready(h_lo, 0))
            section("w_a", Y, ready(y_lo, 0))
            section("b_z", H, ready(h_lo, 0))
            pe.wait_ge(pw_in, 16)
            for i in range(2):
                free(f"pool.{i}")
                for m in range(4):
                    kt = 4 * i + m
                    g = kt // 2
                    pe.wait_ge(d_ready, g + 1)
                    for k in range(2):
                        mm = pe.matmul(bank(f"pool.{i}", m), PW[:, g, k, (kt % 2) * P:(kt % 2 + 1) * P], U[:, 2 * g + k, :],
                                       start=(k == 0), stop=(k == 1))
                mm.then_inc(side_done, 1)
            section("g1", H, ready(h_lo, 0))
            section("c_h", H, ready(h_lo, 0))
            section("w_b", Y, ready(y_lo, 1))
            section("c_c", H, ready(h_lo, 0))
            section("g2", H, ready(h_lo, 0))
            section("c_b", H, ready(h_lo, 0))
            section("c_z", H, ready(h_lo, 0))
            section("w_c", Y, ready(y_lo, 2))
            section("w_out", H, ready(h_lo, 1), rows=True)
            turn_tokens("u_t.0", XN1, 0, xn1)
            turn_tokens("u_t.1", XN1, 4, xn1)
            section("b_val", H, ready(h_lo, 2))
            section("b_gate", H, ready(h_lo, 2))
            section("a_in", H, ready(h_lo, 2), rows=True, tok=strided)
            for u in range(2):
                pe.wait_ge(banks_act, act_after(f"a_in.{u}"))
                free(f"s5_t.{u}")
                for m in range(4):
                    for r in range(4):
                        pr = 4 * m + r
                        mm = pe.transpose(bank(f"s5_t.{u}", m)[:, r * P:(r + 1) * P],
                                          AS[:, u, 2 * pr:2 * pr + 2, :, :].rearrange("c g j q -> c (g j q)"), ident[:, :])
                mm.then_inc(side_done, 1)
            pe.wait_ge(wt_in, 16)
            for i in range(8):
                free(f"s5_z.{i}")
                pe.wait_ge(banks_act, act_after("s5_t.0" if i < 4 else "s5_t.1"))
                for r in range(4):
                    pr = 4 * i + r
                    for m in range(4):
                        ri, g = m // 2, m % 2
                        half = slice(64 * g, 64 * g + 64)
                        mm = pe.matmul(bank(f"s5_z.{i}", m)[half, r * P:(r + 1) * P], WT[half, ri, pr, :], UT[half, pr, :],
                                       start=True, stop=True)
                mm.then_inc(side_done, 1)
            section("a_z2", H, ready(h_lo, 2))
            section("b_z2", H, ready(h_lo, 2))
            pe.wait_ge(t6_in, 16)
            pe.wait_ge(vt_in, 16)
            pe.wait_ge(states, NCH)
            for i in range(2):
                free(f"s5_y.{i}")
                for r in range(8):
                    for m in range(4):
                        oc, g = 2 * i + m // 2, m % 2
                        pr, half = 8 * oc + r, slice(64 * g, 64 * g + 64)
                        o = bank(f"s5_y.{i}", m)[:, r * 64:(r + 1) * 64]
                        pe.matmul(o, UT[half, pr, :], T6[half, pr, :], start=True, stop=False)
                        pe.matmul(o, S[half, 0, pr, :], VT[half, 0, pr, :], start=False, stop=False)
                        mm = pe.matmul(o, S[half, 1, pr, :], VT[half, 1, pr, :], start=False, stop=True)
                mm.then_inc(side_done, 1)
            for i in range(2):
                pe.wait_ge(banks_act, act_after("s5_y.1"))
                turn(f"y_t.{i}", [[(YT[:, t, (4 * i + m) * P:(4 * i + m + 1) * P], None) for t in range(T4)] for m in range(4)])
            pe.wait_ge(ones_in, 1)
            pe.wait_ge(conv_done, 8)
            free("mean")
            for kt in range(KT):
                mm = pe.matmul(bank("mean", 0), ONES[:, :], CP[:, kt, CPAD:], start=(kt == 0), stop=(kt == KT - 1))
            mm.then_inc(side_done, 1)
            section("glu", Y, ready(y_lo, 3))
            free("var")
            for kt in range(KT):
                pe.wait_ge(z_sq, kt + 1)
                mm = pe.matmul(bank("var", 0), ONES[:, :], TMP[:, kt % 2, :], start=(kt == 0), stop=(kt == KT - 1))
                mm.then_inc(sq_used, 1)
            section("pw", Y, ready(y_lo, 4))
            both = lambda kt: H(kt) if kt < 8 else Y(kt - 8)
            section("ev_out", both, lambda kt: pe.wait_ge(h_lo, 24 + kt + 1) if kt < 8 else pe.wait_ge(y_lo, 40 + kt - 8 + 1),
                    rows=True, per=8)
            turn_tokens("u2_t.0", XN2, 0, xn2)
            turn_tokens("u2_t.1", XN2, 4, xn2)
            free("lr")
            pe.wait_ge(lw_lo, 1)
            pe.wait_ge(h_lo, 40)
            for kt in range(KT):
                for i, (wi, ai) in enumerate(halves):
                    mm = pe.matmul(bank("lr", 0), (LWH, LWL)[wi][:, kt, :], (HH, HL)[ai][:, kt, :],
                                   start=(kt == 0 and i == 0), stop=(kt == KT - 1 and i == 2))
            mm.then_inc(hd_side, HS0)
            pe.wait_ge(banks_act, act_after("lr"))

            with pe.Fori(0, HEADS) as h:
                A, B = [PS[:, m, :] for m in range(4)], [PS[:, 4 + m, :] for m in range(4)]
                nowait = lambda kt: None

                def chunk0(j):
                    return h * HEAD_CHUNKS + (N_STATIC + j)

                def evd(k):
                    return h * HDVE + (HD0 + k)

                def eva(k):
                    return h * HACT + k

                pe.wait_ge(hd_dve, evd(-4))
                unit(chunk0(0), A, H, nowait, False)
                pe.wait_ge(hd_dve, evd(0))
                pe.wait_ge(gu_in, h * 32 + 32)
                for m in range(2):
                    mm = pe.matmul(B[m], GU[0:LOWRANK + 1, m * P:(m + 1) * P], LR[0:LOWRANK + 1, :], start=True, stop=True)
                mm.then_inc(hd_side, 1)
                pe.wait_ge(hd_act, eva(4))
                unit(chunk0(4), A, H, nowait, True, tile)
                pe.wait_ge(hd_dve, evd(2))
                unit(chunk0(8), B, H, nowait, False)
                pe.wait_ge(hd_act, eva(8))
                pe.wait_ge(kd_done, h + 1)
                for t in range(TT):
                    for k in range(2):
                        mm = pe.transpose(A[t // 2][:, ((t % 2) * 2 + k) * P:((t % 2) * 2 + k + 1) * P],
                                          KDC[:, k, t * P:(t + 1) * P], ident[:, :])
                mm.then_inc(hd_side, 1)
                pe.wait_ge(hd_act, eva(12))
                pe.wait_ge(ke_done, h + 1)
                for t in range(TT):
                    for k in range(2):
                        mm = pe.matmul(B[0][:, t * P:(t + 1) * P], KE[:, k, t * P:(t + 1) * P], QD[:, k, t * P:(t + 1) * P],
                                       start=(k == 0), stop=(k == 1))
                mm.then_inc(hd_side, 1)
                pe.wait_ge(hd_act, eva(14))
                pe.wait_ge(hd_dve, evd(6))

                def delta(c):
                    if c >= 2:
                        pe.wait_ge(st_done, h * HST + st_after(c - 2))
                    half = slice(64 * (c % 2), 64 * (c % 2) + 64)
                    for k in range(2):
                        mm = pe.matmul(B[2 * (c % 2) + k], KTK[half, c // 2, k, :], V2[half, c // 2, :], start=True, stop=True)
                    mm.then_inc(hd_side, 1)

                delta(0)
                for c in range(GCH):
                    t, half = c // 2, slice(64 * (c % 2), 64 * (c % 2) + 64)
                    if c % 2 == 0:
                        pe.matmul(A[t], ATS[:, t, :], V2[:, t, :], start=True, stop=False, skip_group_check=True)
                    if c + 1 < GCH - 1:
                        delta(c + 1)
                    if c:
                        pe.wait_ge(st_done, h * HST + st_after(c - 1))
                        for k in range(2):
                            mm = pe.matmul(A[t][half, :], QD[:, k, c * CHUNK:(c + 1) * CHUNK], ST[:, (c - 1) % 2, k, :],
                                           start=False, stop=(k == 1), skip_group_check=True)
                        mm.then_inc(hd_side, 1)
                pe.wait_ge(st_done, h * HST + HST)
                for m in range(4):
                    for t in range(TT):
                        if m == 0:
                            pe.wait_ge(hd_dve, evd(6 + t + 1))
                        mm = pe.transpose(B[m][:, t * P:(t + 1) * P], ON[:, t, m * P:(m + 1) * P], ident[:, :])
                    mm.then_inc(hd_side, 1)
                O = acts_of(OH, OL)
                o_ready = lambda kt: pe.wait_ge(o_lo, h * 4 + (kt + 1))
                unit(chunk0(12), A, O, o_ready, True, tile, slot0=0, per=2)
                pe.wait_ge(o_f, h * 4 + 4)
                unit(chunk0(14), B, O, nowait, True, tile, slot0=2, per=2)


def kernel(**inputs):
    import numpy as _np
    import concourse.bacc as _bacc
    from concourse import mybir as _mybir
    from concourse.bass_utils import run_bass_kernel_spmd as _run

    nc = _bacc.Bacc("TRN2", target_bir_lowering=False, num_devices=1)
    arrays, args = {}, {}
    for name in inputs:
        v = _np.ascontiguousarray(inputs[name])
        arrays[f"in_{name}_dram"] = v
        args[name] = nc.dram_tensor(f"in_{name}_dram", v.shape, _mybir.dt.from_np(v.dtype), kind="ExternalInput").ap()
    out = nc.dram_tensor("out_0_dram", (1, SEQ, D), _mybir.dt.float32, kind="ExternalOutput").ap()
    three_branch_s5_gla_kernel(nc, args, out)
    r = _run(nc, [arrays], core_ids=[0])
    return r.results[0]["out_0_dram"]
```

```python
from contextlib import ExitStack

import numpy as np
import concourse.bass as bass
from concourse import mybir

F32 = mybir.dt.float32
F32R = mybir.dt.float32r
U32 = mybir.dt.uint32
ALU = mybir.AluOpType
ACT = mybir.ActivationFunctionType

P = 128
SEQ = 512
D = 1024
KT = D // P
TT = SEQ // P
NC = 512
RING = 4
SGU_GROUPS = 8
CHUNK = 64
POOL_WINDOWS = (2, 4, 8, 16)
PPAD = 16
CONV_K = 31
CPAD = CONV_K - 1
RMS_EPS = 1e-6
LN_EPS = 1e-5
S5_GROUP = 16
S5_STATE = 64
SEG, SEG_CH = 8, 16
T4 = 4
NCH = SEQ // T4
FB = 8
PAIRS = D // (2 * S5_GROUP)
HEADS = 4
HK = 256
HV = 512
LOWRANK = 16
GLA_TAU = 16.0
GCH = SEQ // CHUNK

TWO_PI = 2.0 * np.pi
PI_A = 6.28125
PI_B = float(np.float32(np.floor((TWO_PI - PI_A) * 2 ** 21) / 2 ** 21))
PI_C = float(np.float32(TWO_PI - PI_A - PI_B))
ROUND = 12582912.0

VEC = {n: i for i, n in enumerate(
    ["norm_g", "pool_b", "pool_scale", "conv_w0", "conv_w1", "conv_w2", "conv_b", "norm_pre0", "norm_pre1",
     "b_glu", "conv_b_2", "ln_g2", "ln_b2", "b_pw", "gla_norm_g"])}
VEC_CONV = 16
N_VEC = VEC_CONV + CONV_K

JOBS = []


def _add(name, chunks=0, side=0, a=0, d=0, lo=None):
    JOBS.append((name, chunks, side, a, d, lo))


def _section(name, a=0, d=0, chunks=4):
    for u in range(2):
        _add(f"{name}.{u}", chunks, 0, a, d)


_add("params", side=1, a=3)
_add("h_t.0", side=4, lo=("h", 4))
_add("h_t.1", side=4, lo=("h", 8))
_section("a_v", a=4)
_add("c_t", side=1, a=2)
_section("a_u", a=4)
_section("a_z", a=4)
for _i in range(4):
    _add(f"w_t.{_i}", side=1, a=2, d=2)
_add("sgu_t", side=1, a=2)
_section("g0", a=4)
for _i in range(2):
    _add(f"k.{_i}", side=1, d=4)
for _i in range(2):
    _add(f"sgu.{_i}", side=1, d=4)
_section("b_p", a=4)
_section("w_a", d=4)
_section("b_z", a=4)
for _i in range(2):
    _add(f"pool.{_i}", side=1, d=4)
_section("g1", a=4)
_section("c_h", a=4)
_section("w_b", d=4)
_section("c_c", d=4)
_section("g2", a=4)
_section("c_b", d=4)
_section("c_z", a=4)
_section("w_c", d=4)
_section("w_out", d=4)
_add("u_t.0", side=4, lo=("h", 20))
_add("u_t.1", side=4, lo=("h", 24))
_add("b_val.0", 4, 0, 4)
_add("b_gate.0", 4, 0, 4)
_section("a_in", a=4)
for _u in range(2):
    _add(f"s5_t.{_u}", side=1, a=4)
for _i in range(4):
    _add(f"s5_z.{_i}", side=1, a=4)
_add("b_val.1", 4, 0, 4)
_add("b_gate.1", 4, 0, 4)
_section("a_z2", a=4)
_section("b_z2", a=4)
for _i in range(2):
    _add(f"s5_y.{_i}", side=1, a=4)
for _i in range(2):
    _add(f"y_t.{_i}", side=4, lo=("y", 8 * 3 + 4 * (_i + 1)))
_section("glu", a=4)
_add("mean", side=1, d=1)
_add("ev_a.0", 4, 0, 4)
_add("var", a=1)
_add("ev_a.1", 4, 0, 4)
_section("pw", d=4)
_section("ev_b", d=4)
_add("u2_t.0", side=4, lo=("h", 44))
_add("u2_t.1", side=4, lo=("h", 48))
_add("lr", a=1)
NAMES = [j[0] for j in JOBS]


def _sum(column, upto):
    return sum(j[column] for j in JOBS[:upto])


def chunks_before(name):
    return _sum(1, NAMES.index(name))


def used_after(name):
    return _sum(1, NAMES.index(name) + 1)


def side_after(name, k=0):
    i = NAMES.index(name)
    return _sum(2, i) + (k if k else JOBS[i][2])


def act_after(name, k=0):
    i = NAMES.index(name)
    return _sum(3, i) + (k if k else JOBS[i][3])


def dve_after(name, k=0):
    i = NAMES.index(name)
    return _sum(4, i) + (k if k else JOBS[i][4])


UNITS = [j[0] for j in JOBS if j[1]]
N_STATIC = _sum(1, len(JOBS))
HEAD_CHUNKS = 16
V_AT, R_AT, QK_AT = 0, 4, 8
HST = 5
HSEQ_ACT, HSEQ_DVE = 4, 12


def out_at(last):
    return QK_AT if last else QK_AT + 4


def head_base(h):
    return h * HEAD_CHUNKS + (N_STATIC + 4)


def loaded(h, at, last=False):
    before = 16 * (N_STATIC // RING) + 32
    return h * 80 + before + {V_AT: 16, R_AT: 32, QK_AT: 48 if last else 64, QK_AT + 4: 80}[at]


W_IN = {n: i * D for i, n in enumerate(
    ["a_u", "a_v", "a_z", "b_p", "b_z", "c_h", "c_b", "c_c", "c_z", "g0", "g1", "g2"])}
EV_IN = {n: i * D for i, n in enumerate(["a_in", "a_z2", "b_val", "b_gate", "b_z2"])}


class Order:

    def __init__(self, eng, sem):
        self.eng, self.sem, self.n, self.base = eng, sem, 0, 0

    def inc(self, instruction):
        instruction.then_inc(self.sem, 1)
        self.n += 1
        return self.n

    def wait(self, n=None):
        self.eng.wait_ge(self.sem, self.base + (self.n if n is None else n))


def three_branch_s5_gla_kernel(nc, a, out):
    ctx = ExitStack()
    with ctx:
        def sem(name):
            return ctx.enter_context(nc.semaphore(name))

        at = {}
        start = nc.sbuf_base + -nc.sbuf_base % 32

        def region(name, size):
            at[name] = region.top
            region.top += size
        region.top = start
        for name, size in (("WR", 16384), ("WH", 16384), ("WL", 16384), ("HH", 16384), ("HL", 16384),
                           ("YH", 16384), ("YL", 16384), ("R1", 17344), ("R2", 16384), ("R3", 16384),
                           ("R4", 16384), ("R5", 16384), ("R6", 8192), ("ident", 512), ("PRM", 4 * 8 * N_VEC),
                           ("TMP", 4096), ("LAM", 384), ("SMALL", 376)):
            region(name, size)
        ctx.enter_context(nc.sbuf_tensor("arena", [P, (region.top - nc.sbuf_base + 3) // 4], F32))

        def put(name, where, shape, dt=F32, skip=0):
            return nc.alloc_sbuf_tensor_at(name, [P, *shape], dt, offset=at[where] + skip, align_bytes=4)

        WR = put("WR", "WR", [RING, 2, NC])
        WH = put("WH", "WH", [RING, 2, NC], F32R)
        WL = put("WL", "WL", [RING, 2, NC], F32R)
        HH = put("HH", "HH", [KT, SEQ], F32R)
        HL = put("HL", "HL", [KT, SEQ], F32R)
        YH = put("YH", "YH", [KT, SEQ], F32R)
        YL = put("YL", "YL", [KT, SEQ], F32R)
        ident = put("ident", "ident", [P])
        PRM = put("PRM", "PRM", [8 * N_VEC])
        TMP = put("TMP", "TMP", [2, NC])
        XN0 = put("XN0", "R1", [TT, D])
        V = put("V", "R1", [TT, D])
        CH = put("CH", "R1", [KT, PPAD + SEQ])
        U = put("U", "R2", [KT, SEQ])
        X = put("X", "R3", [TT, D])
        WIN = put("WIN", "R3", [3, PPAD + SEQ])
        M = put("M", "R4", [KT, SEQ])
        XN1 = put("XN1", "R4", [TT, D])
        G = put("G", "R5", [KT, SEQ])
        LNROWS = put("LNROWS", "R5", [2, D])
        SGW = put("SGW", "R5", [SGU_GROUPS, P], skip=8192)
        SGWT = put("SGWT", "R6", [SGU_GROUPS, P])
        SGB = put("SGB", "R6", [SGU_GROUPS, P], skip=4096)
        PW = put("PW", "R6", [4, 2, 256])
        FROW = put("FROW", "R6", [D])
        PR = put("PR", "R6", [3, P])
        GRE = put("GRE", "YH", [PAIRS, 5, S5_GROUP])
        GNI = put("GNI", "YH", [PAIRS, 5, S5_GROUP], skip=10240)
        TM = put("TM", "YH", [PAIRS, 64], skip=20480)
        CRAW = put("CRAW", "YH", [2, 4, P], skip=28672)
        WST = put("WST", "R4", [2, PAIRS, T4, S5_GROUP])
        BRAW = put("BRAW", "R5", [2, PAIRS, S5_GROUP], skip=12288)
        WTS = put("WTS", "R3", [2, PAIRS, 64])
        PT = put("PT", "R3", [2, PAIRS, S5_GROUP])
        DT2 = put("DT2", "R3", [PAIRS, 64], skip=4096)
        LS = put("LS", "R6", [20, PAIRS], skip=1536)
        LAM = put("LAM", "LAM", [3, PAIRS])
        DCOL = put("DCOL", "SMALL", [PAIRS])
        INVC = put("INVC", "SMALL", [PPAD], skip=128)
        MJ = put("MJ", "SMALL", [4], skip=192)
        MJ8 = put("MJ8", "SMALL", [2, 4], skip=208)
        ST1 = put("ST1", "SMALL", [2, PAIRS])
        ST2 = put("ST2", "PRM", [2, PAIRS])
        STAT = put("STAT", "SMALL", [4, 4], skip=272)
        BNA = put("BNA", "SMALL", [4, 2], skip=336)
        EPS = put("EPS", "SMALL", [2], skip=368)
        BNS = put("BNS", "TMP", [TT, 2, 6])
        CP = put("CP", "R1", [KT, CPAD + SEQ])
        UT = put("UT", "R2", [PAIRS, NCH])
        YA = put("YA", "R2", [KT, SEQ])
        WT = [put("WT_re", "R3", [PAIRS, P]), put("WT_im", "R5", [PAIRS, P])]
        VT = [put("VT_0", "R3", [2, PAIRS // 2, P]), put("VT_1", "HL", [2, PAIRS // 2, P])]
        T6 = [put("T6_0", "R5", [PAIRS // 2, P], skip=8192), put("T6_1", "R6", [PAIRS // 2, P])]
        X1 = put("X1", "R3", [TT, D])
        AS = put("AS", "R4", [2, 32, T4, S5_GROUP])
        AZ = put("AZ", "R4", [KT, SEQ])
        BZ = put("BZ", "R5", [KT, SEQ])
        XN2 = put("XN2", "R5", [TT, D])
        MU = put("MU", "R6", [SEQ])
        RS = put("RS", "R6", [SEQ])
        ONES = put("ONES", "R6", [P], skip=2048)
        GLUV = put("GLUV", "R6", [2, NC], skip=4096)
        GATEV = put("GATEV", "R4", [2, NC])
        SQ = put("SQ", "R3", [KT, SEQ])
        TAB = put("TAB", "R6", [2, PAIRS, SEG_CH])
        LAM64 = put("LAM64", "R6", [3, PAIRS], skip=4096)
        Q0 = put("Q0", "R6", [2, PAIRS, SEG_CH // 2], skip=4608)
        SEG1 = put("SEG1", "R5", [2, PAIRS, SEG])
        SEG2 = put("SEG2", "R5", [2, PAIRS, SEG], skip=2048)
        FIX = put("FIX", "R5", [2, FB, SEG - 1, SEG_CH - 1])
        PROW0 = put("PROW0", "R6", [D], skip=4096)
        S = put("S", "YH", [2, PAIRS, NCH])
        YT = put("YT", "HH", [T4, D])
        YO = put("YO", "R2", [TT, D])
        YO2 = put("YO2", "R2", [TT, D])
        QK = put("QK", "R1", [4, SEQ])
        BC = put("BC", "R1", [2, SEQ], skip=8192)
        ET = put("ET", "R1", [2, SEQ], skip=12288)
        LWR = put("LWR", "R4", [KT, LOWRANK], skip=8192)
        LWH = put("LWH", "R4", [KT, P], F32R)
        LWL = put("LWL", "R4", [KT, P], F32R, skip=4096)
        QD = put("QD", "R4", [2, SEQ])
        KE = put("KE", "R4", [2, SEQ], skip=4096)
        KD1 = put("KD1", "R4", [2, TT, CHUNK], skip=8192)
        KTK = put("KTK", "R4", [TT, 2, P], skip=12288)
        PROW1 = put("PROW1", "R4", [D])
        V2 = put("V2", "R5", [TT, HV])
        RR = put("RR", "R5", [4, SEQ], skip=8192)
        ATS = put("ATS", "R6", [TT, P])
        CMASK = put("CMASK", "R6", [P], skip=2048)
        SMASK = put("SMASK", "R6", [2 * SEQ], skip=2560)
        GU = put("GU", "R6", [HK], skip=6656)
        LR = put("LR", "TMP", [SEQ])
        DEC = put("DEC", "TMP", [2, GCH], skip=2048)
        DD = put("DD", "TMP", [2, TT], skip=2112)
        OH = put("OH", "YH", [4, SEQ], F32R)
        OL = put("OL", "YH", [4, SEQ], F32R, skip=8192)
        ST = put("ST", "YL", [2, 2, HV])
        ON = put("ON", "YL", [TT, HV], skip=8192)
        KX = put("KX", "YL", [2, SEQ], skip=8192)
        QX = put("QX", "YL", [2, SEQ], skip=12288)

        PS = ctx.enter_context(nc.psum_tensor("PS", [P, 8, NC], F32))

        def bank(name, m):
            return PS[:, 4 * (NAMES.index(name) % 2) + m, :]

        d_wt = nc.dram_tensor("d_wt", [P, 2, PAIRS, P], F32, kind="Internal").ap()
        d_g = nc.dram_tensor("d_g", [P, 2, PAIRS, P], F32, kind="Internal").ap()
        d_tm = nc.dram_tensor("d_tm", [P, PAIRS, P], F32, kind="Internal").ap()
        d_x1 = nc.dram_tensor("d_x1", [SEQ, D], F32, kind="Internal").ap()

        w_loaded = [sem(f"w_loaded{i}") for i in range(RING)]
        w_hi, w_lo, weights_used = sem("w_hi"), sem("w_lo"), sem("weights_used")
        banks_act, banks_dve, side_done = sem("banks_act"), sem("banks_dve"), sem("side_done")
        act_seq, dve_seq, pool_seq = sem("act_seq"), sem("dve_seq"), sem("pool_seq")
        h_hi, h_lo, y_hi, y_lo = sem("h_hi"), sem("h_lo"), sem("y_hi"), sem("y_lo")
        x_in, prm_in, lam_in, c_in, b_in, sg_in, ln_in, d_in, bs_in = (sem(n) for n in (
            "x_in_unused", "prm_in", "lam_in", "c_in", "b_in", "sg_in", "ln_in", "d_in", "bs_in"))
        pw_in, x_again, frow_in, wt_in, vt_in, t6_in, x1_out, x1_in, prow0_in = (sem(n) for n in (
            "pw_in", "x_again", "frow_in", "wt_in", "vt_in", "t6_in", "x1_out", "x1_in", "prow0_in"))
        s5_out, zeros_out = sem("s5_out"), sem("zeros_out")
        x_in = [sem(f"x_in{t}") for t in range(TT)]
        zeroed = sem("zeroed")
        consts = sem("consts")
        sq0, std0, xn0 = sem("sq0"), sem("std0"), sem("xn0")
        v_std, v_done = sem("v_std"), sem("v_done")
        m_acc, sq_used, ke_done = sem("m_acc"), sem("sq_used"), sem("ke_done")
        lam_exp, lam_ang, lam_sin, lam_den, lam_rec = (sem(n) for n in (
            "lam_exp", "lam_ang", "lam_sin", "lam_den", "lam_rec"))
        pool_g, pool_w, pool_t = sem("pool_g"), sem("pool_w"), sem("pool_t")
        pool_rep = sem("pool_rep")
        sgw_masked = sem("sgw_masked")
        tmp_free = sem("tmp_free")
        ya_ready, d_ready, yb_ready, pads = sem("ya_ready"), sem("d_ready"), sem("yb_ready"), sem("pads")
        cpads = sem("cpads")
        x1_done, xn1, sq1, std1, sq2, std2 = (sem(n) for n in (
            "x1_done", "xn1", "sq1", "std1", "sq2", "std2"))
        states, conv_done = sem("states"), sem("conv_done")
        carried, states_fixed = sem("carried"), sem("states_fixed")
        ya_final, z_cent, z_sq, z_norm, z_act, ones_in = (sem(n) for n in (
            "ya_final", "z_cent", "z_sq", "z_norm", "z_act", "ones_in"))
        sq3, std3, x2_done, sq4, std4, xn2 = (sem(n) for n in ("sq3", "std3", "x2_done", "sq4", "std4", "xn2"))
        lw_in, lw_zero, lw_hi, lw_lo, gla_consts = (sem(n) for n in (
            "lw_in", "lw_zero", "lw_hi", "lw_lo", "gla_consts"))
        gu_in = sem("gu_in")
        e_abs, g_scan, e_q, e_ke, e_d, dec_in, qd_done, kx_done, qx_done = (sem(n) for n in (
            "e_abs", "g_scan", "e_q", "e_ke", "e_d", "dec_in", "qd_done", "kx_done", "qx_done"))
        lr_out, g_out, kt_out, sc_out, d_out, o_out, ot_out = (sem(n) for n in (
            "lr_out", "g_out", "kt_out", "sc_out", "d_out", "o_out", "ot_out"))
        qk_copied, v_copied, r_copied, kt_copied = (sem(n) for n in (
            "qk_copied", "v_copied", "r_copied", "kt_copied"))
        g_read, ats_copied, on_done, y2_add = (sem(n) for n in (
            "g_read", "ats_copied", "on_done", "y2_add"))
        o_sq, o_std, o_f, o_hi, o_lo, rr_in, st_done = (sem(n) for n in (
            "o_sq", "o_std", "o_f", "o_hi", "o_lo", "rr_in", "st_done"))
        sq5, std5, fin, fin_out, prow1_in = sem("sq5"), sem("std5"), sem("fin"), sem("fin_out"), sem("prow1_in")

        def col(name, kt, n=1):
            c = 8 * VEC[name] + kt
            return PRM[:, c:c + n]

        def tokens(dram):
            return dram.rearrange("(t p) d -> p t d", p=P)

        def correction(b, ri, q, slot):
            seg = S[:, :, FB * b:FB * b + FB, :].rearrange("p r g (s j) -> p r g s j", j=SEG_CH)
            shape = [P, FB, SEG - 1, SEG_CH - 1]
            return (FIX[:, slot], seg[:, ri, :, 1:SEG, 0:SEG_CH - 1],
                    TAB[:, q, FB * b:FB * b + FB, 0:SEG_CH - 1].unsqueeze(2).to_broadcast(shape),
                    seg[:, ri ^ q, :, 0:SEG - 1, SEG_CH - 1:SEG_CH].to_broadcast(shape),
                    ALU.subtract if (ri, q) == (0, 1) else ALU.add)

        x_d = tokens(a["x"][0])
        ctx.enter_context(nc.allow_non_contiguous_dma(reason="small S5 tables, loaded once"))
        block = ctx.enter_context(nc.Block())

        @block.sync
        def _(sp):
            for t in range(TT):
                sp.dma_start(X[:, t, :], x_d[:, t, :]).then_inc(x_in[t], 16)
            sp.dma_start(PR[0:8, 0, :], a["norm_g"].rearrange("o (r p) -> (o r) p", p=P)).then_inc(prm_in, 16)
            rows = [("pool_b", 1), ("pool_scale", 1), ("conv_w", 3), ("conv_b", 1), ("norm_pre_2", 2), ("s5_b_glu_2", 1),
                    ("conv_b_2", 1), ("conv_ln_g_2", 1), ("conv_ln_b_2", 1), ("conv_b_pw_2", 1)]
            r0 = 8
            for name, n in rows:
                src = a[name][0] if name == "conv_w" else a[name]
                sp.dma_start(PR[r0:r0 + 8 * n, 0, :], src.rearrange("k (r p) -> (k r) p", p=P)).then_inc(prm_in, 16)
                r0 += 8 * n
            sp.dma_start(PR[r0:r0 + 4, 0, :], a["gla_norm_g_2"].rearrange("o (r p) -> (o r) p", p=P)).then_inc(prm_in, 16)
            taps = a["conv_w_2"][0].rearrange("k (r p) -> (k r) p", p=P)
            sp.dma_start(PR[:, 1, :], taps[0:P, :]).then_inc(prm_in, 16)
            sp.dma_start(PR[0:8 * CONV_K - P, 2, :], taps[P:8 * CONV_K, :]).then_inc(prm_in, 16)

            def halves_out(dst, src, which):
                for g in range(2):
                    half = slice(64 * g, 64 * g + 64)
                    sp.dma_start(dst[half, :, half], src(half)).then_inc(which, 16)

            def chunk(n, src, first=False):
                slot = n % RING
                if n >= RING:
                    sp.wait_ge(w_lo, n - RING + 1)
                sp.dma_start(WR[:, slot, :, :], src.rearrange("(k p) n -> p k n", p=P)).then_inc(w_loaded[slot], 16)

            def c_tables():
                for i, name in enumerate(("s5_c_re_2", "s5_c_im_2")):
                    src = a[name][0].rearrange("(t r g) p n -> r g p t n", r=8, g=2)
                    for r in range(8):
                        for g in range(2):
                            sp.dma_start(CRAW[16 * r:16 * r + 16, i, :, 64 * g:64 * g + 64], src[r, g]).then_inc(c_in, 16)

            def unit(name, src, col0):
                for q in range(4):
                    chunk(chunks_before(name) + q, src[q * 2 * P:(q + 1) * 2 * P, col0:col0 + NC])

            def section(name, src, col0, rows=D):
                n0 = chunks_before(name + ".0")
                per = rows // (2 * P)
                if n0 < RING:
                    for u in range(2):
                        if u:
                            c_tables()
                        for q in range(per):
                            chunk(n0 + u * per + q, src[q * 2 * P:(q + 1) * 2 * P, col0 + u * NC:col0 + (u + 1) * NC])
                    return
                with sp.Fori(0, 2) as u:
                    for q in range(per):
                        slot = q % RING
                        sp.wait_ge(w_lo, u * per + (n0 + q - RING + 1))
                        sp.dma_start(WR[:, slot, :, :],
                                     src[q * 2 * P:(q + 1) * 2 * P, bass.ds(u * NC + col0, NC)]
                                     .rearrange("(k p) n -> p k n", p=P)).then_inc(w_loaded[slot], 16)

            w_in, ev_in = a["w_in"][0], a["ev_w_in_2"][0]
            section("a_v", w_in, W_IN["a_v"])
            sp.wait_ge(zeroed, 1)
            for m in (d_wt[:, 0], d_wt[:, 1], d_g[:, 0], d_g[:, 1], d_tm):
                for g in range(2):
                    rows, cols = slice(64 * g, 64 * g + 64), slice(64 - 64 * g, P - 64 * g)
                    sp.dma_start(m[rows, :, cols],
                                 TMP[rows, 0, 0:64].unsqueeze(1).to_broadcast([64, PAIRS, 64])).then_inc(zeros_out, 16)
            section("a_u", w_in, W_IN["a_u"])
            section("a_z", w_in, W_IN["a_z"])
            section("g0", w_in, W_IN["g0"])
            sp.wait_ge(pool_g, 1)
            halves_out(d_g[:, 0], lambda h: GRE[h, :, 1:5, :].rearrange("p r t q -> p r (t q)"), s5_out)
            halves_out(d_g[:, 1], lambda h: GNI[h, :, 1:5, :].rearrange("p r t q -> p r (t q)"), s5_out)
            sp.wait_ge(banks_act, act_after("w_t.3"))
            sp.wait_ge(banks_dve, dve_after("w_t.3"))
            for ri in range(2):
                halves_out(d_wt[:, ri], lambda h: WTS[h, ri, :, :], s5_out)
            section("b_p", w_in, W_IN["b_p"])
            sp.wait_ge(banks_dve, dve_after("k.1"))
            halves_out(d_tm, lambda h: TM[h, :, :], s5_out)
            sp.wait_ge(side_done, side_after("sgu.1"))
            sp.wait_ge(ya_ready, 8)
            sp.dma_start(PW[:, :, :, :], a["pool_w"][0].rearrange("g (k p) d -> p g k d", p=P)).then_inc(pw_in, 16)
            section("w_a", a["w_branch_a"][0], 0)
            section("b_z", w_in, W_IN["b_z"])
            section("g1", w_in, W_IN["g1"])
            sp.wait_ge(d_ready, 4)
            sp.wait_ge(s5_out, 16 * 10)
            sp.dma_start(X[:, :, :], x_d).then_inc(x_again, 16)
            section("c_h", w_in, W_IN["c_h"])
            sp.wait_ge(side_done, side_after("pool.1"))
            sp.dma_start(FROW[:, :], a["final_g"].rearrange("(o n) -> o n", o=1).broadcast_to([P, D])).then_inc(frow_in, 16)
            section("w_b", a["w_branch_b"][0], 0)
            for name in ("c_c", "g2", "c_b", "c_z"):
                section(name, w_in, W_IN[name])
            section("w_c", a["w_branch_c"][0], 0)
            section("w_out", a["w_out"][0], 0)
            unit("b_val.0", ev_in, EV_IN["b_val"])
            sp.wait_ge(x1_done, 4)
            sp.dma_start(tokens(d_x1), X[:, :, :]).then_inc(x1_out, 16)
            unit("b_gate.0", ev_in, EV_IN["b_gate"])
            sp.wait_ge(x1_out, 16)
            sp.wait_ge(xn1, 4)
            sp.wait_ge(zeros_out, 16 * 10)
            sp.wait_ge(m_acc, 16)
            for ri in range(2):
                sp.dma_start(WT[ri][:, :, :].rearrange("p r n -> p (r n)"), d_wt[:, ri].rearrange("p r n -> p (r n)")).then_inc(wt_in, 16)
            section("a_in", ev_in, EV_IN["a_in"])
            unit("b_val.1", ev_in, EV_IN["b_val"] + NC)
            unit("b_gate.1", ev_in, EV_IN["b_gate"] + NC)
            sp.wait_ge(side_done, side_after("s5_z.3"))

            def vt_in_half(i):
                sp.dma_start(VT[i][:, :, :, :].rearrange("p r g n -> p r (g n)"),
                             d_g[:, :, 16 * i:16 * i + 16, :].rearrange("p r g n -> p r (g n)")).then_inc(vt_in, 16)

            def t6_in_half(i):
                sp.dma_start(T6[i][:, :, :].rearrange("p g n -> p (g n)"),
                             d_tm[:, 16 * i:16 * i + 16, :].rearrange("p g n -> p (g n)")).then_inc(t6_in, 16)

            vt_in_half(0)
            t6_in_half(0)
            section("a_z2", ev_in, EV_IN["a_z2"])
            section("b_z2", ev_in, EV_IN["b_z2"])
            sp.wait_ge(states_fixed, 2)
            t6_in_half(1)
            sp.wait_ge(weights_used, used_after("b_z2.1"))
            vt_in_half(1)
            section("glu", a["s5_w_glu_2"][0], 0)
            ev_out = a["ev_w_out_2"][0]
            section("ev_a", ev_out[0:D, :], 0)
            sp.wait_ge(sq_used, KT)
            sp.dma_start(X1[:, :, :], tokens(d_x1)).then_inc(x1_in, 16)
            sp.wait_ge(tmp_free, 32)
            sp.dma_start(PROW0[:, :], a["norm_post_2"][0:1, :].broadcast_to([P, D])).then_inc(prow0_in, 16)
            section("pw", a["conv_w_pw_2"][0], 0)
            section("ev_b", ev_out[D:2 * D, :], 0)
            od_in, od_out = a["od_w_in_2"][0], a["od_w_out_2"][0]

            def head_chunk(n, j, pieces):
                sp.wait_ge(w_lo, n + (j - RING + 1))
                for c0, width, src in pieces:
                    sp.dma_start(WR[:, j % RING, :, c0:c0 + width],
                                 src.rearrange("(k p) n -> p k n", p=P)).then_inc(w_loaded[j % RING], 16)

            def in_rows(q, col, width):
                return od_in[q * 2 * P:(q + 1) * 2 * P, bass.ds(col, width)]

            def qk_in(n, h):
                for q in range(4):
                    head_chunk(n, q, [(0, HK, in_rows(q, h * HK, HK)), (HK, HK, in_rows(q, h * HK + HEADS * HK, HK))])

            def gu_rows(h):
                sp.dma_start(GU[0:LOWRANK, :], a["gla_w_gate_up_2"][0][:, bass.ds(h * HK, HK)]).then_inc(gu_in, 16)
                sp.dma_start(GU[LOWRANK:LOWRANK + 1, :], a["gla_b_gate_2"][0:1, bass.ds(h * HK, HK)]).then_inc(gu_in, 16)

            qk_in(N_STATIC, 0)
            sp.wait_ge(x2_done, 4)
            gu_rows(0)

            def head(h, last):
                n = head_base(h)
                for q in range(4):
                    head_chunk(n, V_AT + q, [(0, HV, in_rows(q, h * HV + 2 * HEADS * HK, HV))])
                for q in range(4):
                    head_chunk(n, R_AT + q, [(0, HV, in_rows(q, h * HV + (2 * HEADS * HK + HEADS * HV), HV))])
                if not last:
                    sp.wait_ge(g_out, h + 1)
                    gu_rows(h + 1)
                    qk_in(n + QK_AT, h + 1)
                for u in range(2):
                    for q in range(2):
                        head_chunk(n, out_at(last) + 2 * u + q,
                                   [(0, NC, od_out[bass.ds(h * HV + q * 2 * P, 2 * P), u * NC:(u + 1) * NC])])

            with sp.Fori(0, HEADS - 1) as h:
                head(h, False)
            head(HEADS - 1, True)
            sp.wait_ge(ot_out, 4 * HEADS)
            sp.dma_start(PROW1[:, :], a["norm_post_2"][1:2, :].broadcast_to([P, D])).then_inc(prow1_in, 16)
            sp.wait_ge(fin, 4)
            sp.dma_start(tokens(out[0]), YO2[:, :, :]).then_inc(fin_out, 16)
            sp.wait_ge(fin_out, 16)

        @block.gpsimd
        def _(pool):
            seq = Order(pool, pool_seq)
            pool.memset(TMP[:, :, :], 0.0).then_inc(zeroed, 1)
            for i, name in enumerate(("s5_b_re_2", "s5_b_im_2")):
                pool.dma_start(BRAW[:, i, :, :], a[name][0].rearrange("(r g) n q -> (g n) r q", g=2)).then_inc(b_in, 16)
            seq.inc(pool.memset(ident[:, :], 0.0))
            seq.inc(pool.memset(MJ8[:, :, :], 1.0))
            pool.memset(EPS[:, 0:1], RMS_EPS).then_inc(consts, 1)
            pool.memset(EPS[:, 1:2], LN_EPS).then_inc(consts, 1)
            seq.wait()
            pool.affine_select(out=ident[:, :], in_=ident[:, :], compare_op=ALU.not_equal, fill=1.0, base=0,
                               pattern=[[-1, P]], channel_multiplier=1).then_inc(consts, 1)
            seq.inc(pool.affine_select(out=MJ8[:, :, :], in_=MJ8[:, :, :], compare_op=ALU.is_ge, fill=0.0, base=0,
                                       pattern=[[-64, 2], [-16, 4]], channel_multiplier=1))
            seq.wait()
            seq.inc(pool.affine_select(out=MJ8[:, :, :], in_=MJ8[:, :, :], compare_op=ALU.is_ge, fill=0.0, base=15,
                                       pattern=[[64, 2], [16, 4]], channel_multiplier=-1))
            seq.wait()
            pool.tensor_tensor(MJ[:, :], MJ8[:, 0, :], MJ8[:, 1, :], ALU.add).then_inc(consts, 1)
            for c in range(PPAD):
                pool.memset(INVC[:, c:c + 1], 1.0 / (c + 1)).then_inc(consts, 1)

            def tt(o, x, y, op):
                seq.wait()
                return seq.inc(pool.tensor_tensor(o, x, y, op))

            def ts(o, x, s1, s2, op0, op1):
                seq.wait()
                return seq.inc(pool.tensor_scalar(o, x, s1, s2, op0, op1))

            for g in range(2):
                for j in range(T4):
                    pool.dma_start(DCOL[64 * g + 16 * j:64 * g + 16 * j + 16, :],
                                   a["s5_d_2"][0].rearrange("(r g q) -> g q r", g=2, q=S5_GROUP)[g]).then_inc(d_in, 16)
            LRE, LIM, DTL, DT, RE, IM, K, RED, HALF, EX, SN, SH, LR_, LI_, NR, T1, T2, DEN, REC, F0 = range(20)
            l = [LS[:, i, :] for i in range(20)]
            F1 = K
            pool.wait_ge(lam_in, 64)
            pool.wait_ge(lam_exp, 1)
            tt(l[RE], l[LRE], l[DT], ALU.mult)
            tt(l[IM], l[LIM], l[DT], ALU.mult)
            tt(l[T1], l[LRE], l[LRE], ALU.mult)
            tt(l[T2], l[LIM], l[LIM], ALU.mult)
            tt(l[DEN], l[T1], l[T2], ALU.add)
            ts(l[K], l[IM], 1.0 / TWO_PI, ROUND, ALU.mult, ALU.add)
            ts(l[K], l[K], ROUND, -1.0, ALU.subtract, ALU.mult)
            seq.wait()
            pool.tensor_scalar(l[T1], l[K], PI_A, None, ALU.mult).then_inc(lam_den, 1)
            pool.wait_ge(lam_den, 1)
            tt(l[RED], l[IM], l[T1], ALU.add)
            ts(l[T2], l[K], PI_B, None, ALU.mult, ALU.bypass)
            tt(l[RED], l[RED], l[T2], ALU.add)
            ts(l[T1], l[K], PI_C, None, ALU.mult, ALU.bypass)
            tt(l[RED], l[RED], l[T1], ALU.add)
            ts(l[RED], l[RED], 3.1415925, -3.1415925, ALU.min, ALU.max)
            seq.wait()
            pool.tensor_scalar(l[HALF], l[RED], 0.5, None, ALU.mult).then_inc(lam_ang, 1)
            pool.wait_ge(lam_sin, 3)
            tt(l[T1], l[SH], l[SH], ALU.mult)
            tt(l[LI_], l[EX], l[SN], ALU.mult)
            ts(l[T1], l[T1], -2.0, 1.0, ALU.mult, ALU.add)
            tt(l[LR_], l[EX], l[T1], ALU.mult)
            ts(l[NR], l[LR_], -1.0, None, ALU.add, ALU.bypass)
            tt(l[T1], l[NR], l[LRE], ALU.mult)
            tt(l[T2], l[LI_], l[LIM], ALU.mult)
            tt(l[F0], l[T1], l[T2], ALU.add)
            tt(l[T1], l[LI_], l[LRE], ALU.mult)
            tt(l[T2], l[NR], l[LIM], ALU.mult)
            tt(l[F1], l[T1], l[T2], ALU.subtract)
            pool.wait_ge(lam_rec, 1)
            tt(l[F0], l[F0], l[REC], ALU.mult)
            tt(l[F1], l[F1], l[REC], ALU.mult)

            def wide(row):
                return row.unsqueeze(2).to_broadcast([P, PAIRS, S5_GROUP])

            pool.wait_ge(b_in, 32)
            pool.wait_ge(xn0, 4)
            P0, P1 = PT[:, 0, :, :], PT[:, 1, :, :]

            def cmul(ore, oim, xre, xim, yre, yim, signs=(ALU.subtract, ALU.add)):
                tt(P0, xre, yre, ALU.mult)
                tt(P1, xim, yim, ALU.mult)
                tt(ore, P0, P1, signs[0])
                tt(P0, xim, yre, ALU.mult)
                tt(P1, xre, yim, ALU.mult)
                tt(oim, P0, P1, signs[1])

            cmul(WST[:, 0, :, 3, :], WST[:, 1, :, 3, :], BRAW[:, 0, :, :], BRAW[:, 1, :, :], wide(l[F0]), wide(l[F1]))
            for j in (2, 1, 0):
                cmul(WST[:, 0, :, j, :], WST[:, 1, :, j, :], WST[:, 0, :, j + 1, :], WST[:, 1, :, j + 1, :],
                     wide(l[LR_]), wide(l[LI_]))
            seq.wait()
            pool.memset(MJ8[:, 0, 0:1], 0.0).then_inc(pool_w, 1)
            tt(l[T1], l[LR_], l[LR_], ALU.mult)
            tt(l[T2], l[LI_], l[LI_], ALU.mult)
            tt(l[NR], l[LR_], l[LI_], ALU.mult)
            tt(l[T1], l[T1], l[T2], ALU.subtract)
            ts(l[NR], l[NR], 2.0, None, ALU.mult, ALU.bypass)
            tt(l[T2], l[T1], l[T1], ALU.mult)
            tt(l[DEN], l[NR], l[NR], ALU.mult)
            tt(l[IM], l[T1], l[NR], ALU.mult)
            tt(LAM[:, 0, :], l[T2], l[DEN], ALU.subtract)
            ts(LAM[:, 1, :], l[IM], 2.0, None, ALU.mult, ALU.bypass)
            ts(LAM[:, 2, :], l[IM], -2.0, None, ALU.mult, ALU.bypass)
            pool.wait_ge(banks_act, act_after("c_t"))
            for k in range(4):
                cmul(GRE[:, :, k + 1, :], GNI[:, :, k + 1, :], GRE[:, :, k, :], GNI[:, :, k, :],
                     wide(l[LR_]), wide(l[LI_]), signs=(ALU.add, ALU.subtract))
            seq.wait()
            pool.memset(MJ8[:, 0, 1:2], 0.0).then_inc(pool_g, 1)
            pool.wait_ge(d_in, 128)
            pool.wait_ge(consts, 3)

            def dcol():
                return DCOL[:, :].unsqueeze(2).to_broadcast([P, PAIRS, 64])

            def eye(half):
                return ident[:, 64 * half:64 * half + 64].unsqueeze(1).to_broadcast([P, PAIRS, 64])

            tt(TM[:, :, :], dcol(), eye(0), ALU.mult)
            tt(DT2[:, :, :], dcol(), eye(1), ALU.mult)
            seq.wait()
            pool.tensor_tensor(TM[:, :, :], TM[:, :, :], DT2[:, :, :], ALU.add).then_inc(pool_t, 1)
            pool.wait_ge(sg_in, 16)
            pool.memset(SGW[0:CHUNK, :, CHUNK:P], 0.0).then_inc(sgw_masked, 1)
            pool.wait_ge(side_done, side_after("w_t.3"))
            for ri in range(2):
                pool.tensor_copy(WST[:, ri, :, 0:T4 - 1, :],
                                 WST[:, ri, :, T4 - 1:T4, :].to_broadcast([P, PAIRS, T4 - 1, S5_GROUP])).then_inc(pool_rep, 1)
            pool.wait_ge(side_done, side_after("sgu.1"))
            pool.memset(CH[:, :, 0:PPAD], 0.0).then_inc(pads, 1)
            pool.wait_ge(s5_out, 16 * 10)
            pool.memset(WIN[:, :, 0:PPAD], 0.0).then_inc(pads, 1)
            pool.wait_ge(tmp_free, 16)
            pool.memset(CP[:, :, 0:CPAD], 0.0).then_inc(cpads, 1)
            pool.wait_ge(weights_used, used_after("w_c.1"))
            pool.memset(S[:, :, :, 0:1], 0.0).then_inc(states, 1)
            pool.wait_ge(m_acc, 16)
            pool.wait_ge(x1_done, 4)
            for i in range(2):
                seq.wait()
                seq.inc(pool.tensor_copy(TAB[:, i, :, 0:1], LAM[:, i, :].unsqueeze(2)))
            n = 1
            while n < SEG_CH:
                by = [TAB[:, i, :, n - 1:n].to_broadcast([P, PAIRS, n]) for i in range(2)]
                x = [TAB[:, i, :, 0:n] for i in range(2)]
                q0, q1 = Q0[:, 0, :, 0:n], Q0[:, 1, :, 0:n]
                for i, (y0, y1, op) in enumerate(((by[0], by[1], ALU.subtract), (by[1], by[0], ALU.add))):
                    tt(q0, x[0], y0, ALU.mult)
                    tt(q1, x[1], y1, ALU.mult)
                    tt(TAB[:, i, :, n:2 * n], q0, q1, op)
                n *= 2
            for i in range(2):
                ts(LAM64[:, i, :].unsqueeze(2), TAB[:, i, :, SEG_CH - 1:SEG_CH], 1.0, None, ALU.mult, ALU.bypass)
            ts(LAM64[:, 2, :].unsqueeze(2), TAB[:, 1, :, SEG_CH - 1:SEG_CH], -1.0, None, ALU.mult, ALU.bypass)
            seq.wait()
            pool.wait_ge(banks_act, act_after("s5_z.3"))
            SV = S[:, :, :, :].rearrange("p r g (s j) -> p r g s j", j=SEG_CH)
            per_step = 4
            first = seq.n

            def chunk_of(v, j):
                return v[:, :, :, :, bass.ds(j, 1)].rearrange("p r g s j -> p r g (s j)")

            with pool.Fori(0, SEG_CH - 1) as j:
                seq.base, seq.n = j * per_step, first
                now, nxt = chunk_of(SV, j), chunk_of(SV, j + 1)
                nre, nim = chunk_of(SV[:, 0:1], j + 1), chunk_of(SV[:, 1:2], j + 1)
                pool.wait_ge(states, j + 1)
                seq.inc(pool.tensor_tensor(SEG1[:, :, :, :], LAM[:, 0:1, :].unsqueeze(3).to_broadcast([P, 2, PAIRS, SEG]), now, ALU.mult))
                seq.inc(pool.tensor_tensor(SEG2[:, :, :, :], LAM[:, 1:3, :].unsqueeze(3).to_broadcast([P, 2, PAIRS, SEG]), now, ALU.mult))
                seq.wait()
                seq.inc(pool.tensor_tensor(nxt, nxt, SEG1[:, :, :, :], ALU.add))
                seq.wait()
                seq.inc(pool.tensor_tensor(nim, nim, SEG2[:, 0:1, :, :], ALU.add))
                pool.tensor_tensor(nre, nre, SEG2[:, 1:2, :, :], ALU.add).then_inc(states, 1)
                assert seq.n - first == per_step
            seq.base, seq.n = 0, first + per_step * (SEG_CH - 1)
            pool.wait_ge(states, SEG_CH)
            for g in range(1, SEG):
                now, nxt = [S[:, :, :, SEG_CH * k - 1:SEG_CH * k] for k in (g, g + 1)]
                tt(ST1[:, :, :].unsqueeze(3), LAM64[:, 0:1, :].to_broadcast([P, 2, PAIRS]).unsqueeze(3), now, ALU.mult)
                tt(ST2[:, :, :].unsqueeze(3), LAM64[:, 1:3, :].unsqueeze(3), now, ALU.mult)
                tt(nxt, nxt, ST1[:, :, :].unsqueeze(3), ALU.add)
                tt(nxt[:, 1:2], nxt[:, 1:2], ST2[:, 0:1, :].unsqueeze(3), ALU.add)
                seq.wait()
                o = pool.tensor_tensor(nxt[:, 0:1], nxt[:, 0:1], ST2[:, 1:2, :].unsqueeze(3), ALU.add)
                if g < SEG - 1:
                    seq.inc(o)
                else:
                    o.then_inc(carried, 1)
            pool.wait_ge(carried, 1)
            for b in range(PAIRS // FB):
                for q in range(2):
                    fix, into, by, end, op = correction(b, 0, q, 0)
                    tt(fix, by, end, ALU.mult)
                    seq.wait()
                    o = pool.tensor_tensor(into, into, fix, op)
                    if q == 0 or b < PAIRS // FB - 1:
                        seq.inc(o)
                    else:
                        o.then_inc(states_fixed, 1)
            pool.wait_ge(x2_done, 4)
            seq.inc(pool.memset(CMASK[:, :], 1.0))
            seq.inc(pool.memset(ATS[:, :, :], 0.0))
            seq.inc(pool.memset(SMASK[:, :], 1.0))
            seq.inc(pool.memset(LR[0:32, :], 1.0))
            seq.wait()
            seq.inc(pool.affine_select(out=CMASK[:, :], in_=CMASK[:, :], compare_op=ALU.is_ge, fill=0.0, base=0,
                                       pattern=[[1, P]], channel_multiplier=-1))
            seq.inc(pool.memset(SMASK[:, :].rearrange("p (c t) -> p c t", t=CHUNK)[:, :, 0:1], 0.0))
            seq.wait()
            pool.memset(CMASK[0:CHUNK, CHUNK:P], 0.0).then_inc(gla_consts, 1)
            pool.wait_ge(xn2, 4)
            pool.memset(YO2[:, :, :], 0.0).then_inc(y2_add, 8)

        @block.scalar
        def _(act):
            seq = Order(act, act_seq)
            state = {"unit": 0, "hi": 0, "y": 0}

            lam = LS
            act.dma_start(lam[:, 0, :], a["s5_lambda_re_2"][0].rearrange("(r g) n -> (g n) r", g=2)).then_inc(lam_in, 16)
            act.dma_start(lam[:, 1, :], a["s5_lambda_im_2"][0].rearrange("(r g) n -> (g n) r", g=2)).then_inc(lam_in, 16)
            for g in range(2):
                act.dma_start(lam[64 * g:64 * g + 64, 2, :],
                              a["s5_log_dt_2"].rearrange("o (r g) -> g o r", g=2)[g].broadcast_to([64, PAIRS])).then_inc(lam_in, 16)
            def split(units=1):
                for _u in range(units):
                    if state["unit"] >= len(UNITS):
                        return
                    name = UNITS[state["unit"]]
                    for n in range(chunks_before(name), used_after(name)):
                        act.wait_ge(w_loaded[n % RING], 16 * (n // RING + 1))
                        if n >= RING:
                            act.wait_ge(weights_used, n - RING + 1)
                        act.activation(WH[:, n % RING, :, :], WR[:, n % RING, :, :], ACT.Copy).then_inc(w_hi, 1)
                    state["unit"] += 1

            def rms(src, n, junk, waits, sq, std):
                for t in range(n):
                    waits(t)
                    act.activation(junk(t), src(t), ACT.Square, accum_out=STAT[:, 0, t:t + 1]).then_inc(sq, 1)
                act.wait_ge(sq, n)
                act.activation(STAT[:, 1, 0:n], STAT[:, 0, 0:n], ACT.Sqrt, scale=1.0 / D, bias=EPS[:, 0:1]).then_inc(std, 1)

            def turned(job, kt0, vec, before=None):
                for m in range(4):
                    act.wait_ge(side_done, side_after(job, m + 1))
                    act.activation(HH[:, kt0 + m, :], bank(job, m), ACT.Copy, scale=col(vec, kt0 + m)).then_inc(h_hi, 1)

            def evac(job, outs, func, waits=None, inc=banks_act, **kw):
                act.wait_ge(weights_used if job in UNITS else side_done,
                            used_after(job) if job in UNITS else side_after(job))
                for m, o in enumerate(outs):
                    if waits:
                        waits(m)
                    extra = {k: v(m) for k, v in kw.items()}
                    act.activation(o, bank(job, m), func, **extra).then_inc(inc, 1)

            def via_tmp(job, func, to=TMP, **kw):
                act.wait_ge(weights_used, used_after(job))
                for m in range(4):
                    if state["hi"] >= 2:
                        act.wait_ge(tmp_free, state["hi"] - 1)
                    extra = {k: v(m) for k, v in kw.items()}
                    act.activation(to[:, state["hi"] % 2, :], bank(job, m), func, **extra).then_inc(banks_act, 1)
                    state["hi"] += 1

            def y_halves(ready, count, src, kts):
                for kt in kts:
                    act.wait_ge(ready, count(kt))
                    act.activation(YH[:, kt, :], src(kt), ACT.Copy).then_inc(y_hi, 1)

            act.wait_ge(consts, 2)
            rms(lambda t: X[:, t, :], TT, lambda t: XN0[:, t, :], lambda t: act.wait_ge(x_in[t], 16), sq0, std0)
            act.wait_ge(side_done, side_after("params"))
            for i, n in enumerate((116, 128, 120)):
                act.activation(PRM[:, 128 * i:128 * i + n], bank("params", i)[:, 0:n], ACT.Copy).then_inc(banks_act, 1)
            act.wait_ge(banks_act, act_after("params"))
            turned("h_t.0", 0, "norm_g")
            turned("h_t.1", 4, "norm_g")
            split()
            for i, name in enumerate(("sgu_ln_g", "sgu_ln_b")):
                act.dma_start(LNROWS[:, i, :], a[name].broadcast_to([P, D])).then_inc(ln_in, 16)
            act.dma_start(SGW[:, :, :], a["sgu_w"][0].rearrange("g i j -> i g j")).then_inc(sg_in, 16)
            act.dma_start(SGB[:, :, :].rearrange("p g i -> p (g i)"),
                          a["sgu_b"].rearrange("o g i -> o (g i)").broadcast_to([P, D])).then_inc(bs_in, 16)
            act.wait_ge(lam_in, 64)
            act.activation(LS[:, 3, :], LS[:, 2, :], ACT.Exp).then_inc(lam_exp, 1)
            act.wait_ge(lam_ang, 1)
            act.activation(LS[:, 9, :], LS[:, 4, :], ACT.Exp).then_inc(lam_sin, 1)
            act.activation(LS[:, 10, :], LS[:, 7, :], ACT.Sin).then_inc(lam_sin, 1)
            act.activation(LS[:, 11, :], LS[:, 8, :], ACT.Sin).then_inc(lam_sin, 1)

            def v_free(m):
                act.wait_ge(side_done, side_after("h_t.1"))

            split()
            evac("a_v.0", [V[:, m, 0:NC] for m in range(4)], ACT.Gelu_apprx_tanh, waits=v_free)
            split()
            evac("a_v.1", [V[:, m, NC:D] for m in range(4)], ACT.Gelu_apprx_tanh)
            act.wait_ge(side_done, side_after("c_t"))
            act.activation(GRE[:, :, 0, :], bank("c_t", 0).rearrange("p (r q) -> p r q", q=S5_GROUP), ACT.Copy).then_inc(banks_act, 1)
            act.activation(GNI[:, :, 0, :], bank("c_t", 1).rearrange("p (r q) -> p r q", q=S5_GROUP), ACT.Copy,
                           scale=-1.0).then_inc(banks_act, 1)
            split()
            evac("a_u.0", [U[:, m, :] for m in range(4)], ACT.Gelu_apprx_tanh)
            split()
            evac("a_u.1", [U[:, 4 + m, :] for m in range(4)], ACT.Gelu_apprx_tanh)
            act.wait_ge(v_std, 4)
            act.activation(STAT[:, 2, :], BNA[:, :, 1], ACT.Sqrt, bias=EPS[:, 1:2]).then_inc(v_std, 1)
            split()
            via_tmp("a_z.0", ACT.Silu)
            split()
            via_tmp("a_z.1", ACT.Silu)
            act.wait_ge(pool_t, 1)
            for i in range(4):
                act.wait_ge(side_done, side_after(f"w_t.{i}"))
                for ri in range(2):
                    act.activation(WTS[0:64, ri, 8 * i:8 * i + 8, :],
                                   bank(f"w_t.{i}", 2 * ri)[0:64, :].rearrange("p (r n) -> p r n", r=8),
                                   ACT.Copy).then_inc(banks_act, 1)
            for m in range(2):
                if not m:
                    act.wait_ge(side_done, side_after("sgu_t"))
                act.activation(SGWT[:, 4 * m:4 * m + 4, :], bank("sgu_t", m).rearrange("p (g i) -> p g i", g=4),
                               ACT.Copy).then_inc(banks_act, 1)
            split()
            act.wait_ge(v_done, 4)
            evac("g0.0", [G[:, m, :] for m in range(4)], ACT.Sigmoid)
            split()
            evac("g0.1", [G[:, 4 + m, :] for m in range(4)], ACT.Sigmoid)
            act.wait_ge(s5_out, 16 * 10)
            y_halves(ya_ready, lambda kt: kt + 1, lambda kt: U[:, kt, :], range(4))
            split()
            y_halves(ya_ready, lambda kt: kt + 1, lambda kt: U[:, kt, :], range(4, 8))
            act.wait_ge(pads, 1)
            evac("b_p.0", [CH[:, m, PPAD:] for m in range(4)], ACT.Copy)
            split()
            evac("b_p.1", [CH[:, 4 + m, PPAD:] for m in range(4)], ACT.Copy)
            split()
            split()
            split()
            act.wait_ge(d_ready, 4)
            evac("b_z.0", [CH[:, m, PPAD:] for m in range(4)], ACT.Silu)
            split()
            evac("b_z.1", [CH[:, 4 + m, PPAD:] for m in range(4)], ACT.Silu)
            act.wait_ge(weights_used, used_after("w_a.1"))
            y_halves(yb_ready, lambda kt: kt + 1, lambda kt: CH[:, kt, PPAD:], range(8))
            split()
            act.wait_ge(banks_dve, dve_after("w_a.1"))
            evac("g1.0", [G[:, m, :] for m in range(4)], ACT.Sigmoid)
            split()
            evac("g1.1", [G[:, 4 + m, :] for m in range(4)], ACT.Sigmoid)
            split()
            act.wait_ge(y_lo, 16)
            evac("c_h.0", [CH[:, m, PPAD:] for m in range(4)], ACT.Copy)
            split()
            evac("c_h.1", [CH[:, 4 + m, PPAD:] for m in range(4)], ACT.Copy)
            split()
            split()
            split()
            split()
            split()
            act.wait_ge(banks_dve, dve_after("w_b.1"))
            evac("g2.0", [G[:, m, :] for m in range(4)], ACT.Sigmoid)
            split()
            evac("g2.1", [G[:, 4 + m, :] for m in range(4)], ACT.Sigmoid)
            split()
            split()
            split()
            act.wait_ge(weights_used, used_after("w_b.1"))
            act.wait_ge(banks_dve, dve_after("c_b.1"))
            via_tmp("c_z.0", ACT.Silu)
            y_halves(tmp_free, lambda kt: 8 + kt + 1, lambda kt: U[:, kt, :], range(4))
            split()
            via_tmp("c_z.1", ACT.Silu)
            y_halves(tmp_free, lambda kt: 8 + kt + 1, lambda kt: U[:, kt, :], range(4, 8))
            split()
            split()
            act.wait_ge(weights_used, used_after("c_z.1"))
            for kt in range(KT):
                act.wait_ge(m_acc, 8 + kt + 1)
                act.activation(HH[:, kt, :], M[:, kt, :], ACT.Copy).then_inc(h_hi, 1)
            split()
            split()

            act.wait_ge(h_lo, 16)
            rms(lambda t: X[:, t, :], TT, lambda t: XN1[:, t, :], 
                lambda t: act.wait_ge(banks_dve, dve_after("w_out.1", t + 1)), sq1, std1)
            rms(lambda t: X[:, t, :], TT, lambda t: XN1[:, t, :], lambda t: act.wait_ge(x1_done, t + 1), sq2, std2)
            turned("u_t.0", 0, "norm_pre0")
            turned("u_t.1", 4, "norm_pre0")

            split()
            act.wait_ge(cpads, 1)
            evac("b_val.0", [CP[:, m, CPAD:] for m in range(4)], ACT.Copy)
            split()
            via_tmp("b_gate.0", ACT.Sigmoid, GATEV)
            for u in range(2):
                split()
                act.wait_ge(weights_used, used_after(f"a_in.{u}"))
                if u == 0:
                    act.wait_ge(tmp_free, 20)
                for j in range(T4):
                    act.activation(AS[:, u, :, j, :], bank(f"a_in.{u}", j).rearrange("p (g q) -> p g q", q=S5_GROUP),
                                   ACT.Copy).then_inc(banks_act, 1)
            for u in range(2):
                evac(f"s5_t.{u}", [UT[:, 16 * u + 4 * m:16 * u + 4 * m + 4, :].rearrange("p r c -> p (r c)")
                                   for m in range(4)], ACT.Copy)
            for i in range(4):
                act.wait_ge(side_done, side_after(f"s5_z.{i}"))
                for m in range(4):
                    r0 = 8 * i + 4 * (m % 2)
                    act.activation(S[:, m // 2, r0:r0 + 4, 1:NCH],
                                   bank(f"s5_z.{i}", m).rearrange("p (r c) -> p r c", c=NCH)[:, :, 0:NCH - 1],
                                   ACT.Copy).then_inc(banks_act, 1)
            split()
            evac("b_val.1", [CP[:, 4 + m, CPAD:] for m in range(4)], ACT.Copy)
            split()
            via_tmp("b_gate.1", ACT.Sigmoid, GATEV)
            split()
            act.wait_ge(tmp_free, 24)
            evac("a_z2.0", [AZ[:, m, :] for m in range(4)], ACT.Silu)
            split()
            evac("a_z2.1", [AZ[:, 4 + m, :] for m in range(4)], ACT.Silu)
            split()
            act.wait_ge(states_fixed, 2)
            evac("b_z2.0", [BZ[:, m, :] for m in range(4)], ACT.Silu)
            split()
            act.wait_ge(side_done, side_after("s5_y.0"))
            evac("b_z2.1", [BZ[:, 4 + m, :] for m in range(4)], ACT.Silu)
            for i in range(2):
                act.wait_ge(side_done, side_after(f"s5_y.{i}"))
                for m in range(4):
                    kt = 4 * i + m
                    dst = YT[:, :, kt * P:(kt + 1) * P].rearrange("c t (x q) -> c x t q", q=S5_GROUP)
                    act.activation(dst, bank(f"s5_y.{i}", m).rearrange("p (x t q) -> p x t q", x=8, t=T4),
                                   ACT.Gelu_apprx_tanh).then_inc(banks_act, 1)
            for i in range(2):
                for m in range(4):
                    act.wait_ge(side_done, side_after(f"y_t.{i}", m + 1))
                    act.activation(YH[:, 4 * i + m, :].rearrange("p (c t) -> p t c", t=T4),
                                   bank(f"y_t.{i}", m).rearrange("p (t c) -> p t c", t=T4), ACT.Copy).then_inc(y_hi, 1)

            def ya_halves(kts):
                for kt in kts:
                    act.wait_ge(ya_final, kt + 1)
                    act.activation(HH[:, kt, :], YA[:, kt, :], ACT.Copy).then_inc(h_hi, 1)

            split()
            via_tmp("glu.0", ACT.Sigmoid, GLUV, bias=lambda m: col("b_glu", m))
            split()
            ya_halves(range(4))
            via_tmp("glu.1", ACT.Sigmoid, GLUV, bias=lambda m: col("b_glu", 4 + m))
            ya_halves(range(4, 8))
            for kt in range(KT):
                act.wait_ge(z_cent, kt + 1)
                act.activation(SQ[:, kt, :], CP[:, kt, CPAD:], ACT.Square).then_inc(z_sq, 1)
            split()
            act.wait_ge(h_lo, 32)
            evac("ev_a.0", [YO[:, m, 0:NC] for m in range(4)], ACT.Copy)
            act.wait_ge(sq_used, KT)
            act.activation(RS[:, :], bank("var", 0), ACT.Sqrt, bias=EPS[:, 0:1]).then_inc(banks_act, 1)
            for kt in range(KT):
                act.wait_ge(z_norm, kt + 1)
                act.activation(CP[:, kt, CPAD:], CP[:, kt, CPAD:], ACT.Silu, scale=col("ln_g2", kt),
                               bias=col("ln_b2", kt)).then_inc(z_act, 1)
                act.wait_ge(z_act, kt + 1)
                act.activation(YH[:, kt, :], CP[:, kt, CPAD:], ACT.Copy).then_inc(y_hi, 1)
            split()
            evac("ev_a.1", [YO[:, m, NC:D] for m in range(4)], ACT.Copy)
            split()
            for u in range(2):
                if u:
                    split()
                for m in range(4):
                    kt = 4 * u + m
                    act.wait_ge(banks_dve, dve_after(f"pw.{u}", m + 1))
                    act.activation(HH[:, kt, :], BZ[:, kt, :], ACT.Copy).then_inc(h_hi, 1)
            split()
            act.wait_ge(h_lo, 40)
            rms(lambda t: YO[:, t, :], TT, lambda t: XN2[:, t, :],
                lambda t: act.wait_ge(banks_dve, dve_after("ev_b.1", t + 1)), sq3, std3)
            rms(lambda t: X1[:, t, :], TT, lambda t: XN2[:, t, :], lambda t: act.wait_ge(x2_done, t + 1), sq4, std4)
            turned("u2_t.0", 0, "norm_pre1")
            turned("u2_t.1", 4, "norm_pre1")

            act.wait_ge(h_lo, 32)
            act.dma_start(LWR[:, :, :], a["od_w_in_2"][0][:, 6 * D:6 * D + LOWRANK].rearrange("(k p) n -> p k n", p=P)).then_inc(lw_in, 16)
            act.wait_ge(lw_in, 16)
            act.wait_ge(lw_zero, 2)
            act.activation(LWH[:, :, 0:LOWRANK], LWR[:, :, :], ACT.Copy).then_inc(lw_hi, 1)
            act.wait_ge(gla_consts, 1)
            act.wait_ge(lr_out, 1)
            act.activation(LR[0:LOWRANK, :], bank("lr", 0)[0:LOWRANK, :], ACT.Copy).then_inc(banks_act, 1)

            A, B = [PS[:, m, :] for m in range(4)], [PS[:, 4 + m, :] for m in range(4)]

            def hsplit(n, j0, count, value):
                for j in range(j0, j0 + count):
                    act.wait_ge(w_loaded[j % RING], value)
                    act.wait_ge(weights_used, n + (j - RING + 1))
                    act.activation(WH[:, j % RING, :, :], WR[:, j % RING, :, :], ACT.Copy).then_inc(w_hi, 1)

            def qk_out(n, banks):
                act.wait_ge(weights_used, n)
                for m in range(4):
                    act.activation(QK[:, m, :], banks[m], ACT.Copy).then_inc(qk_copied, 1)

            hsplit(N_STATIC, 0, 4, 16 * (N_STATIC // RING) + 32)
            qk_out(N_STATIC + 4, A)
            junk = [KE[:, 0, :], KE[:, 1, :], QD[:, 0, :], QD[:, 1, :]]

            def head(h, last):
                n = head_base(h)
                seq.base, seq.n = h * HSEQ_ACT, 0
                hsplit(n, V_AT, 4, loaded(h, V_AT))
                act.wait_ge(g_out, h + 1)
                for m in range(2):
                    seq.inc(act.activation(ET[:, m, :], B[m], ACT.Abs))
                for m in range(2):
                    seq.wait(m + 1)
                    seq.inc(act.activation(ET[:, m, :], ET[:, m, :], ACT.Exp, scale=-1.0))
                for m in range(2):
                    seq.wait(m + 3)
                    act.activation(ET[:, m, :], ET[:, m, :], ACT.Ln, bias=1.0).then_inc(e_abs, 1)
                act.wait_ge(g_scan, h * 2 + 1)
                act.activation(ET[:, :, :], BC[:, :, :], ACT.Exp, scale=1.0 / GLA_TAU).then_inc(e_q, 1)
                act.activation(DEC[:, :, :], BC[:, :, :].rearrange("p k (c t) -> p k c t", t=CHUNK)[:, :, :, CHUNK - 1],
                               ACT.Exp, scale=1.0 / GLA_TAU).then_inc(dec_in, 1)
                act.wait_ge(qd_done, h + 1)
                act.activation(ET[:, :, :], BC[:, :, :], ACT.Exp, scale=-1.0 / GLA_TAU).then_inc(e_ke, 1)
                act.wait_ge(g_scan, h * 2 + 2)
                act.wait_ge(ke_done, h + 1)
                act.activation(ET[:, :, :], KX[:, :, :], ACT.Exp, scale=1.0 / GLA_TAU).then_inc(e_d, 1)
                hsplit(n, R_AT, 4, loaded(h, R_AT))
                act.wait_ge(weights_used, n + 4)
                for m in range(4):
                    act.activation(V2[:, m, :], A[m], ACT.Copy).then_inc(v_copied, 1)
                hsplit(n, QK_AT, 4, loaded(h, QK_AT, last))
                act.wait_ge(weights_used, n + 8)
                for m in range(4):
                    act.activation(RR[:, m, :], B[m], ACT.Silu).then_inc(r_copied, 1)
                act.wait_ge(kt_out, h + 1)
                for m in range(2):
                    act.activation(KTK[:, 2 * m:2 * m + 2, :, :].rearrange("p t k n -> p (t k n)"),
                                   A[m], ACT.Copy).then_inc(kt_copied, 1)
                for m in range(4):
                    act.wait_ge(o_out, h * 4 + (m + 1))
                    act.activation(junk[m], A[m], ACT.Square, accum_out=STAT[:, 0, m:m + 1]).then_inc(o_sq, 1)
                act.wait_ge(o_sq, h * 4 + 4)
                act.activation(STAT[:, 1, :], STAT[:, 0, :], ACT.Sqrt, scale=1.0 / HV, bias=EPS[:, 0:1]).then_inc(o_std, 1)
                if not last:
                    hsplit(n, out_at(last), 2, loaded(h, out_at(last)))
                for m in range(4):
                    act.wait_ge(o_f, h * 4 + (m + 1))
                    act.activation(OH[:, m, :], RR[:, m, :], ACT.Copy).then_inc(o_hi, 1)
                if not last:
                    qk_out(n + 12, B)
                    hsplit(n, out_at(last) + 2, 2, loaded(h, out_at(last)))

            with act.Fori(0, HEADS - 1) as h:
                head(h, False)
            head(HEADS - 1, True)

            act.wait_ge(y2_add, 8 * (HEADS + 1))
            rms(lambda t: YO2[:, t, :], TT, lambda t: XN2[:, t, :], lambda t: None, sq5, std5)

        @block.vector
        def _(dve):
            seq = Order(dve, dve_seq)
            state = {"unit": 0, "via": 0}

            def split(units=1):
                for _u in range(units):
                    if state["unit"] >= len(UNITS):
                        return
                    name = UNITS[state["unit"]]
                    for n in range(chunks_before(name), used_after(name)):
                        s = n % RING
                        dve.wait_ge(w_hi, n + 1)
                        dve.tensor_tensor(WL[:, s, :, :], WR[:, s, :, :], WH[:, s, :, :].bitcast(F32),
                                          ALU.subtract).then_inc(w_lo, 1)
                    state["unit"] += 1

            def done(job):
                dve.wait_ge(weights_used if job in UNITS else side_done,
                            used_after(job) if job in UNITS else side_after(job))

            def rstd(k):
                seq.inc(dve.reciprocal(STAT[:, 3, :], STAT[:, k, :]))
                seq.wait()

            def turned(job, kt0, vec, version):
                for m in range(4):
                    kt = kt0 + m
                    dve.wait_ge(h_hi, 8 * version + kt + 1)
                    dve.scalar_tensor_tensor(HL[:, kt, :], bank(job, m), col(vec, kt), HH[:, kt, :].bitcast(F32),
                                             ALU.mult, ALU.subtract).then_inc(h_lo, 1)

            def y_low(version, src, kts):
                for kt in kts:
                    dve.wait_ge(y_hi, 8 * version + kt + 1)
                    dve.tensor_tensor(YL[:, kt, :], src(kt), YH[:, kt, :].bitcast(F32), ALU.subtract).then_inc(y_lo, 1)

            def h_low(version, src, kts):
                for kt in kts:
                    dve.wait_ge(h_hi, 8 * version + kt + 1)
                    dve.tensor_tensor(HL[:, kt, :], src(kt), HH[:, kt, :].bitcast(F32), ALU.subtract).then_inc(h_lo, 1)

            def times_tmp(dsts, src=TMP):
                for i, (job, m, d) in enumerate(dsts):
                    dve.wait_ge(banks_act, act_after(job, m + 1))
                    dve.tensor_tensor(d, d, src[:, state["via"] % 2, :], ALU.mult).then_inc(tmp_free, 1)
                    state["via"] += 1

            dve.wait_ge(std0, 1)
            rstd(1)
            for t in range(TT):
                dve.tensor_scalar(XN0[:, t, :], X[:, t, :], STAT[:, 3, t:t + 1], None, ALU.mult).then_inc(xn0, 1)
            dve.wait_ge(banks_act, act_after("params"))
            turned("h_t.0", 0, "norm_g", 0)
            turned("h_t.1", 4, "norm_g", 0)
            split()
            dve.wait_ge(lam_den, 1)
            dve.reciprocal(LS[:, 18, :], LS[:, 17, :]).then_inc(lam_rec, 1)
            split()
            split()
            split()
            for t in range(TT):
                dve.wait_ge(banks_act, act_after("a_v.1", t + 1))
                if t == 0:
                    dve.wait_ge(zeros_out, 16 * 10)
                for u in range(2):
                    seq.inc(dve.bn_stats(BNS[:, t, u, :], V[:, t, u * NC:(u + 1) * NC]))
                seq.wait()
                dve.bn_aggr(BNA[:, t, :], BNS[:, t, :, :]).then_inc(v_std, 1)
            split()
            dve.wait_ge(v_std, 5)
            rstd(2)
            dve.wait_ge(ln_in, 32)
            n = [seq.inc(dve.tensor_scalar(V[:, t, :], V[:, t, :], BNA[:, t, 0:1], STAT[:, 3, t:t + 1],
                                           ALU.subtract, ALU.mult)) for t in range(TT)]
            for t in range(TT):
                seq.wait(n[t])
                n[t] = seq.inc(dve.tensor_tensor(V[:, t, :], V[:, t, :], LNROWS[:, 0, :], ALU.mult))
            split()
            for t in range(TT):
                seq.wait(n[t])
                dve.tensor_tensor(V[:, t, :], V[:, t, :], LNROWS[:, 1, :], ALU.add).then_inc(v_done, 1)
            times_tmp([("a_z.0", m, U[:, m, :]) for m in range(4)])
            split()
            times_tmp([("a_z.1", m, U[:, 4 + m, :]) for m in range(4)])
            dve.wait_ge(pool_t, 1)
            dve.wait_ge(consts, 4)
            for i in range(4):
                done(f"w_t.{i}")
                for ri in range(2):
                    dve.tensor_copy(WTS[64:P, ri, 8 * i:8 * i + 8, :],
                                    bank(f"w_t.{i}", 2 * ri + 1)[64:P, :].rearrange("p (r n) -> p r n", r=8)).then_inc(banks_dve, 1)
            split()
            split()
            for i in range(2):
                done(f"k.{i}")
                for m in range(4):
                    oc, g = 2 * i + m // 2, m % 2
                    lags = bank(f"k.{i}", m)[64 * g:64 * g + 64, :].rearrange("p (r l q) -> p r l q", r=8, l=T4)
                    tm = TM[64 * g:64 * g + 64, 8 * oc:8 * oc + 8, :].rearrange("p r (t q) -> p r t q", q=S5_GROUP)
                    for lag in range(T4):
                        if lag:
                            seq.wait()
                        for t in range(lag, T4):
                            o = dve.scalar_tensor_tensor(tm[:, :, t, :], lags[:, :, lag, :], MJ[64 * g:64 * g + 64, t - lag:t - lag + 1],
                                                         tm[:, :, t, :], ALU.mult, ALU.add)
                            if lag == T4 - 1:
                                o.then_inc(banks_dve, 1)
                            else:
                                seq.inc(o)
            dve.wait_ge(bs_in, 16)
            dve.wait_ge(tmp_free, 8)

            def sgu_out(i):
                done(f"sgu.{i}")
                for m in range(4):
                    g = 4 * i + m
                    dve.tensor_tensor(TMP[:, m % 2, :].rearrange("p (n i) -> p n i", i=P),
                                      bank(f"sgu.{i}", m).rearrange("p (n i) -> p n i", i=P),
                                      SGB[:, g, :].unsqueeze(1).to_broadcast([P, TT, P]), ALU.add).then_inc(banks_dve, 1)
                    dve.wait_ge(banks_dve, dve_after(f"sgu.{i}", m + 1))
                    dve.tensor_tensor(U[:, g, :], U[:, g, :], TMP[:, m % 2, :], ALU.mult).then_inc(ya_ready, 1)

            sgu_out(0)
            sgu_out(1)
            dve.wait_ge(ya_ready, 8)
            y_low(0, lambda kt: U[:, kt, :], range(8))
            split()
            split()
            dve.wait_ge(pads, 2)
            dve.wait_ge(consts, 4 + PPAD)

            def windows(k):
                w = POOL_WINDOWS[k]
                for kt in (2 * k, 2 * k + 1):
                    dve.wait_ge(banks_act, act_after(f"b_p.{kt // 4}", kt % 4 + 1))
                    src, step = CH[:, kt, :], 1
                    slot = 0
                    while step < w:
                        seq.inc(dve.tensor_tensor(WIN[:, slot, PPAD:], src[:, PPAD:], src[:, PPAD - step:PPAD - step + SEQ], ALU.add))
                        src, slot, step = WIN[:, slot, :], slot ^ 1, 2 * step
                        seq.wait()
                    seq.inc(dve.tensor_tensor(WIN[:, 2, PPAD:PPAD + w], src[:, PPAD:PPAD + w], INVC[:, 0:w], ALU.mult))
                    seq.inc(dve.scalar_tensor_tensor(U[:, kt, w:], src[:, PPAD + w:], 1.0 / w, CH[:, kt, PPAD + w:],
                                                     ALU.mult, ALU.subtract))
                    seq.wait()
                    o = dve.tensor_tensor(U[:, kt, 0:w], WIN[:, 2, PPAD:PPAD + w], CH[:, kt, PPAD:PPAD + w], ALU.subtract)
                    if kt % 2:
                        o.then_inc(d_ready, 1)
                    else:
                        seq.inc(o)

            windows(0)
            windows(1)
            split()
            done("w_a.0")
            for m in range(4):
                dve.tensor_tensor(M[:, m, :], bank("w_a.0", m), G[:, m, :], ALU.mult).then_inc(banks_dve, 1)
            split()
            windows(2)
            done("w_a.1")
            for m in range(4):
                dve.tensor_tensor(M[:, 4 + m, :], bank("w_a.1", m), G[:, 4 + m, :], ALU.mult).then_inc(banks_dve, 1)
            windows(3)
            split()
            split()
            for i in range(2):
                done(f"pool.{i}")
                for m in range(4):
                    kt = 4 * i + m
                    if kt >= 2:
                        dve.wait_ge(yb_ready, kt - 1)
                    dve.tensor_scalar(TMP[:, m % 2, :], bank(f"pool.{i}", m), col("pool_b", kt), col("pool_scale", kt),
                                      ALU.add, ALU.mult).then_inc(banks_dve, 1)
                    dve.wait_ge(banks_dve, dve_after(f"pool.{i}", m + 1))
                    if m == 0:
                        dve.wait_ge(banks_act, act_after(f"b_z.{i}"))
                    dve.tensor_tensor(CH[:, kt, PPAD:], CH[:, kt, PPAD:], TMP[:, m % 2, :], ALU.mult).then_inc(yb_ready, 1)
            dve.wait_ge(yb_ready, 8)
            y_low(1, lambda kt: CH[:, kt, PPAD:], range(8))
            split()
            split()
            split()
            split()

            def merge(job, u, version=None):
                done(job)
                for m in range(4):
                    kt = 4 * u + m
                    dve.tensor_tensor(TMP[:, m % 2, :], bank(job, m), G[:, kt, :], ALU.mult).then_inc(banks_dve, 1)
                    dve.wait_ge(banks_dve, dve_after(job, m + 1))
                    dve.tensor_tensor(M[:, kt, :], M[:, kt, :], TMP[:, m % 2, :], ALU.add).then_inc(m_acc, 1)

            split()
            dve.wait_ge(banks_act, act_after("g1.1"))
            dve.wait_ge(banks_dve, dve_after("w_a.1"))
            merge("w_b.0", 0)
            split()
            merge("w_b.1", 1)
            for u in range(2):
                split()
                done(f"c_c.{u}")
                dve.wait_ge(banks_act, act_after(f"c_h.{u}"))
                for m in range(4):
                    kt = 4 * u + m
                    dve.tensor_tensor(CH[:, kt, PPAD:], bank(f"c_c.{u}", m), CH[:, kt, PPAD:], ALU.mult).then_inc(banks_dve, 1)
                dve.wait_ge(side_done, side_after("pool.1"))
                for m in range(4):
                    kt = 4 * u + m
                    dve.wait_ge(banks_dve, dve_after(f"c_c.{u}", m + 1))
                    seq.inc(dve.tensor_scalar(U[:, kt, :], CH[:, kt, PPAD:], col("conv_w2", kt), col("conv_b", kt), ALU.mult, ALU.add))
                for k, s in ((1, 1), (0, 2)):
                    first = seq.n - 3
                    for m in range(4):
                        kt = 4 * u + m
                        seq.wait(first + m)
                        seq.inc(dve.scalar_tensor_tensor(U[:, kt, :], CH[:, kt, PPAD - s:PPAD - s + SEQ], col(f"conv_w{k}", kt),
                                                         U[:, kt, :], ALU.mult, ALU.add))
            split()
            split()
            split()
            seq.wait()
            for u in range(2):
                done(f"c_b.{u}")
                for m in range(4):
                    kt = 4 * u + m
                    dve.tensor_tensor(U[:, kt, :], bank(f"c_b.{u}", m), U[:, kt, :], ALU.mult).then_inc(banks_dve, 1)
                split()
            for u in range(2):
                dve.wait_ge(banks_dve, dve_after(f"c_b.{u}"))
                times_tmp([(f"c_z.{u}", m, U[:, 4 * u + m, :]) for m in range(4)])
                y_low(2, lambda kt: U[:, kt, :], range(4 * u, 4 * u + 4))
                split()
            dve.wait_ge(banks_act, act_after("g2.1"))
            dve.wait_ge(m_acc, 8)
            merge("w_c.0", 0)
            split()
            merge("w_c.1", 1)
            h_low(1, lambda kt: M[:, kt, :], range(8))
            split()
            dve.wait_ge(x_again, 16)
            for u in range(2):
                done(f"w_out.{u}")
                for t in range(TT):
                    dve.tensor_tensor(X[:, t, u * NC:(u + 1) * NC], bank(f"w_out.{u}", t), X[:, t, u * NC:(u + 1) * NC],
                                      ALU.add).then_inc(banks_dve, 1)
                if u == 0:
                    split()
            dve.wait_ge(std1, 1)
            rstd(1)
            dve.wait_ge(frow_in, 16)
            for t in range(TT):
                dve.scalar_tensor_tensor(X[:, t, :], X[:, t, :], STAT[:, 3, t:t + 1], FROW[:, :], ALU.mult, ALU.mult).then_inc(x1_done, 1)
            dve.wait_ge(std2, 1)
            rstd(1)
            for t in range(TT):
                dve.tensor_scalar(XN1[:, t, :], X[:, t, :], STAT[:, 3, t:t + 1], None, ALU.mult).then_inc(xn1, 1)
            turned("u_t.0", 0, "norm_pre0", 2)
            turned("u_t.1", 4, "norm_pre0", 2)

            split()
            split()
            times_tmp([("b_gate.0", m, CP[:, m, CPAD:]) for m in range(4)], GATEV)
            dve.wait_ge(cpads, 1)

            def taps():
                for kt0 in range(0, KT, 2):
                    for k in range(CONV_K):
                        for s in range(2):
                            yield kt0 + s, k, s

            todo = list(taps())
            conv = {"i": 0}

            def convolve(n):
                for kt, k, s in todo[conv["i"]:conv["i"] + n]:
                    w = PRM[:, 8 * (VEC_CONV + k) + kt:8 * (VEC_CONV + k) + kt + 1]
                    if k == 0:
                        if kt >= 2:
                            dve.wait_ge(conv_done, kt - 1)
                        conv[s] = seq.inc(dve.tensor_scalar(TMP[:, s, :], CP[:, kt, 0:SEQ], w, col("conv_b_2", kt), ALU.mult, ALU.add))
                    else:
                        seq.wait(conv[s])
                        last = k == CONV_K - 1
                        o = dve.scalar_tensor_tensor(CP[:, kt, CPAD:] if last else TMP[:, s, :], CP[:, kt, k:k + SEQ], w,
                                                     TMP[:, s, :], ALU.mult, ALU.add)
                        if last:
                            o.then_inc(conv_done, 1)
                        else:
                            conv[s] = seq.inc(o)
                    conv["i"] += 1

            dve.wait_ge(tmp_free, 20)
            dve.wait_ge(m_acc, 16)
            convolve(30)
            split()
            convolve(30)
            split()
            convolve(64)
            split()
            split()
            times_tmp([("b_gate.1", m, CP[:, 4 + m, CPAD:]) for m in range(4)], GATEV)
            dve.wait_ge(tmp_free, 24)
            convolve(26)
            split()
            convolve(30)
            split()
            dve.wait_ge(carried, 1)
            for b in range(PAIRS // FB):
                for q in range(2):
                    fix, into, by, end, op = correction(b, 1, q, 1)
                    seq.wait()
                    seq.inc(dve.tensor_tensor(fix, by, end, ALU.mult))
                    seq.wait()
                    o = dve.tensor_tensor(into, into, fix, op)
                    if q == 0 or b < PAIRS // FB - 1:
                        seq.inc(o)
                    else:
                        o.then_inc(states_fixed, 1)
            split()
            convolve(30)
            split()
            convolve(len(todo))

            for i in range(2):
                for m in range(4):
                    kt = 4 * i + m
                    dve.wait_ge(y_hi, 24 + kt + 1)
                    src = bank(f"y_t.{i}", m).rearrange("p (t c) -> p t c", t=T4)
                    seq.inc(dve.tensor_copy(YA[:, kt, :].rearrange("p (c t) -> p t c", t=T4), src))
                    dve.tensor_tensor(YL[:, kt, :].rearrange("p (c t) -> p t c", t=T4), src,
                                      YH[:, kt, :].bitcast(F32).rearrange("p (c t) -> p t c", t=T4), ALU.subtract).then_inc(y_lo, 1)
            dve.wait_ge(side_done, side_after("s5_y.1"))
            dve.memset(ONES[:, :], 1.0 / D).then_inc(ones_in, 1)
            seq.wait()
            split()
            for u in range(2):
                if u:
                    split()
                    h_low(3, lambda kt: YA[:, kt, :], range(4))
                times_tmp([(f"glu.{u}", m, YA[:, 4 * u + m, :]) for m in range(4)], GLUV)
                for m in range(4):
                    dve.wait_ge(tmp_free, 24 + 4 * u + m + 1)
                    kt = 4 * u + m
                    if kt == 0:
                        dve.wait_ge(banks_act, act_after("a_z2.1"))
                    dve.tensor_tensor(YA[:, kt, :], YA[:, kt, :], AZ[:, kt, :], ALU.mult).then_inc(ya_final, 1)
            h_low(3, lambda kt: YA[:, kt, :], range(4, 8))
            done("mean")
            dve.tensor_copy(MU[:, :], bank("mean", 0)).then_inc(banks_dve, 1)
            dve.wait_ge(banks_dve, dve_after("mean"))
            dve.wait_ge(conv_done, 8)
            for kt in range(KT):
                dve.tensor_tensor(CP[:, kt, CPAD:], CP[:, kt, CPAD:], MU[:, :], ALU.subtract).then_inc(z_cent, 1)
            split()
            dve.wait_ge(banks_act, act_after("var"))
            seq.inc(dve.reciprocal(RS[:, :], RS[:, :]))
            seq.wait()
            dve.wait_ge(z_sq, 8)
            for kt in range(KT):
                dve.tensor_tensor(CP[:, kt, CPAD:], CP[:, kt, CPAD:], RS[:, :], ALU.mult).then_inc(z_norm, 1)
            y_low(4, lambda kt: CP[:, kt, CPAD:], range(8))
            split()
            split()
            for u in range(2):
                if u:
                    split()
                done(f"pw.{u}")
                if u == 0:
                    dve.wait_ge(banks_act, act_after("b_z2.1"))
                for m in range(4):
                    kt = 4 * u + m
                    dve.scalar_tensor_tensor(BZ[:, kt, :], bank(f"pw.{u}", m), col("b_pw", kt), BZ[:, kt, :],
                                             ALU.add, ALU.mult).then_inc(banks_dve, 1)
                h_low(4, lambda kt: BZ[:, kt, :], range(4 * u, 4 * u + 4))
            split()
            dve.wait_ge(banks_act, act_after("ev_a.1"))
            for u in range(2):
                done(f"ev_b.{u}")
                for t in range(TT):
                    dve.tensor_tensor(YO[:, t, u * NC:(u + 1) * NC], bank(f"ev_b.{u}", t), YO[:, t, u * NC:(u + 1) * NC],
                                      ALU.add).then_inc(banks_dve, 1)
            dve.wait_ge(std3, 1)
            rstd(1)
            dve.wait_ge(prow0_in, 16)
            dve.wait_ge(x1_in, 16)
            for t in range(TT):
                seq.inc(dve.scalar_tensor_tensor(YO[:, t, :], YO[:, t, :], STAT[:, 3, t:t + 1], PROW0[:, :], ALU.mult, ALU.mult))
            for t in range(TT):
                seq.wait(seq.n - TT + 1 + t)
                dve.tensor_tensor(X1[:, t, :], X1[:, t, :], YO[:, t, :], ALU.add).then_inc(x2_done, 1)
            dve.wait_ge(std4, 1)
            rstd(1)
            for t in range(TT):
                dve.tensor_scalar(XN2[:, t, :], X1[:, t, :], STAT[:, 3, t:t + 1], None, ALU.mult).then_inc(xn2, 1)
            dve.memset(LWH[:, :, :].bitcast(F32), 0.0).then_inc(lw_zero, 1)
            dve.memset(LWL[:, :, :].bitcast(F32), 0.0).then_inc(lw_zero, 1)
            turned("u2_t.0", 0, "norm_pre1", 5)
            turned("u2_t.1", 4, "norm_pre1", 5)
            dve.wait_ge(lw_hi, 1)
            dve.tensor_tensor(LWL[:, :, 0:LOWRANK], LWR[:, :, :], LWH[:, :, 0:LOWRANK].bitcast(F32), ALU.subtract).then_inc(lw_lo, 1)

            dve.wait_ge(gla_consts, 1)
            A, B = [PS[:, m, :] for m in range(4)], [PS[:, 4 + m, :] for m in range(4)]

            def hsplit(n, j0, count):
                for j in range(j0, j0 + count):
                    s = j % RING
                    dve.wait_ge(w_hi, n + (j + 1))
                    dve.tensor_tensor(WL[:, s, :, :], WR[:, s, :, :], WH[:, s, :, :].bitcast(F32),
                                      ALU.subtract).then_inc(w_lo, 1)

            hsplit(N_STATIC, 0, 4)
            hsplit(head_base(0), V_AT, 2)
            seq0 = seq.n

            def chunks4(v):
                return v.rearrange("p k (t c i) -> p k t c i", c=2, i=CHUNK)

            def head(h, last):
                n = head_base(h)
                seq.base, seq.n = h * HSEQ_DVE + seq0, 0
                hsplit(n, V_AT + 2, 2)
                for m in range(2):
                    dve.wait_ge(e_abs, h * 2 + (m + 1))
                    dve.scalar_tensor_tensor(ET[:, m, :], B[m], 0.0, ET[:, m, :], ALU.min, ALU.subtract).then_inc(g_read, 1)
                dve.wait_ge(g_read, h * 2 + 2)
                dve.tensor_tensor_scan(BC[:, :, :].rearrange("p k t -> p (k t)"), SMASK[:, :],
                                       ET[:, :, :].rearrange("p k t -> p (k t)"), 0.0, ALU.mult, ALU.add).then_inc(g_scan, 1)
                dve.wait_ge(e_q, h + 1)
                dve.wait_ge(qk_copied, h * 4 + 4)
                dve.scalar_tensor_tensor(QD[:, :, :], QK[:, 0:2, :], float(HK) ** -0.5, ET[:, :, :], ALU.mult, ALU.mult).then_inc(qd_done, 1)
                dve.wait_ge(e_ke, h + 1)
                dve.tensor_tensor(KE[:, :, :], QK[:, 2:4, :], ET[:, :, :], ALU.mult).then_inc(ke_done, 1)
                dve.wait_ge(g_scan, h * 2 + 1)
                b4 = BC[:, :, :].rearrange("p k (c t) -> p (k c) t", t=CHUNK)
                dve.tensor_tensor(KX[:, :, :].rearrange("p k (c t) -> p (k c) t", t=CHUNK),
                                  b4[:, :, CHUNK - 1:CHUNK].to_broadcast([P, 2 * GCH, CHUNK]), b4, ALU.subtract).then_inc(g_scan, 1)
                dve.wait_ge(dec_in, h + 1)
                dec = DEC[:, :, :].rearrange("p k (t c) -> p k t c", c=2)
                seq.inc(dve.tensor_tensor(DD[:, :, :], dec[:, :, :, 0], dec[:, :, :, 1], ALU.mult))
                dve.wait_ge(qd_done, h + 1)
                for k in range(2):
                    qd, qx = [v[:, k, :].rearrange("p (t c i) -> p t c i", c=2, i=CHUNK) for v in (QD, QX)]
                    seq.inc(dve.tensor_copy(qx[:, :, 0, :], qd[:, :, 0, :]))
                    seq.inc(dve.tensor_tensor(qx[:, :, 1, :], qd[:, :, 1, :],
                                              dec[:, k, :, 0:1].to_broadcast([P, TT, CHUNK]), ALU.mult))
                seq.wait(5)
                dve.memset(BNA[:, 0, 0:1], 0.0).then_inc(qx_done, 1)
                dve.wait_ge(e_d, h + 1)
                for k in range(2):
                    kr, et, kx = [v.rearrange("p (t c i) -> p t c i", c=2, i=CHUNK) for v in (QK[:, 2 + k, :], ET[:, k, :], KX[:, k, :])]
                    seq.inc(dve.tensor_tensor(KD1[:, k, :, :], kr[:, :, 0, :], et[:, :, 0, :], ALU.mult))
                    seq.inc(dve.tensor_tensor(kx[:, :, 1, :], kr[:, :, 1, :], et[:, :, 1, :], ALU.mult))
                for k in range(2):
                    seq.wait(6 + 2 * k)
                    kx = KX[:, k, :].rearrange("p (t c i) -> p t c i", c=2, i=CHUNK)
                    seq.inc(dve.tensor_tensor(kx[:, :, 0, :], KD1[:, k, :, :],
                                              dec[:, k, :, 1:2].to_broadcast([P, TT, CHUNK]), ALU.mult))
                seq.wait(11)
                dve.memset(BNA[:, 0, 1:2], 0.0).then_inc(kx_done, 1)
                hsplit(n, R_AT, 4)
                hsplit(n, QK_AT, 4)
                for m in range(4):
                    dve.wait_ge(r_copied, h * 4 + (m + 1))
                    if m == 3:
                        dve.wait_ge(sc_out, h + 1)
                    dve.tensor_scalar(RR[:, m, :], RR[:, m, :], col("gla_norm_g", m), None, ALU.mult).then_inc(rr_in, 1)
                for t in range(TT):
                    dve.copy_predicated(ATS[:, t, :], CMASK[:, :].bitcast(U32), A[2][:, t * P:(t + 1) * P]).then_inc(ats_copied, 1)
                dve.wait_ge(ats_copied, h * 5 + 4)
                dve.tensor_copy(ATS[0:CHUNK, :, CHUNK:P],
                                A[3][0:CHUNK, 0:TT * CHUNK].rearrange("p (t i) -> p t i", i=CHUNK)).then_inc(ats_copied, 1)
                for t in range(TT - 1):
                    dve.wait_ge(d_out, h * 3 + (t + 1))
                    delta = PS[:, 4 + 2 * (t % 2):6 + 2 * (t % 2), :]
                    if t == 0:
                        dve.tensor_copy(ST[:, 0, :, :], delta).then_inc(st_done, 1)
                        continue
                    dve.wait_ge(st_done, h * HST + (2 * t - 1))
                    if t == 2:
                        dve.wait_ge(o_out, h * 4 + 2)
                    for k in range(2):
                        dve.scalar_tensor_tensor(ST[:, t % 2, k, :], ST[:, (t - 1) % 2, k, :], DD[:, k, t:t + 1], delta[:, k, :],
                                                 ALU.mult, ALU.add).then_inc(st_done, 1)
                dve.wait_ge(o_std, h + 1)
                seq.inc(dve.reciprocal(STAT[:, 3, :], STAT[:, 1, :]))
                seq.wait()
                for m in range(TT):
                    dve.tensor_scalar(ON[:, m, :], A[m], STAT[:, 3, m:m + 1], None, ALU.mult).then_inc(on_done, 1)
                if not last:
                    hsplit(n, out_at(last), 2)
                dve.wait_ge(rr_in, h * 4 + 4)
                for m in range(4):
                    dve.wait_ge(ot_out, h * 4 + (m + 1))
                    dve.tensor_tensor(RR[:, m, :], A[m], RR[:, m, :], ALU.mult).then_inc(o_f, 1)
                for m in range(4):
                    dve.wait_ge(o_hi, h * 4 + (m + 1))
                    dve.tensor_tensor(OL[:, m, :], RR[:, m, :], OH[:, m, :].bitcast(F32), ALU.subtract).then_inc(o_lo, 1)
                if not last:
                    hsplit(n, out_at(last) + 2, 2)
                dve.wait_ge(y2_add, h * 8 + 8)
                for u in range(2):
                    if u and not last:
                        hsplit(n, HEAD_CHUNKS + V_AT, 2)
                    dve.wait_ge(weights_used, n + (out_at(last) + 2 * (u + 1)))
                    for t in range(TT):
                        dve.tensor_tensor(YO2[:, t, u * NC:(u + 1) * NC], (B, A)[u][t], YO2[:, t, u * NC:(u + 1) * NC],
                                          ALU.add).then_inc(y2_add, 1)
                assert seq.n == HSEQ_DVE

            with dve.Fori(0, HEADS - 1) as h:
                head(h, False)
            head(HEADS - 1, True)
            seq.base, seq.n = 0, seq0 + HEADS * HSEQ_DVE

            dve.wait_ge(std5, 1)
            rstd(1)
            dve.wait_ge(prow1_in, 16)
            for t in range(TT):
                seq.inc(dve.scalar_tensor_tensor(YO2[:, t, :], YO2[:, t, :], STAT[:, 3, t:t + 1], PROW1[:, :], ALU.mult, ALU.mult))
            for t in range(TT):
                seq.wait(seq.n - TT + 1 + t)
                dve.tensor_tensor(YO2[:, t, :], X1[:, t, :], YO2[:, t, :], ALU.add).then_inc(fin, 1)

        @block.tensor
        def _(pe):
            state = {"n": 0}

            def free(name, skip=True):
                i = NAMES.index(name)
                if i < 2:
                    return
                prev = JOBS[i - 2]
                if _sum(3, i - 1):
                    pe.wait_ge(banks_act, _sum(3, i - 1))
                if _sum(4, i - 1):
                    pe.wait_ge(banks_dve, _sum(4, i - 1))
                if prev[5]:
                    pe.wait_ge(h_lo if prev[5][0] == "h" else y_lo, prev[5][1])

            halves = ((0, 0), (0, 1), (1, 0))

            def unit(n0, out_banks, acts, kt_ready, rows, tok=None, slot0=0, per=4, chunks=None, bank_ready=None):
                for q in chunks or range(per):
                    s = (slot0 + q) % RING
                    pe.wait_ge(w_lo, n0 + (q + 1))
                    for kk in range(2):
                        kt = 2 * q + kk
                        kt_ready(kt)
                        for m in range(4):
                            if bank_ready and kt == 0:
                                bank_ready(m)
                            for i, (wi, ai) in enumerate(halves):
                                w, x = (WH, WL)[wi], acts(kt)[ai]
                                if rows:
                                    st, mv = tok(x, m), w[:, s, kk, :]
                                else:
                                    st, mv = w[:, s, kk, m * P:(m + 1) * P], x
                                mm = pe.matmul(out_banks[m], st, mv, start=(kt == 0 and i == 0), stop=(kt == 2 * per - 1 and i == 2))
                    mm.then_inc(weights_used, 1)

            def tile(x, m):
                return x[:, m * P:(m + 1) * P]

            def strided(x, m):
                return x.rearrange("p (c j) -> p j c", j=T4)[:, m, :]

            def acts_of(hi, lo):
                return lambda kt: (hi[:, kt, :], lo[:, kt, :])

            def ready(s, version):
                return lambda kt: pe.wait_ge(s, 8 * version + min(kt, 7) + 1)

            H, Y = acts_of(HH, HL), acts_of(YH, YL)

            def section(name, acts, r, rows=False, tok=tile, per=4, units=(0, 1)):
                for u in units:
                    job = f"{name}.{u}"
                    free(job)
                    unit(chunks_before(job), [bank(job, m) for m in range(4)], acts, r if u == 0 else (lambda kt: None),
                         rows, tok, per=per)

            def run(names, acts, r):
                first = NAMES.index(names[0] + ".0")
                need = [(_sum(3, first + i - 1), _sum(4, first + i - 1)) for i in range(2 * len(names))]
                r(7)
                n0 = chunks_before(names[0] + ".0")
                da, dd = need[2][0] - need[0][0], need[2][1] - need[0][1]
                assert all(need[i + 2] == (need[i][0] + da, need[i][1] + dd) for i in range(2 * len(names) - 2)), names
                prev = [JOBS[first + i - 2][5] for i in range(2)]
                for p in prev:
                    if p:
                        pe.wait_ge(h_lo if p[0] == "h" else y_lo, p[1])
                with pe.Fori(0, len(names)) as s:
                    for u in range(2):
                        if need[u][0]:
                            pe.wait_ge(banks_act, s * da + need[u][0])
                        if need[u][1]:
                            pe.wait_ge(banks_dve, s * dd + need[u][1])
                        job = f"{names[0]}.{u}"
                        unit(s * 8 + (n0 + 4 * u), [bank(job, m) for m in range(4)], acts, lambda kt: None, False)

            def turn(job, srcs, sem_=None):
                free(job)
                for m, four in enumerate(srcs):
                    for t, (src, wait) in enumerate(four):
                        if wait:
                            wait()
                        mm = pe.transpose(bank(job, m)[:, t * P:(t + 1) * P], src, ident[:, :])
                    mm.then_inc(side_done, 1)

            def turn_tokens(job, x, kt0, s):
                turn(job, [[(x[:, t, (kt0 + m) * P:(kt0 + m + 1) * P], lambda t=t: pe.wait_ge(s, t + 1)) for t in range(TT)]
                           for m in range(4)])

            pe.wait_ge(consts, 4)
            pe.wait_ge(prm_in, 16 * 14)
            for i, n in enumerate((116, P, 8 * CONV_K - P)):
                mm = pe.transpose(bank("params", i)[:, 0:n], PR[0:n, i, :], ident[0:n, 0:n])
            mm.then_inc(side_done, 1)
            turn_tokens("h_t.0", XN0, 0, xn0)
            turn_tokens("h_t.1", XN0, 4, xn0)
            section("a_v", H, ready(h_lo, 0), rows=True)
            pe.wait_ge(c_in, 16 * 32)
            free("c_t")
            for i in range(2):
                for t in range(4):
                    mm = pe.transpose(bank("c_t", i)[:, t * P:(t + 1) * P], CRAW[:, i, t, :], ident[:, :])
            mm.then_inc(side_done, 1)
            section("a_u", H, ready(h_lo, 0))
            section("a_z", H, ready(h_lo, 0))
            pe.wait_ge(pool_w, 1)
            for i in range(4):
                free(f"w_t.{i}")
                for r in range(8):
                    for m in range(4):
                        ri, g = m // 2, m % 2
                        half = slice(64 * g, 64 * g + 64)
                        mm = pe.matmul(bank(f"w_t.{i}", m)[half, r * 64:(r + 1) * 64],
                                       WST[half, ri, 8 * i + r, :, :].rearrange("p j q -> p (j q)"), ident[half, half],
                                       start=True, stop=True)
                mm.then_inc(side_done, 1)
            pe.wait_ge(sgw_masked, 1)
            free("sgu_t")
            for g in range(SGU_GROUPS):
                mm = pe.transpose(bank("sgu_t", g // 4)[:, (g % 4) * P:(g % 4 + 1) * P], SGW[:, g, :], ident[:, :])
            mm.then_inc(side_done, 1)
            section("g0", H, ready(h_lo, 0))
            pe.wait_ge(pool_g, 1)
            pe.wait_ge(pool_rep, 2)
            for i in range(2):
                free(f"k.{i}")
                for r in range(8):
                    for m in range(4):
                        oc, g = 2 * i + m // 2, m % 2
                        pr, half = 8 * oc + r, slice(64 * g, 64 * g + 64)
                        for ri, lags in enumerate((GRE, GNI)):
                            mm = pe.matmul(bank(f"k.{i}", m)[half, r * 64:(r + 1) * 64],
                                           WST[half, ri, pr, :, :].rearrange("p j q -> p (j q)"),
                                           lags[half, pr, 0:T4, :].rearrange("p l q -> p (l q)"),
                                           start=(ri == 0), stop=(ri == 1))
                mm.then_inc(side_done, 1)
            pe.wait_ge(v_done, 4)
            for i in range(2):
                free(f"sgu.{i}")
                if i == 0:
                    pe.wait_ge(banks_act, act_after("sgu_t"))
                for m in range(4):
                    g = 4 * i + m
                    for t in range(TT):
                        mm = pe.matmul(bank(f"sgu.{i}", m)[:, t * P:(t + 1) * P], V[:, t, g * P:(g + 1) * P], SGWT[:, g, :],
                                       start=True, stop=True)
                mm.then_inc(side_done, 1)
            section("b_p", H, ready(h_lo, 0))
            section("w_a", Y, ready(y_lo, 0))
            section("b_z", H, ready(h_lo, 0))
            pe.wait_ge(pw_in, 16)
            for i in range(2):
                free(f"pool.{i}")
                for m in range(4):
                    kt = 4 * i + m
                    g = kt // 2
                    pe.wait_ge(d_ready, g + 1)
                    for k in range(2):
                        mm = pe.matmul(bank(f"pool.{i}", m), PW[:, g, k, (kt % 2) * P:(kt % 2 + 1) * P], U[:, 2 * g + k, :],
                                       start=(k == 0), stop=(k == 1))
                mm.then_inc(side_done, 1)
            section("g1", H, ready(h_lo, 0))
            section("c_h", H, ready(h_lo, 0))
            section("w_b", Y, ready(y_lo, 1))
            section("c_c", H, ready(h_lo, 0))
            section("g2", H, ready(h_lo, 0))
            section("c_b", H, ready(h_lo, 0))
            section("c_z", H, ready(h_lo, 0))
            section("w_c", Y, ready(y_lo, 2))
            section("w_out", H, ready(h_lo, 1), rows=True)
            turn_tokens("u_t.0", XN1, 0, xn1)
            turn_tokens("u_t.1", XN1, 4, xn1)
            section("b_val", H, ready(h_lo, 2), units=(0,))
            section("b_gate", H, ready(h_lo, 2), units=(0,))
            section("a_in", H, ready(h_lo, 2), rows=True, tok=strided)
            for u in range(2):
                pe.wait_ge(banks_act, act_after(f"a_in.{u}"))
                free(f"s5_t.{u}")
                for m in range(4):
                    for r in range(4):
                        pr = 4 * m + r
                        mm = pe.transpose(bank(f"s5_t.{u}", m)[:, r * P:(r + 1) * P],
                                          AS[:, u, 2 * pr:2 * pr + 2, :, :].rearrange("c g j q -> c (g j q)"), ident[:, :])
                mm.then_inc(side_done, 1)
            pe.wait_ge(wt_in, 32)
            for i in range(4):
                free(f"s5_z.{i}")
                pe.wait_ge(banks_act, act_after("s5_t.0" if i < 2 else "s5_t.1"))
                for m in range(4):
                    for r in range(4):
                        pr = 8 * i + 4 * (m % 2) + r
                        mm = pe.matmul(bank(f"s5_z.{i}", m)[:, r * P:(r + 1) * P], WT[m // 2][:, pr, :], UT[:, pr, :],
                                       start=True, stop=True)
                mm.then_inc(side_done, 1)
            section("b_val", H, ready(h_lo, 2), units=(1,))
            section("b_gate", H, ready(h_lo, 2), units=(1,))
            section("a_z2", H, ready(h_lo, 2))
            section("b_z2", H, ready(h_lo, 2))
            pe.wait_ge(states_fixed, 2)
            for i in range(2):
                free(f"s5_y.{i}")
                pe.wait_ge(t6_in, 16 * (i + 1))
                pe.wait_ge(vt_in, 16 * (i + 1))
                for r in range(PAIRS // 2):
                    pr = 16 * i + r
                    o = bank(f"s5_y.{i}", r // 4)[:, (r % 4) * P:(r % 4 + 1) * P]
                    pe.matmul(o, UT[:, pr, :], T6[i][:, r, :], start=True, stop=False)
                    pe.matmul(o, S[:, 0, pr, :], VT[i][:, 0, r, :], start=False, stop=False)
                    mm = pe.matmul(o, S[:, 1, pr, :], VT[i][:, 1, r, :], start=False, stop=True)
                mm.then_inc(side_done, 1)
            for i in range(2):
                pe.wait_ge(banks_act, act_after("s5_y.1"))
                turn(f"y_t.{i}", [[(YT[:, t, (4 * i + m) * P:(4 * i + m + 1) * P], None) for t in range(T4)] for m in range(4)])
            section("glu", Y, ready(y_lo, 3))
            pe.wait_ge(ones_in, 1)
            pe.wait_ge(conv_done, 8)
            free("mean")
            for kt in range(KT):
                mm = pe.matmul(bank("mean", 0), ONES[:, :], CP[:, kt, CPAD:], start=(kt == 0), stop=(kt == KT - 1))
            mm.then_inc(side_done, 1)
            section("ev_a", H, ready(h_lo, 3), rows=True, units=(0,))
            free("var")
            for kt in range(KT):
                pe.wait_ge(z_sq, kt + 1)
                mm = pe.matmul(bank("var", 0), ONES[:, :], SQ[:, kt, :], start=(kt == 0), stop=(kt == KT - 1))
                mm.then_inc(sq_used, 1)
            section("ev_a", H, ready(h_lo, 3), rows=True, units=(1,))
            section("pw", Y, ready(y_lo, 4))
            section("ev_b", H, ready(h_lo, 4), rows=True)
            turn_tokens("u2_t.0", XN2, 0, xn2)
            turn_tokens("u2_t.1", XN2, 4, xn2)
            free("lr")
            pe.wait_ge(lw_lo, 1)
            pe.wait_ge(h_lo, 48)
            for kt in range(KT):
                for i, (wi, ai) in enumerate(halves):
                    mm = pe.matmul(bank("lr", 0), (LWH, LWL)[wi][:, kt, :], (HH, HL)[ai][:, kt, :],
                                   start=(kt == 0 and i == 0), stop=(kt == KT - 1 and i == 2))
            mm.then_inc(lr_out, 1)
            pe.wait_ge(banks_act, act_after("lr"))

            A, B = [PS[:, m, :] for m in range(4)], [PS[:, 4 + m, :] for m in range(4)]
            nowait = lambda kt: None
            unit(N_STATIC, A, H, nowait, False)

            def head(h, last):
                n = head_base(h)
                pe.wait_ge(gu_in, h * 32 + 32)
                pe.wait_ge(y2_add, h * 8 + 4)
                for m in range(2):
                    mm = pe.matmul(B[m], GU[0:LOWRANK + 1, m * P:(m + 1) * P], LR[0:LOWRANK + 1, :], start=True, stop=True)
                mm.then_inc(g_out, 1)
                pe.wait_ge(qk_copied, h * 4 + 4)
                unit(n + V_AT, A, H, nowait, True, tile, bank_ready=lambda m: pe.wait_ge(y2_add, h * 8 + (4 + m + 1)))
                pe.wait_ge(g_read, h * 2 + 2)
                unit(n + R_AT, B, H, nowait, False)
                pe.wait_ge(v_copied, h * 4 + 4)
                pe.wait_ge(kx_done, h + 1)
                for t in range(TT):
                    for k in range(2):
                        mm = pe.transpose(A[t // 2][:, ((t % 2) * 2 + k) * P:((t % 2) * 2 + k + 1) * P],
                                          KX[:, k, t * P:(t + 1) * P], ident[:, :])
                mm.then_inc(kt_out, 1)
                for t in range(TT):
                    for k in range(2):
                        pe.matmul(A[2][:, t * P:(t + 1) * P], KE[:, k, t * P:(t + 1) * P], QD[:, k, t * P:(t + 1) * P],
                                  start=(k == 0), stop=(k == 1))
                for t in range(TT):
                    for k in range(2):
                        mm = pe.matmul(A[3][0:CHUNK, t * CHUNK:(t + 1) * CHUNK], KD1[:, k, t, :],
                                       QD[:, k, t * P + CHUNK:(t + 1) * P], start=(k == 0), stop=(k == 1))
                mm.then_inc(sc_out, 1)

                def delta(t):
                    for k in range(2):
                        mm = pe.matmul(B[2 * (t % 2) + k], KTK[:, t, k, :], V2[:, t, :], start=True, stop=True)
                    mm.then_inc(d_out, 1)

                pe.wait_ge(r_copied, h * 4 + 4)
                pe.wait_ge(kt_copied, h * 2 + 2)
                delta(0)
                delta(1)
                pe.wait_ge(ats_copied, h * 5 + 5)
                for t in range(TT):
                    mm = pe.matmul(A[t], ATS[:, t, :], V2[:, t, :], start=True, stop=(t == 0), skip_group_check=True)
                    if t == 0:
                        mm.then_inc(o_out, 1)
                pe.wait_ge(st_done, h * HST + 1)
                delta(2)
                pe.wait_ge(qx_done, h + 1)
                for t in range(1, TT):
                    pe.wait_ge(st_done, h * HST + (2 * t - 1))
                    for k in range(2):
                        mm = pe.matmul(A[t], QX[:, k, t * P:(t + 1) * P], ST[:, (t - 1) % 2, k, :],
                                       start=False, stop=(k == 1), skip_group_check=True)
                    mm.then_inc(o_out, 1)
                if not last:
                    pe.wait_ge(st_done, h * HST + HST)
                    unit(n + QK_AT, B, H, nowait, False, chunks=(0, 1))
                pe.wait_ge(on_done, h * 4 + 4)
                for m in range(4):
                    for t in range(TT):
                        mm = pe.transpose(A[m][:, t * P:(t + 1) * P], ON[:, t, m * P:(m + 1) * P], ident[:, :])
                    mm.then_inc(ot_out, 1)
                if not last:
                    unit(n + QK_AT, B, H, nowait, False, chunks=(2, 3))
                O = acts_of(OH, OL)
                o_ready = lambda kt: pe.wait_ge(o_lo, h * 4 + (kt + 1))
                free_b = None if last else lambda m: pe.wait_ge(qk_copied, h * 4 + (4 + m + 1))
                if last:
                    pe.wait_ge(st_done, h * HST + HST)
                unit(n + out_at(last), B, O, o_ready, True, tile, slot0=0, per=2, bank_ready=free_b)
                pe.wait_ge(o_f, h * 4 + 4)
                unit(n + (out_at(last) + 2), A, O, nowait, True, tile, slot0=2, per=2)

            with pe.Fori(0, HEADS - 1) as h:
                head(h, False)
            head(HEADS - 1, True)


def kernel(**inputs):
    import numpy as _np
    import concourse.bacc as _bacc
    from concourse import mybir as _mybir
    from concourse.bass_utils import run_bass_kernel_spmd as _run

    nc = _bacc.Bacc("TRN2", target_bir_lowering=False, num_devices=1)
    arrays, args = {}, {}
    for name in inputs:
        v = _np.ascontiguousarray(inputs[name])
        arrays[f"in_{name}_dram"] = v
        args[name] = nc.dram_tensor(f"in_{name}_dram", v.shape, _mybir.dt.from_np(v.dtype), kind="ExternalInput").ap()
    out = nc.dram_tensor("out_0_dram", (1, SEQ, D), _mybir.dt.float32, kind="ExternalOutput").ap()
    three_branch_s5_gla_kernel(nc, args, out)
    r = _run(nc, [arrays], core_ids=[0])
    return r.results[0]["out_0_dram"]
```

```python
from contextlib import ExitStack

import numpy as np
import concourse.bass as bass
from concourse import mybir

F32 = mybir.dt.float32
F32R = mybir.dt.float32r
U32 = mybir.dt.uint32
ALU = mybir.AluOpType
ACT = mybir.ActivationFunctionType

P = 128
SEQ = 512
D = 1024
KT = D // P
TT = SEQ // P
NC = 512
RING = 4
SGU_GROUPS = 8
CHUNK = 64
POOL_WINDOWS = (2, 4, 8, 16)
PPAD = 16
CONV_K = 31
CPAD = CONV_K - 1
RMS_EPS = 1e-6
LN_EPS = 1e-5
S5_GROUP = 16
SEG, SEG_CH = 8, 16
T4 = 4
NCH = SEQ // T4
FB = 4
FIX_POOL = [(b, 0) for b in range(7)]
FIX_DVE = [(b, 1) for b in range(8)] + [(7, 0)]
FIX_HALF = 4
PAIRS = D // (2 * S5_GROUP)
PP = PAIRS - 8
HEADS = 4
HK = 256
HV = 512
LOWRANK = 16
GLA_TAU = 16.0
GCH = SEQ // CHUNK

TWO_PI = 2.0 * np.pi
PI_A = 6.28125
PI_B = float(np.float32(np.floor((TWO_PI - PI_A) * 2 ** 21) / 2 ** 21))
PI_C = float(np.float32(TWO_PI - PI_A - PI_B))
ROUND = 12582912.0

VEC = {n: i for i, n in enumerate(
    ["norm_g", "pool_b", "pool_scale", "conv_w0", "conv_w1", "conv_w2", "conv_b", "norm_pre0", "norm_pre1",
     "b_glu", "conv_b_2", "ln_g2", "ln_b2", "b_pw", "gla_norm_g"])}
VEC_CONV = 16
N_VEC = VEC_CONV + CONV_K

JOBS = []


def _add(name, chunks=0, side=0, a=0, d=0, lo=None):
    JOBS.append((name, chunks, side, a, d, lo))


def _section(name, a=0, d=0, chunks=4):
    for u in range(2):
        _add(f"{name}.{u}", chunks, 0, a, d)


_add("params", side=1, a=3)
_add("h_t.0", side=4, lo=("h", 4))
_add("h_t.1", side=4, lo=("h", 8))
_section("a_v", a=4)
_add("c_t", side=1, a=2)
_section("a_u", a=4)
_section("a_z", a=4)
for _i in range(4):
    _add(f"w_t.{_i}", side=1, a=2, d=2)
_add("sgu_t", side=1, a=2)
_section("g0", a=4)
for _i in range(2):
    _add(f"k.{_i}", side=1, a=4)
for _i in range(2):
    _add(f"sgu.{_i}", side=1, d=4)
_section("b_p", a=4)
_section("w_a", d=4)
_section("b_z", a=4)
for _i in range(2):
    _add(f"pool.{_i}", side=1, d=4)
_section("g1", a=4)
_section("c_h", a=4)
_section("w_b", d=4)
_section("c_c", d=4)
_section("g2", a=4)
_section("c_b", d=4)
_section("c_z", a=4)
_section("w_c", d=4)
_section("w_out", d=4)
_add("u_t.0", side=4, lo=("h", 20))
_add("u_t.1", side=4, lo=("h", 24))
_add("b_val.0", 4, 0, 4)
_add("b_gate.0", 4, 0, 4)
_section("a_in", a=4)
for _u in range(2):
    _add(f"s5_t.{_u}", side=1, a=4)
for _i in range(4):
    _add(f"s5_z.{_i}", side=1, a=4)
_add("b_val.1", 4, 0, 4)
_add("b_gate.1", 4, 0, 4)
_section("a_z2", a=4)
_section("b_z2", a=4)
for _i in range(2):
    _add(f"s5_y.{_i}", side=4, a=4)
for _i in range(2):
    _add(f"y_t.{_i}", side=4, a=4)
_section("glu", a=4)
_add("mean", side=1, d=1)
_add("ev_a.0", 4, 0, 4)
_add("var", a=1)
_add("ev_a.1", 4, 0, 4)
_section("pw", d=4)
_section("ev_b", d=4)
_add("u2_t.0", side=4, lo=("h", 44))
_add("u2_t.1", side=4, lo=("h", 48))
_add("lr", a=1)
NAMES = [j[0] for j in JOBS]


def _sum(column, upto):
    return sum(j[column] for j in JOBS[:upto])


def chunks_before(name):
    return _sum(1, NAMES.index(name))


def used_after(name):
    return _sum(1, NAMES.index(name) + 1)


def side_after(name, k=0):
    i = NAMES.index(name)
    return _sum(2, i) + (k if k else JOBS[i][2])


def act_after(name, k=0):
    i = NAMES.index(name)
    return _sum(3, i) + (k if k else JOBS[i][3])


def dve_after(name, k=0):
    i = NAMES.index(name)
    return _sum(4, i) + (k if k else JOBS[i][4])


UNITS = [j[0] for j in JOBS if j[1]]
N_STATIC = _sum(1, len(JOBS))
HEAD_CHUNKS = 16
V_AT, R_AT, QK_AT = 0, 4, 8
HST = 5
HSEQ_ACT, HSEQ_DVE = 6, 12


def out_at(last):
    return QK_AT if last else QK_AT + 4


def head_base(h):
    return h * HEAD_CHUNKS + (N_STATIC + 4)


def loaded(h, at, last=False):
    before = 16 * (N_STATIC // RING) + 32
    return h * 80 + before + {V_AT: 16, R_AT: 32, QK_AT: 48 if last else 64, QK_AT + 4: 80}[at]


W_IN = {n: i * D for i, n in enumerate(
    ["a_u", "a_v", "a_z", "b_p", "b_z", "c_h", "c_b", "c_c", "c_z", "g0", "g1", "g2"])}
EV_IN = {n: i * D for i, n in enumerate(["a_in", "a_z2", "b_val", "b_gate", "b_z2"])}


class Order:

    def __init__(self, eng, sem):
        self.eng, self.sem, self.n, self.base = eng, sem, 0, 0

    def inc(self, instruction):
        instruction.then_inc(self.sem, 1)
        self.n += 1
        return self.n

    def wait(self, n=None):
        self.eng.wait_ge(self.sem, self.base + (self.n if n is None else n))


def three_branch_s5_gla_kernel(nc, a, out):
    ctx = ExitStack()
    with ctx:
        def sem(name):
            return ctx.enter_context(nc.semaphore(name))

        at = {}
        start = nc.sbuf_base + -nc.sbuf_base % 32

        def region(name, size):
            at[name] = region.top
            region.top += size
        region.top = start
        for name, size in (("WR", 16384), ("WH", 16384), ("WL", 16384), ("HH", 16384), ("HL", 16384),
                           ("YH", 16384), ("YL", 16384), ("R1", 17344), ("R2", 16384), ("R3", 16384),
                           ("R4", 16384), ("R5", 16384), ("R6", 8192), ("ident", 512), ("PRM", 4 * 8 * N_VEC),
                           ("TMP", 4096), ("LAM", 384), ("SMALL", 376)):
            region(name, size)
        ctx.enter_context(nc.sbuf_tensor("arena", [P, (region.top - nc.sbuf_base + 3) // 4], F32))

        def put(name, where, shape, dt=F32, skip=0):
            return nc.alloc_sbuf_tensor_at(name, [P, *shape], dt, offset=at[where] + skip, align_bytes=4)

        WR = put("WR", "WR", [RING, 2, NC])
        WH = put("WH", "WH", [RING, 2, NC], F32R)
        WL = put("WL", "WL", [RING, 2, NC], F32R)
        HH = put("HH", "HH", [KT, SEQ], F32R)
        HL = put("HL", "HL", [KT, SEQ], F32R)
        YH = put("YH", "YH", [KT, SEQ], F32R)
        YL = put("YL", "YL", [KT, SEQ], F32R)
        ident = put("ident", "ident", [P])
        PRM = put("PRM", "PRM", [8 * N_VEC])
        TMP = put("TMP", "TMP", [2, NC])
        XN0 = put("XN0", "R1", [TT, D])
        V = put("V", "R1", [TT, D])
        CH = put("CH", "R1", [KT, PPAD + SEQ])
        U = put("U", "R2", [KT, SEQ])
        X = put("X", "R3", [TT, D])
        WIN = put("WIN", "R3", [3, PPAD + SEQ])
        M = put("M", "R4", [KT, SEQ])
        XN1 = put("XN1", "R4", [TT, D])
        G = put("G", "R5", [KT, SEQ])
        LNROWS = put("LNROWS", "R5", [2, D])
        SGW = put("SGW", "R5", [SGU_GROUPS, P], skip=8192)
        SGWT = put("SGWT", "R6", [SGU_GROUPS, P])
        SGB = put("SGB", "R6", [SGU_GROUPS, P], skip=4096)
        PW = put("PW", "R6", [4, 2, 256])
        FROW = put("FROW", "R6", [D])
        PR = put("PR", "R6", [3, P])
        GRE = put("GRE", "YH", [PAIRS, 5, S5_GROUP])
        GNI = put("GNI", "YH", [PAIRS, 5, S5_GROUP], skip=10240)
        TM = put("TM", "YH", [PAIRS, 64], skip=20480)
        CRAW = put("CRAW", "YH", [2, 4, P], skip=28672)
        KS = put("KS", "YH", [PAIRS // 2, T4, S5_GROUP], skip=28672)
        WST = put("WST", "R4", [2, PAIRS, T4, S5_GROUP])
        BRAW = put("BRAW", "R5", [2, PAIRS, S5_GROUP], skip=12288)
        WTS = put("WTS", "R3", [2, PAIRS, 64])
        PT = put("PT", "R3", [2, PAIRS, S5_GROUP])
        DT2 = put("DT2", "R3", [PAIRS, 64], skip=4096)
        LS = put("LS", "R6", [20, PAIRS], skip=1536)
        LAM = put("LAM", "LAM", [3, PAIRS])
        DCOL = put("DCOL", "SMALL", [PAIRS])
        INVC = put("INVC", "SMALL", [PPAD], skip=128)
        MJ = put("MJ", "SMALL", [4], skip=192)
        MJ8 = put("MJ8", "SMALL", [2, 4], skip=208)
        ST1 = put("ST1", "SMALL", [2, PAIRS])
        ST2 = put("ST2", "PRM", [2, PAIRS])
        STAT = put("STAT", "SMALL", [4, 4], skip=272)
        BNA = put("BNA", "SMALL", [4, 2], skip=336)
        EPS = put("EPS", "SMALL", [2], skip=368)
        BNS = put("BNS", "R6", [TT, 2, 6])
        CP = put("CP", "R1", [KT, CPAD + SEQ])
        UT = put("UT", "R2", [PAIRS, NCH])
        YA = put("YA", "R2", [KT, SEQ])
        WT = [put("WT_re", "R3", [PAIRS, P]), put("WT_im", "R5", [PAIRS, P])]
        VT = [put("VT_0", "R3", [2, PAIRS // 2, P]), put("VT_1", "HL", [2, PAIRS // 2, P])]
        T6 = [put("T6_0", "R5", [PAIRS // 2, P], skip=8192), put("T6_1", "HH", [PAIRS // 2, P])]
        X1 = put("X1", "R3", [TT, D])
        AS = put("AS", "R4", [2, 32, T4, S5_GROUP])
        AZ = put("AZ", "R4", [KT, SEQ])
        BZ = put("BZ", "R5", [KT, SEQ])
        XN2 = put("XN2", "R5", [TT, D])
        MU = put("MU", "R6", [SEQ])
        RS = put("RS", "R6", [SEQ])
        ONES = put("ONES", "R6", [P], skip=2048)
        GLUV = put("GLUV", "R6", [2, NC], skip=4096)
        GATEV = put("GATEV", "R4", [2, NC])
        SQ = put("SQ", "R3", [KT, SEQ])
        TAB = put("TAB", "R6", [2, PAIRS, SEG_CH])
        LAM64 = put("LAM64", "R6", [3, PAIRS], skip=4096)
        Q0 = put("Q0", "R6", [2, PAIRS, SEG_CH // 2], skip=4608)
        SEG1 = put("SEG1", "R5", [2, PAIRS, SEG])
        SEG2 = put("SEG2", "R5", [2, PAIRS, SEG], skip=2048)
        SEGV = put("SEGV", "R5", [2, 2, PAIRS - PP, SEG], skip=4096)
        FIX = put("FIX", "R6", [2, FB, SEG - 1, SEG_CH - 1], skip=4608)
        PROW0 = put("PROW0", "YL", [D])
        S = put("S", "YH", [2, PAIRS, NCH])
        YT = put("YT", "R3", [T4, D])
        YO = put("YO", "R2", [TT, D])
        YO2 = put("YO2", "R2", [TT, D])
        QK = put("QK", "R1", [4, SEQ])
        BC = put("BC", "R1", [2, SEQ], skip=8192)
        ET = put("ET", "R1", [2, SEQ], skip=12288)
        LWR = put("LWR", "R4", [KT, LOWRANK], skip=8192)
        LWH = put("LWH", "R4", [KT, P], F32R)
        LWL = put("LWL", "R4", [KT, P], F32R, skip=4096)
        QD = put("QD", "R4", [2, SEQ])
        KE = put("KE", "R4", [2, SEQ], skip=4096)
        KD1 = put("KD1", "R4", [2, TT, CHUNK], skip=8192)
        KTK = put("KTK", "R4", [TT, 2, P], skip=12288)
        PROW1 = put("PROW1", "R4", [D])
        V2 = put("V2", "R5", [TT, HV])
        RR = put("RR", "R5", [4, SEQ], skip=8192)
        ATS = put("ATS", "R6", [TT, P])
        CMASK = put("CMASK", "R6", [P], skip=2048)
        SMASK = put("SMASK", "R6", [2 * SEQ], skip=2560)
        GU = put("GU", "R6", [HK], skip=6656)
        LR = put("LR", "TMP", [SEQ])
        DEC = put("DEC", "TMP", [2, GCH], skip=2048)
        DD = put("DD", "TMP", [2, TT], skip=2112)
        OH = put("OH", "YH", [4, SEQ], F32R)
        OL = put("OL", "YH", [4, SEQ], F32R, skip=8192)
        ST = put("ST", "YL", [2, 2, HV])
        ON = put("ON", "YL", [TT, HV], skip=8192)
        KX = put("KX", "YL", [2, SEQ], skip=8192)
        QX = put("QX", "YL", [2, SEQ], skip=12288)

        PS = ctx.enter_context(nc.psum_tensor("PS", [P, 8, NC], F32))

        def bank(name, m):
            return PS[:, 4 * (NAMES.index(name) % 2) + m, :]

        d_wt = nc.dram_tensor("d_wt", [P, 2, PAIRS, P], F32, kind="Internal").ap()
        d_g = nc.dram_tensor("d_g", [P, 2, PAIRS, P], F32, kind="Internal").ap()
        d_tm = nc.dram_tensor("d_tm", [P, PAIRS, P], F32, kind="Internal").ap()
        d_x1 = nc.dram_tensor("d_x1", [SEQ, D], F32, kind="Internal").ap()

        w_loaded = [sem(f"w_loaded{i}") for i in range(RING)]
        w_hi, w_lo, weights_used = sem("w_hi"), sem("w_lo"), sem("weights_used")
        banks_act, banks_dve, side_done = sem("banks_act"), sem("banks_dve"), sem("side_done")
        act_seq, dve_seq, pool_seq = sem("act_seq"), sem("dve_seq"), sem("pool_seq")
        h_hi, h_lo, y_hi, y_lo = sem("h_hi"), sem("h_lo"), sem("y_hi"), sem("y_lo")
        prm_in, lam_in, c_in, b_in, sg_in, ln_in, d_in, bs_in = (sem(n) for n in (
            "prm_in", "lam_in", "c_in", "b_in", "sg_in", "ln_in", "d_in", "bs_in"))
        pw_in, x_again, frow_in, wt_in, vt_in, t6_in, x1_out, x1_in, prow0_in = (sem(n) for n in (
            "pw_in", "x_again", "frow_in", "wt_in", "vt_in", "t6_in", "x1_out", "x1_in", "prow0_in"))
        s5_out, zeros_out = sem("s5_out"), sem("zeros_out")
        x_in = [sem(f"x_in{t}") for t in range(TT)]
        zeroed, lagged, tiles_done = sem("zeroed"), sem("lagged"), sem("tiles_done")
        consts = sem("consts")
        sq0, std0, xn0 = sem("sq0"), sem("std0"), sem("xn0")
        v_std, v_done = sem("v_std"), sem("v_done")
        m_acc, sq_used, ke_done = sem("m_acc"), sem("sq_used"), sem("ke_done")
        lam_exp, lam_ang, lam_sin, lam_den, lam_rec = (sem(n) for n in (
            "lam_exp", "lam_ang", "lam_sin", "lam_den", "lam_rec"))
        pool_g, pool_w, pool_t = sem("pool_g"), sem("pool_w"), sem("pool_t")
        pool_rep = sem("pool_rep")
        sgw_masked = sem("sgw_masked")
        tmp_free = sem("tmp_free")
        ya_ready, d_ready, yb_ready, pads = sem("ya_ready"), sem("d_ready"), sem("yb_ready"), sem("pads")
        cpads = sem("cpads")
        x1_done, xn1, sq1, std1, sq2, std2 = (sem(n) for n in (
            "x1_done", "xn1", "sq1", "std1", "sq2", "std2"))
        states, conv_done = sem("states"), sem("conv_done")
        dve_states = sem("dve_states")
        carried, fixed_pool, fixed_dve = sem("carried"), sem("fixed_pool"), sem("fixed_dve")
        ya_gated, z_cent, z_sq, z_norm, z_act, ones_in = (sem(n) for n in (
            "ya_gated", "z_cent", "z_sq", "z_norm", "z_act", "ones_in"))
        sq3, std3, x2_done, sq4, std4, xn2 = (sem(n) for n in ("sq3", "std3", "x2_done", "sq4", "std4", "xn2"))
        lw_in, lw_zero, lw_hi, lw_lo, gla_consts = (sem(n) for n in (
            "lw_in", "lw_zero", "lw_hi", "lw_lo", "gla_consts"))
        gu_in = sem("gu_in")
        e_abs, g_scan, e_q, e_ke, e_d, dec_in, qd_done, kx_done, qx_done = (sem(n) for n in (
            "e_abs", "g_scan", "e_q", "e_ke", "e_d", "dec_in", "qd_done", "kx_done", "qx_done"))
        lr_out, g_out, kt_out, sc_out, d_out, o_out, ot_out = (sem(n) for n in (
            "lr_out", "g_out", "kt_out", "sc_out", "d_out", "o_out", "ot_out"))
        qk_copied, v_copied, r_copied, kt_copied = (sem(n) for n in (
            "qk_copied", "v_copied", "r_copied", "kt_copied"))
        g_read, ats_copied, on_done, y2_add = (sem(n) for n in (
            "g_read", "ats_copied", "on_done", "y2_add"))
        o_sq, o_std, o_f, o_hi, o_lo, rr_in, st_done = (sem(n) for n in (
            "o_sq", "o_std", "o_f", "o_hi", "o_lo", "rr_in", "st_done"))
        y2_zero = sem("y2_zero")
        sq5, std5, fin, fin_out, prow1_in = sem("sq5"), sem("std5"), sem("fin"), sem("fin_out"), sem("prow1_in")

        def col(name, kt, n=1):
            c = 8 * VEC[name] + kt
            return PRM[:, c:c + n]

        def tokens(dram):
            return dram.rearrange("(t p) d -> p t d", p=P)

        def correction(b, ri, q, slot):
            seg = S[:, :, FB * b:FB * b + FB, :].rearrange("p r g (s j) -> p r g s j", j=SEG_CH)
            shape = [P, FB, SEG - 1, SEG_CH - 1]
            return (FIX[:, slot], seg[:, ri, :, 1:SEG, 0:SEG_CH - 1],
                    TAB[:, q, FB * b:FB * b + FB, 0:SEG_CH - 1].unsqueeze(2).to_broadcast(shape),
                    seg[:, ri ^ q, :, 0:SEG - 1, SEG_CH - 1:SEG_CH].to_broadcast(shape),
                    ALU.subtract if (ri, q) == (0, 1) else ALU.add)

        x_d = tokens(a["x"][0])
        ctx.enter_context(nc.allow_non_contiguous_dma(reason="small S5 tables, loaded once"))
        block = ctx.enter_context(nc.Block())

        @block.sync
        def _(sp):
            for t in range(TT):
                sp.dma_start(X[:, t, :], x_d[:, t, :]).then_inc(x_in[t], 16)
            sp.dma_start(PR[0:8, 0, :], a["norm_g"].rearrange("o (r p) -> (o r) p", p=P)).then_inc(prm_in, 16)
            rows = [("pool_b", 1), ("pool_scale", 1), ("conv_w", 3), ("conv_b", 1), ("norm_pre_2", 2), ("s5_b_glu_2", 1),
                    ("conv_b_2", 1), ("conv_ln_g_2", 1), ("conv_ln_b_2", 1), ("conv_b_pw_2", 1)]
            r0 = 8
            for name, n in rows:
                src = a[name][0] if name == "conv_w" else a[name]
                sp.dma_start(PR[r0:r0 + 8 * n, 0, :], src.rearrange("k (r p) -> (k r) p", p=P)).then_inc(prm_in, 16)
                r0 += 8 * n
            sp.dma_start(PR[r0:r0 + 4, 0, :], a["gla_norm_g_2"].rearrange("o (r p) -> (o r) p", p=P)).then_inc(prm_in, 16)
            taps = a["conv_w_2"][0].rearrange("k (r p) -> (k r) p", p=P)
            sp.dma_start(PR[:, 1, :], taps[0:P, :]).then_inc(prm_in, 16)
            sp.dma_start(PR[0:8 * CONV_K - P, 2, :], taps[P:8 * CONV_K, :]).then_inc(prm_in, 16)

            def halves_out(dst, src, which):
                for g in range(2):
                    half = slice(64 * g, 64 * g + 64)
                    sp.dma_start(dst[half, :, half], src(half)).then_inc(which, 16)

            def chunk(n, src, first=False):
                slot = n % RING
                if n >= RING:
                    sp.wait_ge(w_lo, n - RING + 1)
                sp.dma_start(WR[:, slot, :, :], src.rearrange("(k p) n -> p k n", p=P)).then_inc(w_loaded[slot], 16)

            def c_tables():
                for i, name in enumerate(("s5_c_re_2", "s5_c_im_2")):
                    src = a[name][0].rearrange("(t r g) p n -> r g p t n", r=8, g=2)
                    for r in range(8):
                        for g in range(2):
                            sp.dma_start(CRAW[16 * r:16 * r + 16, i, :, 64 * g:64 * g + 64], src[r, g]).then_inc(c_in, 16)

            def unit(name, src, col0):
                for q in range(4):
                    chunk(chunks_before(name) + q, src[q * 2 * P:(q + 1) * 2 * P, col0:col0 + NC])

            def section(name, src, col0, rows=D):
                n0 = chunks_before(name + ".0")
                per = rows // (2 * P)
                if n0 < RING:
                    for u in range(2):
                        if u:
                            c_tables()
                        for q in range(per):
                            chunk(n0 + u * per + q, src[q * 2 * P:(q + 1) * 2 * P, col0 + u * NC:col0 + (u + 1) * NC])
                    return
                with sp.Fori(0, 2) as u:
                    for q in range(per):
                        slot = q % RING
                        sp.wait_ge(w_lo, u * per + (n0 + q - RING + 1))
                        sp.dma_start(WR[:, slot, :, :],
                                     src[q * 2 * P:(q + 1) * 2 * P, bass.ds(u * NC + col0, NC)]
                                     .rearrange("(k p) n -> p k n", p=P)).then_inc(w_loaded[slot], 16)

            w_in, ev_in = a["w_in"][0], a["ev_w_in_2"][0]
            section("a_v", w_in, W_IN["a_v"])
            section("a_u", w_in, W_IN["a_u"])
            sp.wait_ge(zeroed, 1)
            for m in (d_wt[:, 0], d_wt[:, 1], d_g[:, 0], d_g[:, 1], d_tm):
                for g in range(2):
                    rows, cols = slice(64 * g, 64 * g + 64), slice(64 - 64 * g, P - 64 * g)
                    sp.dma_start(m[rows, :, cols],
                                 TMP[rows, 0, 0:64].unsqueeze(1).to_broadcast([64, PAIRS, 64])).then_inc(zeros_out, 16)
            section("a_z", w_in, W_IN["a_z"])
            section("g0", w_in, W_IN["g0"])
            sp.wait_ge(pool_g, 1)
            halves_out(d_g[:, 0], lambda h: GRE[h, :, 1:5, :].rearrange("p r t q -> p r (t q)"), s5_out)
            halves_out(d_g[:, 1], lambda h: GNI[h, :, 1:5, :].rearrange("p r t q -> p r (t q)"), s5_out)
            sp.wait_ge(banks_act, act_after("w_t.3"))
            sp.wait_ge(banks_dve, dve_after("w_t.3"))
            for ri in range(2):
                halves_out(d_wt[:, ri], lambda h: WTS[h, ri, :, :], s5_out)
            section("b_p", w_in, W_IN["b_p"])
            sp.wait_ge(lagged, 2)
            halves_out(d_tm, lambda h: TM[h, :, :], s5_out)
            sp.wait_ge(side_done, side_after("sgu.1"))
            sp.wait_ge(ya_ready, 8)
            sp.dma_start(PW[:, :, :, :], a["pool_w"][0].rearrange("g (k p) d -> p g k d", p=P)).then_inc(pw_in, 16)
            section("w_a", a["w_branch_a"][0], 0)
            section("b_z", w_in, W_IN["b_z"])
            section("g1", w_in, W_IN["g1"])
            sp.wait_ge(d_ready, 4)
            sp.wait_ge(s5_out, 16 * 10)
            sp.dma_start(X[:, :, :], x_d).then_inc(x_again, 16)
            section("c_h", w_in, W_IN["c_h"])
            sp.wait_ge(side_done, side_after("pool.1"))
            sp.dma_start(FROW[:, :], a["final_g"].rearrange("(o n) -> o n", o=1).broadcast_to([P, D])).then_inc(frow_in, 16)
            section("w_b", a["w_branch_b"][0], 0)
            for name in ("c_c", "g2", "c_b", "c_z"):
                section(name, w_in, W_IN[name])
            section("w_c", a["w_branch_c"][0], 0)
            section("w_out", a["w_out"][0], 0)
            unit("b_val.0", ev_in, EV_IN["b_val"])
            sp.wait_ge(x1_done, 4)
            sp.dma_start(tokens(d_x1), X[:, :, :]).then_inc(x1_out, 16)
            unit("b_gate.0", ev_in, EV_IN["b_gate"])
            sp.wait_ge(x1_out, 16)
            sp.wait_ge(xn1, 4)
            sp.wait_ge(zeros_out, 16 * 10)
            sp.wait_ge(m_acc, 16)
            for ri in range(2):
                sp.dma_start(WT[ri][:, :, :].rearrange("p r n -> p (r n)"), d_wt[:, ri].rearrange("p r n -> p (r n)")).then_inc(wt_in, 16)
            section("a_in", ev_in, EV_IN["a_in"])
            unit("b_val.1", ev_in, EV_IN["b_val"] + NC)
            unit("b_gate.1", ev_in, EV_IN["b_gate"] + NC)
            sp.wait_ge(side_done, side_after("s5_z.3"))

            def vt_in_half(i):
                sp.dma_start(VT[i][:, :, :, :].rearrange("p r g n -> p r (g n)"),
                             d_g[:, :, 16 * i:16 * i + 16, :].rearrange("p r g n -> p r (g n)")).then_inc(vt_in, 16)

            def t6_in_half(i):
                sp.dma_start(T6[i][:, :, :].rearrange("p g n -> p (g n)"),
                             d_tm[:, 16 * i:16 * i + 16, :].rearrange("p g n -> p (g n)")).then_inc(t6_in, 16)

            vt_in_half(0)
            t6_in_half(0)
            section("a_z2", ev_in, EV_IN["a_z2"])
            section("b_z2", ev_in, EV_IN["b_z2"])
            unit("glu.0", a["s5_w_glu_2"][0], 0)
            sp.wait_ge(weights_used, used_after("b_z2.1"))
            vt_in_half(1)
            t6_in_half(1)
            unit("glu.1", a["s5_w_glu_2"][0], NC)
            ev_out = a["ev_w_out_2"][0]
            section("ev_a", ev_out[0:D, :], 0)
            sp.wait_ge(sq_used, KT)
            sp.dma_start(X1[:, :, :], tokens(d_x1)).then_inc(x1_in, 16)
            sp.wait_ge(ya_gated, 8)
            sp.dma_start(LWR[:, :, :], a["od_w_in_2"][0][:, 6 * D:6 * D + LOWRANK].rearrange("(k p) n -> p k n", p=P)).then_inc(lw_in, 16)
            section("pw", a["conv_w_pw_2"][0], 0)
            section("ev_b", ev_out[D:2 * D, :], 0)
            sp.wait_ge(weights_used, used_after("pw.1"))
            sp.dma_start(PROW0[:, :], a["norm_post_2"][0:1, :].broadcast_to([P, D])).then_inc(prow0_in, 16)
            od_in, od_out = a["od_w_in_2"][0], a["od_w_out_2"][0]

            def head_chunk(n, j, pieces):
                sp.wait_ge(w_lo, n + (j - RING + 1))
                for c0, width, src in pieces:
                    sp.dma_start(WR[:, j % RING, :, c0:c0 + width],
                                 src.rearrange("(k p) n -> p k n", p=P)).then_inc(w_loaded[j % RING], 16)

            def in_rows(q, col, width):
                return od_in[q * 2 * P:(q + 1) * 2 * P, bass.ds(col, width)]

            def qk_in(n, h):
                for q in range(4):
                    head_chunk(n, q, [(0, HK, in_rows(q, h * HK, HK)), (HK, HK, in_rows(q, h * HK + HEADS * HK, HK))])

            def gu_rows(h):
                sp.dma_start(GU[0:LOWRANK, :], a["gla_w_gate_up_2"][0][:, bass.ds(h * HK, HK)]).then_inc(gu_in, 16)
                sp.dma_start(GU[LOWRANK:LOWRANK + 1, :], a["gla_b_gate_2"][0:1, bass.ds(h * HK, HK)]).then_inc(gu_in, 16)

            qk_in(N_STATIC, 0)
            gu_rows(0)

            def head(h, last):
                n = head_base(h)
                for q in range(4):
                    head_chunk(n, V_AT + q, [(0, HV, in_rows(q, h * HV + 2 * HEADS * HK, HV))])
                for q in range(4):
                    head_chunk(n, R_AT + q, [(0, HV, in_rows(q, h * HV + (2 * HEADS * HK + HEADS * HV), HV))])
                if not last:
                    sp.wait_ge(g_out, h + 1)
                    gu_rows(h + 1)
                    qk_in(n + QK_AT, h + 1)
                for u in range(2):
                    for q in range(2):
                        head_chunk(n, out_at(last) + 2 * u + q,
                                   [(0, NC, od_out[bass.ds(h * HV + q * 2 * P, 2 * P), u * NC:(u + 1) * NC])])

            with sp.Fori(0, HEADS - 1) as h:
                head(h, False)
            head(HEADS - 1, True)
            sp.wait_ge(ot_out, 4 * HEADS)
            sp.dma_start(PROW1[:, :], a["norm_post_2"][1:2, :].broadcast_to([P, D])).then_inc(prow1_in, 16)
            for t in range(TT):
                sp.wait_ge(fin, t + 1)
                sp.dma_start(tokens(out[0])[:, t, :], YO2[:, t, :]).then_inc(fin_out, 16)
            sp.wait_ge(fin_out, 16 * TT)

        @block.gpsimd
        def _(pool):
            seq = Order(pool, pool_seq)
            pool.memset(TMP[:, :, :], 0.0).then_inc(zeroed, 1)
            for i, name in enumerate(("s5_b_re_2", "s5_b_im_2")):
                pool.dma_start(BRAW[:, i, :, :], a[name][0].rearrange("(r g) n q -> (g n) r q", g=2)).then_inc(b_in, 16)
            seq.inc(pool.memset(ident[:, :], 0.0))
            seq.inc(pool.memset(MJ8[:, :, :], 1.0))
            pool.memset(EPS[:, 0:1], RMS_EPS).then_inc(consts, 1)
            pool.memset(EPS[:, 1:2], LN_EPS).then_inc(consts, 1)
            seq.wait()
            pool.affine_select(out=ident[:, :], in_=ident[:, :], compare_op=ALU.not_equal, fill=1.0, base=0,
                               pattern=[[-1, P]], channel_multiplier=1).then_inc(consts, 1)
            seq.inc(pool.affine_select(out=MJ8[:, :, :], in_=MJ8[:, :, :], compare_op=ALU.is_ge, fill=0.0, base=0,
                                       pattern=[[-64, 2], [-16, 4]], channel_multiplier=1))
            seq.wait()
            seq.inc(pool.affine_select(out=MJ8[:, :, :], in_=MJ8[:, :, :], compare_op=ALU.is_ge, fill=0.0, base=15,
                                       pattern=[[64, 2], [16, 4]], channel_multiplier=-1))
            seq.wait()
            pool.tensor_tensor(MJ[:, :], MJ8[:, 0, :], MJ8[:, 1, :], ALU.add).then_inc(consts, 1)
            for c in range(PPAD):
                pool.memset(INVC[:, c:c + 1], 1.0 / (c + 1)).then_inc(consts, 1)

            def tt(o, x, y, op):
                seq.wait()
                return seq.inc(pool.tensor_tensor(o, x, y, op))

            def ts(o, x, s1, s2, op0, op1):
                seq.wait()
                return seq.inc(pool.tensor_scalar(o, x, s1, s2, op0, op1))

            for g in range(2):
                for j in range(T4):
                    pool.dma_start(DCOL[64 * g + 16 * j:64 * g + 16 * j + 16, :],
                                   a["s5_d_2"][0].rearrange("(r g q) -> g q r", g=2, q=S5_GROUP)[g]).then_inc(d_in, 16)
            LRE, LIM, DTL, DT, RE, IM, K, RED, HALF, EX, SN, SH, LR_, LI_, NR, T1, T2, DEN, REC, F0 = range(20)
            l = [LS[:, i, :] for i in range(20)]
            F1 = K
            pool.wait_ge(lam_in, 64)
            pool.wait_ge(lam_exp, 1)
            tt(l[RE], l[LRE], l[DT], ALU.mult)
            tt(l[IM], l[LIM], l[DT], ALU.mult)
            tt(l[T1], l[LRE], l[LRE], ALU.mult)
            tt(l[T2], l[LIM], l[LIM], ALU.mult)
            tt(l[DEN], l[T1], l[T2], ALU.add)
            ts(l[K], l[IM], 1.0 / TWO_PI, ROUND, ALU.mult, ALU.add)
            ts(l[K], l[K], ROUND, -1.0, ALU.subtract, ALU.mult)
            seq.wait()
            pool.tensor_scalar(l[T1], l[K], PI_A, None, ALU.mult).then_inc(lam_den, 1)
            pool.wait_ge(lam_den, 1)
            tt(l[RED], l[IM], l[T1], ALU.add)
            ts(l[T2], l[K], PI_B, None, ALU.mult, ALU.bypass)
            tt(l[RED], l[RED], l[T2], ALU.add)
            ts(l[T1], l[K], PI_C, None, ALU.mult, ALU.bypass)
            tt(l[RED], l[RED], l[T1], ALU.add)
            ts(l[RED], l[RED], 3.1415925, -3.1415925, ALU.min, ALU.max)
            seq.wait()
            pool.tensor_scalar(l[HALF], l[RED], 0.5, None, ALU.mult).then_inc(lam_ang, 1)
            pool.wait_ge(lam_sin, 3)
            tt(l[T1], l[SH], l[SH], ALU.mult)
            tt(l[LI_], l[EX], l[SN], ALU.mult)
            ts(l[T1], l[T1], -2.0, 1.0, ALU.mult, ALU.add)
            tt(l[LR_], l[EX], l[T1], ALU.mult)
            ts(l[NR], l[LR_], -1.0, None, ALU.add, ALU.bypass)
            tt(l[T1], l[NR], l[LRE], ALU.mult)
            tt(l[T2], l[LI_], l[LIM], ALU.mult)
            tt(l[F0], l[T1], l[T2], ALU.add)
            tt(l[T1], l[LI_], l[LRE], ALU.mult)
            tt(l[T2], l[NR], l[LIM], ALU.mult)
            tt(l[F1], l[T1], l[T2], ALU.subtract)
            pool.wait_ge(lam_rec, 1)
            tt(l[F0], l[F0], l[REC], ALU.mult)
            tt(l[F1], l[F1], l[REC], ALU.mult)

            def wide(row):
                return row.unsqueeze(2).to_broadcast([P, PAIRS, S5_GROUP])

            pool.wait_ge(b_in, 32)
            pool.wait_ge(xn0, 4)
            P0, P1 = PT[:, 0, :, :], PT[:, 1, :, :]

            def cmul(ore, oim, xre, xim, yre, yim, signs=(ALU.subtract, ALU.add)):
                tt(P0, xre, yre, ALU.mult)
                tt(P1, xim, yim, ALU.mult)
                tt(ore, P0, P1, signs[0])
                tt(P0, xim, yre, ALU.mult)
                tt(P1, xre, yim, ALU.mult)
                tt(oim, P0, P1, signs[1])

            cmul(WST[:, 0, :, 3, :], WST[:, 1, :, 3, :], BRAW[:, 0, :, :], BRAW[:, 1, :, :], wide(l[F0]), wide(l[F1]))
            for j in (2, 1, 0):
                cmul(WST[:, 0, :, j, :], WST[:, 1, :, j, :], WST[:, 0, :, j + 1, :], WST[:, 1, :, j + 1, :],
                     wide(l[LR_]), wide(l[LI_]))
            seq.wait()
            pool.memset(MJ8[:, 0, 0:1], 0.0).then_inc(pool_w, 1)
            tt(l[T1], l[LR_], l[LR_], ALU.mult)
            tt(l[T2], l[LI_], l[LI_], ALU.mult)
            tt(l[NR], l[LR_], l[LI_], ALU.mult)
            tt(l[T1], l[T1], l[T2], ALU.subtract)
            ts(l[NR], l[NR], 2.0, None, ALU.mult, ALU.bypass)
            tt(l[T2], l[T1], l[T1], ALU.mult)
            tt(l[DEN], l[NR], l[NR], ALU.mult)
            tt(l[IM], l[T1], l[NR], ALU.mult)
            tt(LAM[:, 0, :], l[T2], l[DEN], ALU.subtract)
            ts(LAM[:, 1, :], l[IM], 2.0, None, ALU.mult, ALU.bypass)
            ts(LAM[:, 2, :], l[IM], -2.0, None, ALU.mult, ALU.bypass)
            pool.wait_ge(banks_act, act_after("c_t"))
            for k in range(4):
                cmul(GRE[:, :, k + 1, :], GNI[:, :, k + 1, :], GRE[:, :, k, :], GNI[:, :, k, :],
                     wide(l[LR_]), wide(l[LI_]), signs=(ALU.add, ALU.subtract))
            seq.wait()
            pool.memset(MJ8[:, 0, 1:2], 0.0).then_inc(pool_g, 1)
            pool.wait_ge(d_in, 128)
            pool.wait_ge(consts, 3)

            def dcol():
                return DCOL[:, :].unsqueeze(2).to_broadcast([P, PAIRS, 64])

            def eye(half):
                return ident[:, 64 * half:64 * half + 64].unsqueeze(1).to_broadcast([P, PAIRS, 64])

            tt(TM[:, :, :], dcol(), eye(0), ALU.mult)
            tt(DT2[:, :, :], dcol(), eye(1), ALU.mult)
            seq.wait()
            pool.tensor_tensor(TM[:, :, :], TM[:, :, :], DT2[:, :, :], ALU.add).then_inc(pool_t, 1)
            pool.wait_ge(sg_in, 16)
            pool.memset(SGW[0:CHUNK, :, CHUNK:P], 0.0).then_inc(sgw_masked, 1)
            pool.wait_ge(side_done, side_after("w_t.3"))
            for ri in range(2):
                pool.tensor_copy(WST[:, ri, :, 0:T4 - 1, :],
                                 WST[:, ri, :, T4 - 1:T4, :].to_broadcast([P, PAIRS, T4 - 1, S5_GROUP])).then_inc(pool_rep, 1)
            pool.wait_ge(side_done, side_after("sgu.1"))
            pool.memset(CH[:, :, 0:PPAD], 0.0).then_inc(pads, 1)
            pool.wait_ge(s5_out, 16 * 10)
            pool.memset(WIN[:, :, 0:PPAD], 0.0).then_inc(pads, 1)
            pool.wait_ge(tmp_free, 16)
            pool.memset(CP[:, :, 0:CPAD], 0.0).then_inc(cpads, 1)
            pool.wait_ge(weights_used, used_after("w_c.1"))
            pool.memset(S[:, :, :, 0:1], 0.0).then_inc(states, 1)
            pool.wait_ge(m_acc, 16)
            pool.wait_ge(x1_done, 4)
            for i in range(2):
                seq.wait()
                seq.inc(pool.tensor_copy(TAB[:, i, :, 0:1], LAM[:, i, :].unsqueeze(2)))
            n = 1
            while n < SEG_CH:
                by = [TAB[:, i, :, n - 1:n].to_broadcast([P, PAIRS, n]) for i in range(2)]
                x = [TAB[:, i, :, 0:n] for i in range(2)]
                q0, q1 = Q0[:, 0, :, 0:n], Q0[:, 1, :, 0:n]
                for i, (y0, y1, op) in enumerate(((by[0], by[1], ALU.subtract), (by[1], by[0], ALU.add))):
                    tt(q0, x[0], y0, ALU.mult)
                    tt(q1, x[1], y1, ALU.mult)
                    tt(TAB[:, i, :, n:2 * n], q0, q1, op)
                n *= 2
            for i in range(2):
                ts(LAM64[:, i, :].unsqueeze(2), TAB[:, i, :, SEG_CH - 1:SEG_CH], 1.0, None, ALU.mult, ALU.bypass)
            ts(LAM64[:, 2, :].unsqueeze(2), TAB[:, 1, :, SEG_CH - 1:SEG_CH], -1.0, None, ALU.mult, ALU.bypass)
            seq.wait()
            pool.wait_ge(banks_act, act_after("s5_z.3"))
            SV = S[:, :, :, :].rearrange("p r g (s j) -> p r g s j", j=SEG_CH)
            per_step = 4
            first = seq.n

            def chunk_of(v, j):
                return v[:, :, :, :, bass.ds(j, 1)].rearrange("p r g s j -> p r g (s j)")

            with pool.Fori(0, SEG_CH - 1) as j:
                seq.base, seq.n = j * per_step, first
                now, nxt = chunk_of(SV[:, :, 0:PP], j), chunk_of(SV[:, :, 0:PP], j + 1)
                nre, nim = chunk_of(SV[:, 0:1, 0:PP], j + 1), chunk_of(SV[:, 1:2, 0:PP], j + 1)
                pool.wait_ge(states, j + 1)
                seq.inc(pool.tensor_tensor(SEG1[:, :, 0:PP, :], LAM[:, 0:1, 0:PP].unsqueeze(3).to_broadcast([P, 2, PP, SEG]), now, ALU.mult))
                seq.inc(pool.tensor_tensor(SEG2[:, :, 0:PP, :], LAM[:, 1:3, 0:PP].unsqueeze(3).to_broadcast([P, 2, PP, SEG]), now, ALU.mult))
                seq.wait()
                seq.inc(pool.tensor_tensor(nxt, nxt, SEG1[:, :, 0:PP, :], ALU.add))
                seq.wait()
                seq.inc(pool.tensor_tensor(nim, nim, SEG2[:, 0:1, 0:PP, :], ALU.add))
                pool.tensor_tensor(nre, nre, SEG2[:, 1:2, 0:PP, :], ALU.add).then_inc(states, 1)
                assert seq.n - first == per_step
            seq.base, seq.n = 0, first + per_step * (SEG_CH - 1)
            pool.wait_ge(states, SEG_CH)
            pool.wait_ge(dve_states, 1)
            for g in range(1, SEG):
                now, nxt = [S[:, :, :, SEG_CH * k - 1:SEG_CH * k] for k in (g, g + 1)]
                tt(ST1[:, :, :].unsqueeze(3), LAM64[:, 0:1, :].to_broadcast([P, 2, PAIRS]).unsqueeze(3), now, ALU.mult)
                tt(ST2[:, :, :].unsqueeze(3), LAM64[:, 1:3, :].unsqueeze(3), now, ALU.mult)
                tt(nxt, nxt, ST1[:, :, :].unsqueeze(3), ALU.add)
                tt(nxt[:, 1:2], nxt[:, 1:2], ST2[:, 0:1, :].unsqueeze(3), ALU.add)
                seq.wait()
                o = pool.tensor_tensor(nxt[:, 0:1], nxt[:, 0:1], ST2[:, 1:2, :].unsqueeze(3), ALU.add)
                if g < SEG - 1:
                    seq.inc(o)
                else:
                    o.then_inc(carried, 1)
            pool.wait_ge(carried, 1)
            for n, (b, ri) in enumerate(FIX_POOL):
                for q in range(2):
                    fix, into, by, end, op = correction(b, ri, q, 0)
                    tt(fix, by, end, ALU.mult)
                    seq.wait()
                    o = pool.tensor_tensor(into, into, fix, op)
                    if q and n in (FIX_HALF - 1, len(FIX_POOL) - 1):
                        o.then_inc(fixed_pool, 1)
                        pool.wait_ge(fixed_pool, 1 + (n > FIX_HALF))
                    else:
                        seq.inc(o)
            pool.wait_ge(banks_act, act_after("a_z2.1"))
            for kt in range(KT):
                pool.wait_ge(y_lo, 24 + kt + 1)
                pool.tensor_tensor(YA[:, kt, :], YA[:, kt, :], AZ[:, kt, :], ALU.mult).then_inc(ya_gated, 1)
            pool.wait_ge(sq_used, KT)
            pool.wait_ge(z_norm, KT)
            pool.wait_ge(tmp_free, 32)
            seq.inc(pool.memset(CMASK[:, :], 1.0))
            seq.inc(pool.memset(ATS[:, :, :], 0.0))
            seq.inc(pool.memset(SMASK[:, :], 1.0))
            seq.inc(pool.memset(LR[0:32, :], 1.0))
            seq.wait()
            seq.inc(pool.affine_select(out=CMASK[:, :], in_=CMASK[:, :], compare_op=ALU.is_ge, fill=0.0, base=0,
                                       pattern=[[1, P]], channel_multiplier=-1))
            seq.inc(pool.memset(SMASK[:, :].rearrange("p (c t) -> p c t", t=CHUNK)[:, :, 0:1], 0.0))
            seq.wait()
            pool.memset(CMASK[0:CHUNK, CHUNK:P], 0.0).then_inc(gla_consts, 1)
            pool.memset(MJ8[:, 0, 2:3], 0.0).then_inc(y2_add, 8)
            pool.wait_ge(xn2, 4)
            pool.memset(YO2[:, :, :], 0.0).then_inc(y2_zero, 1)

        @block.scalar
        def _(act):
            seq = Order(act, act_seq)
            state = {"chunk": 0, "hi": 0}

            lam = LS
            act.dma_start(lam[:, 0, :], a["s5_lambda_re_2"][0].rearrange("(r g) n -> (g n) r", g=2)).then_inc(lam_in, 16)
            act.dma_start(lam[:, 1, :], a["s5_lambda_im_2"][0].rearrange("(r g) n -> (g n) r", g=2)).then_inc(lam_in, 16)
            for g in range(2):
                act.dma_start(lam[64 * g:64 * g + 64, 2, :],
                              a["s5_log_dt_2"].rearrange("o (r g) -> g o r", g=2)[g].broadcast_to([64, PAIRS])).then_inc(lam_in, 16)
            def split(count=4):
                for n in range(state["chunk"], min(state["chunk"] + count, N_STATIC)):
                    act.wait_ge(w_loaded[n % RING], 16 * (n // RING + 1))
                    if n >= RING:
                        act.wait_ge(weights_used, n - RING + 1)
                    act.activation(WH[:, n % RING, :, :], WR[:, n % RING, :, :], ACT.Copy).then_inc(w_hi, 1)
                state["chunk"] = min(state["chunk"] + count, N_STATIC)

            def rms_tile(x, t, junk, sq, std):
                act.activation(junk, x, ACT.Square, accum_out=STAT[:, 0, t:t + 1]).then_inc(sq, 1)
                act.wait_ge(sq, t + 1)
                act.activation(STAT[:, 1, t:t + 1], STAT[:, 0, t:t + 1], ACT.Sqrt, scale=1.0 / D, bias=EPS[:, 0:1]).then_inc(std, 1)

            def load_sqrt():
                act.activation(BNA[:, 0, 0:1], EPS[:, 0:1], ACT.Sqrt)

            def turned(job, kt0, vec):
                for m in range(4):
                    act.wait_ge(side_done, side_after(job, m + 1))
                    act.activation(HH[:, kt0 + m, :], bank(job, m), ACT.Copy, scale=col(vec, kt0 + m)).then_inc(h_hi, 1)

            def hsplit(n, j0, count, value):
                for j in range(j0, j0 + count):
                    act.wait_ge(w_loaded[j % RING], value)
                    act.wait_ge(weights_used, n + (j - RING + 1))
                    act.activation(WH[:, j % RING, :, :], WR[:, j % RING, :, :], ACT.Copy).then_inc(w_hi, 1)

            def evac(job, outs, func, waits=None, inc=banks_act, **kw):
                act.wait_ge(weights_used if job in UNITS else side_done,
                            used_after(job) if job in UNITS else side_after(job))
                for m, o in enumerate(outs):
                    if waits:
                        waits(m)
                    extra = {k: v(m) for k, v in kw.items()}
                    act.activation(o, bank(job, m), func, **extra).then_inc(inc, 1)

            def via_tmp(job, func, to=TMP, **kw):
                act.wait_ge(weights_used, used_after(job))
                for m in range(4):
                    if state["hi"] >= 2:
                        act.wait_ge(tmp_free, state["hi"] - 1)
                    extra = {k: v(m) for k, v in kw.items()}
                    act.activation(to[:, state["hi"] % 2, :], bank(job, m), func, **extra).then_inc(banks_act, 1)
                    state["hi"] += 1

            def y_halves(ready, count, src, kts):
                for kt in kts:
                    act.wait_ge(ready, count(kt))
                    act.activation(YH[:, kt, :], src(kt), ACT.Copy).then_inc(y_hi, 1)

            act.wait_ge(consts, 2)
            for t in range(TT):
                act.wait_ge(x_in[t], 16)
                rms_tile(X[:, t, :], t, XN0[:, t, :], sq0, std0)
            act.wait_ge(side_done, side_after("params"))
            for i, n in enumerate((116, 128, 120)):
                act.activation(PRM[:, 128 * i:128 * i + n], bank("params", i)[:, 0:n], ACT.Copy).then_inc(banks_act, 1)
            act.wait_ge(banks_act, act_after("params"))
            turned("h_t.0", 0, "norm_g")
            split(2)
            turned("h_t.1", 4, "norm_g")
            split(2)
            for i, name in enumerate(("sgu_ln_g", "sgu_ln_b")):
                act.dma_start(LNROWS[:, i, :], a[name].broadcast_to([P, D])).then_inc(ln_in, 16)
            act.dma_start(SGW[:, :, :], a["sgu_w"][0].rearrange("g i j -> i g j")).then_inc(sg_in, 16)
            act.dma_start(SGB[:, :, :].rearrange("p g i -> p (g i)"),
                          a["sgu_b"].rearrange("o g i -> o (g i)").broadcast_to([P, D])).then_inc(bs_in, 16)
            act.wait_ge(lam_in, 64)
            act.activation(LS[:, 3, :], LS[:, 2, :], ACT.Exp).then_inc(lam_exp, 1)
            act.wait_ge(lam_ang, 1)
            act.activation(LS[:, 9, :], LS[:, 4, :], ACT.Exp).then_inc(lam_sin, 1)
            act.activation(LS[:, 10, :], LS[:, 7, :], ACT.Sin).then_inc(lam_sin, 1)
            act.activation(LS[:, 11, :], LS[:, 8, :], ACT.Sin).then_inc(lam_sin, 1)

            def v_free(m):
                act.wait_ge(side_done, side_after("h_t.1"))

            split()
            evac("a_v.0", [V[:, m, 0:NC] for m in range(4)], ACT.Gelu_apprx_tanh, waits=v_free)
            split()
            evac("a_v.1", [V[:, m, NC:D] for m in range(4)], ACT.Gelu_apprx_tanh)
            act.wait_ge(side_done, side_after("c_t"))
            act.activation(GRE[:, :, 0, :], bank("c_t", 0).rearrange("p (r q) -> p r q", q=S5_GROUP), ACT.Copy).then_inc(banks_act, 1)
            act.activation(GNI[:, :, 0, :], bank("c_t", 1).rearrange("p (r q) -> p r q", q=S5_GROUP), ACT.Copy,
                           scale=-1.0).then_inc(banks_act, 1)
            split()
            evac("a_u.0", [U[:, m, :] for m in range(4)], ACT.Gelu_apprx_tanh)
            split()
            evac("a_u.1", [U[:, 4 + m, :] for m in range(4)], ACT.Gelu_apprx_tanh)
            act.wait_ge(v_std, 4)
            act.activation(STAT[:, 2, :], BNA[:, :, 1], ACT.Sqrt, bias=EPS[:, 1:2]).then_inc(v_std, 1)
            split()
            act.wait_ge(zeros_out, 16 * 10)
            via_tmp("a_z.0", ACT.Silu)
            split()
            via_tmp("a_z.1", ACT.Silu)
            act.wait_ge(pool_t, 1)
            for i in range(4):
                act.wait_ge(side_done, side_after(f"w_t.{i}"))
                for ri in range(2):
                    act.activation(WTS[0:64, ri, 8 * i:8 * i + 8, :],
                                   bank(f"w_t.{i}", 2 * ri)[0:64, :].rearrange("p (r n) -> p r n", r=8),
                                   ACT.Copy).then_inc(banks_act, 1)
            for m in range(2):
                if not m:
                    act.wait_ge(side_done, side_after("sgu_t"))
                act.activation(SGWT[:, 4 * m:4 * m + 4, :], bank("sgu_t", m).rearrange("p (g i) -> p g i", g=4),
                               ACT.Copy).then_inc(banks_act, 1)
            split()
            act.wait_ge(v_done, 4)
            evac("g0.0", [G[:, m, :] for m in range(4)], ACT.Sigmoid)
            split()
            evac("g0.1", [G[:, 4 + m, :] for m in range(4)], ACT.Sigmoid)
            for i in range(2):
                act.wait_ge(side_done, side_after(f"k.{i}"))
                if i:
                    act.wait_ge(lagged, 1)
                for m in range(4):
                    half, r0 = slice(64 * (m % 2), 64 * (m % 2) + 64), 8 * (m // 2)
                    act.activation(KS[half, r0:r0 + 8, :, :], bank(f"k.{i}", m)[half, :].rearrange("p (r l q) -> p r l q", r=8, l=T4),
                                   ACT.Copy).then_inc(banks_act, 1)
            act.wait_ge(s5_out, 16 * 10)
            y_halves(ya_ready, lambda kt: kt + 1, lambda kt: U[:, kt, :], range(8))
            split()
            act.wait_ge(pads, 1)
            evac("b_p.0", [CH[:, m, PPAD:] for m in range(4)], ACT.Copy)
            split()
            evac("b_p.1", [CH[:, 4 + m, PPAD:] for m in range(4)], ACT.Copy)
            split()
            split()
            split()
            act.wait_ge(d_ready, 4)
            evac("b_z.0", [CH[:, m, PPAD:] for m in range(4)], ACT.Silu)
            split()
            evac("b_z.1", [CH[:, 4 + m, PPAD:] for m in range(4)], ACT.Silu)
            act.wait_ge(weights_used, used_after("w_a.1"))
            y_halves(yb_ready, lambda kt: kt + 1, lambda kt: CH[:, kt, PPAD:], range(8))
            split()
            act.wait_ge(banks_dve, dve_after("w_a.1"))
            evac("g1.0", [G[:, m, :] for m in range(4)], ACT.Sigmoid)
            split()
            evac("g1.1", [G[:, 4 + m, :] for m in range(4)], ACT.Sigmoid)
            split()
            act.wait_ge(y_lo, 16)
            evac("c_h.0", [CH[:, m, PPAD:] for m in range(4)], ACT.Copy)
            split()
            evac("c_h.1", [CH[:, 4 + m, PPAD:] for m in range(4)], ACT.Copy)
            split()
            split()
            split()
            split()
            split()
            act.wait_ge(banks_dve, dve_after("w_b.1"))
            evac("g2.0", [G[:, m, :] for m in range(4)], ACT.Sigmoid)
            split()
            evac("g2.1", [G[:, 4 + m, :] for m in range(4)], ACT.Sigmoid)
            split()
            split()
            split()
            act.wait_ge(weights_used, used_after("w_b.1"))
            act.wait_ge(banks_dve, dve_after("c_b.1"))
            via_tmp("c_z.0", ACT.Silu)
            y_halves(tmp_free, lambda kt: 8 + kt + 1, lambda kt: U[:, kt, :], range(4))
            split()
            via_tmp("c_z.1", ACT.Silu)
            y_halves(tmp_free, lambda kt: 8 + kt + 1, lambda kt: U[:, kt, :], range(4, 8))
            split()
            act.wait_ge(weights_used, used_after("c_z.1"))
            for u in range(2):
                for kt in range(4 * u, 4 * u + 4):
                    act.wait_ge(m_acc, 8 + kt + 1)
                    act.activation(HH[:, kt, :], M[:, kt, :], ACT.Copy).then_inc(h_hi, 1)
                split()

            load_sqrt()
            act.wait_ge(h_lo, 16)
            for t in range(TT):
                act.wait_ge(banks_dve, dve_after("w_out.1", t + 1))
                rms_tile(X[:, t, :], t, XN1[:, t, :], sq1, std1)
                if t == TT - 1:
                    split(1)
                act.wait_ge(x1_done, t + 1)
                rms_tile(X[:, t, :], t, XN1[:, t, :], sq2, std2)
            split(1)
            turned("u_t.0", 0, "norm_pre0")
            split(2)
            turned("u_t.1", 4, "norm_pre0")

            split()
            act.wait_ge(cpads, 1)
            evac("b_val.0", [CP[:, m, CPAD:] for m in range(4)], ACT.Copy)
            split()
            via_tmp("b_gate.0", ACT.Sigmoid, GATEV)
            for u in range(2):
                split()
                act.wait_ge(weights_used, used_after(f"a_in.{u}"))
                if u == 0:
                    act.wait_ge(tmp_free, 20)
                for j in range(T4):
                    act.activation(AS[:, u, :, j, :], bank(f"a_in.{u}", j).rearrange("p (g q) -> p g q", q=S5_GROUP),
                                   ACT.Copy).then_inc(banks_act, 1)
            for u in range(2):
                evac(f"s5_t.{u}", [UT[:, 16 * u + 4 * m:16 * u + 4 * m + 4, :].rearrange("p r c -> p (r c)")
                                   for m in range(4)], ACT.Copy)
            for i in range(4):
                act.wait_ge(side_done, side_after(f"s5_z.{i}"))
                for m in range(4):
                    r0 = 8 * i + 4 * (m % 2)
                    act.activation(S[:, m // 2, r0:r0 + 4, 1:NCH],
                                   bank(f"s5_z.{i}", m).rearrange("p (r c) -> p r c", c=NCH)[:, :, 0:NCH - 1],
                                   ACT.Copy).then_inc(banks_act, 1)
            split()
            evac("b_val.1", [CP[:, 4 + m, CPAD:] for m in range(4)], ACT.Copy)
            split()
            via_tmp("b_gate.1", ACT.Sigmoid, GATEV)
            split()
            act.wait_ge(tmp_free, 24)
            evac("a_z2.0", [AZ[:, m, :] for m in range(4)], ACT.Silu)
            split()
            evac("a_z2.1", [AZ[:, 4 + m, :] for m in range(4)], ACT.Silu)
            split()
            split()
            act.wait_ge(carried, 1)
            evac("b_z2.0", [BZ[:, m, :] for m in range(4)], ACT.Silu)
            for m in range(4):
                act.wait_ge(side_done, side_after("s5_y.0", m + 1))
                act.activation(BZ[:, 4 + m, :], bank("b_z2.1", m), ACT.Silu).then_inc(banks_act, 1)
            for i in range(2):
                for m in range(4):
                    act.wait_ge(side_done, side_after(f"s5_y.{i}", m + 1) if i else side_after("s5_y.0"))
                    kt = 4 * i + m
                    dst = YT[:, :, kt * P:(kt + 1) * P].rearrange("c t (x q) -> c x t q", q=S5_GROUP)
                    act.activation(dst, bank(f"s5_y.{i}", m).rearrange("p (x t q) -> p x t q", x=8, t=T4),
                                   ACT.Gelu_apprx_tanh).then_inc(banks_act, 1)
            for i in range(2):
                for m in range(4):
                    act.wait_ge(side_done, side_after(f"y_t.{i}", m + 1))
                    src = bank(f"y_t.{i}", m).rearrange("p (t c) -> p t c", t=T4)
                    act.activation(YH[:, 4 * i + m, :].rearrange("p (c t) -> p t c", t=T4), src, ACT.Copy).then_inc(y_hi, 1)
                    act.activation(YA[:, 4 * i + m, :].rearrange("p (c t) -> p t c", t=T4), src, ACT.Copy).then_inc(banks_act, 1)

            def ya_halves(kts):
                for kt in kts:
                    act.wait_ge(tmp_free, 24 + kt + 1)
                    act.activation(HH[:, kt, :], YA[:, kt, :], ACT.Copy).then_inc(h_hi, 1)

            split()
            via_tmp("glu.0", ACT.Sigmoid, GLUV, bias=lambda m: col("b_glu", m))
            split()
            ya_halves(range(4))
            via_tmp("glu.1", ACT.Sigmoid, GLUV, bias=lambda m: col("b_glu", 4 + m))
            ya_halves(range(4, 8))
            for kt in range(KT):
                act.wait_ge(z_cent, kt + 1)
                act.activation(SQ[:, kt, :], CP[:, kt, CPAD:], ACT.Square).then_inc(z_sq, 1)
            split()
            act.wait_ge(h_lo, 32)
            evac("ev_a.0", [YO[:, m, 0:NC] for m in range(4)], ACT.Copy)
            act.wait_ge(sq_used, KT)
            act.activation(RS[:, :], bank("var", 0), ACT.Sqrt, bias=EPS[:, 0:1]).then_inc(banks_act, 1)
            for kt in range(KT):
                act.wait_ge(z_norm, kt + 1)
                act.activation(CP[:, kt, CPAD:], CP[:, kt, CPAD:], ACT.Silu, scale=col("ln_g2", kt),
                               bias=col("ln_b2", kt)).then_inc(z_act, 1)
                act.wait_ge(z_act, kt + 1)
                act.activation(YH[:, kt, :], CP[:, kt, CPAD:], ACT.Copy).then_inc(y_hi, 1)
            split()
            evac("ev_a.1", [YO[:, m, NC:D] for m in range(4)], ACT.Copy)
            split()
            for u in range(2):
                if u:
                    split()
                for m in range(4):
                    kt = 4 * u + m
                    act.wait_ge(banks_dve, dve_after(f"pw.{u}", m + 1))
                    act.activation(HH[:, kt, :], BZ[:, kt, :], ACT.Copy).then_inc(h_hi, 1)
            split()
            load_sqrt()
            act.wait_ge(h_lo, 40)
            w0 = 16 * (N_STATIC // RING) + 32
            for t in range(TT):
                act.wait_ge(banks_dve, dve_after("ev_b.1", t + 1))
                rms_tile(YO[:, t, :], t, XN2[:, t, :], sq3, std3)
                if t == TT - 1:
                    hsplit(N_STATIC, 0, 1, w0)
                act.wait_ge(x2_done, t + 1)
                rms_tile(X1[:, t, :], t, XN2[:, t, :], sq4, std4)
            hsplit(N_STATIC, 1, 1, w0)
            turned("u2_t.0", 0, "norm_pre1")
            hsplit(N_STATIC, 2, 1, w0)
            turned("u2_t.1", 4, "norm_pre1")
            hsplit(N_STATIC, 3, 1, w0)

            act.wait_ge(lw_in, 16)
            act.wait_ge(lw_zero, 2)
            act.activation(LWH[:, :, 0:LOWRANK], LWR[:, :, :], ACT.Copy).then_inc(lw_hi, 1)
            act.wait_ge(gla_consts, 1)
            act.wait_ge(lr_out, 1)
            act.activation(LR[0:LOWRANK, :], PS[0:LOWRANK, 0, :], ACT.Copy).then_inc(banks_act, 1)

            A, B = [PS[:, m, :] for m in range(4)], [PS[:, 4 + m, :] for m in range(4)]

            def qk_out(n, banks):
                act.wait_ge(weights_used, n)
                for m in range(4):
                    act.activation(QK[:, m, :], banks[m], ACT.Copy).then_inc(qk_copied, 1)

            qk_out(N_STATIC + 4, B)
            junk = [KE[:, 0, :], KE[:, 1, :], QD[:, 0, :], QD[:, 1, :]]

            def head(h, last):
                n = head_base(h)
                seq.base, seq.n = h * HSEQ_ACT, 0
                hsplit(n, V_AT, 4, loaded(h, V_AT))
                act.wait_ge(g_out, h + 1)
                for m in range(2):
                    seq.inc(act.activation(ET[:, m, :], B[m], ACT.Abs))
                for m in range(2):
                    seq.wait(m + 1)
                    seq.inc(act.activation(ET[:, m, :], ET[:, m, :], ACT.Exp, scale=-1.0))
                for m in range(2):
                    seq.wait(m + 3)
                    act.activation(ET[:, m, :], ET[:, m, :], ACT.Ln, bias=1.0).then_inc(e_abs, 1)
                act.wait_ge(g_scan, h * 2 + 1)
                act.activation(ET[:, :, :], BC[:, :, :], ACT.Exp, scale=1.0 / GLA_TAU).then_inc(e_q, 1)
                act.activation(DEC[:, :, :], BC[:, :, :].rearrange("p k (c t) -> p k c t", t=CHUNK)[:, :, :, CHUNK - 1],
                               ACT.Exp, scale=1.0 / GLA_TAU).then_inc(dec_in, 1)
                act.wait_ge(qd_done, h + 1)
                act.activation(ET[:, :, :], BC[:, :, :], ACT.Exp, scale=-1.0 / GLA_TAU).then_inc(e_ke, 1)
                act.wait_ge(g_scan, h * 2 + 2)
                act.wait_ge(ke_done, h + 1)
                act.activation(ET[:, :, :], KX[:, :, :], ACT.Exp, scale=1.0 / GLA_TAU).then_inc(e_d, 1)
                hsplit(n, R_AT, 4, loaded(h, R_AT))
                act.wait_ge(weights_used, n + 4)
                for m in range(4):
                    act.activation(V2[:, m, :], A[m], ACT.Copy).then_inc(v_copied, 1)
                seq.inc(act.activation(STAT[:, 2, 0:1], EPS[:, 0:1], ACT.Silu))
                hsplit(n, QK_AT, 3, loaded(h, QK_AT, last))
                act.wait_ge(weights_used, n + 8)
                for m in range(4):
                    act.activation(RR[:, m, :], B[m], ACT.Silu).then_inc(r_copied, 1)
                act.wait_ge(kt_out, h + 1)
                for m in range(2):
                    act.activation(KTK[:, 2 * m:2 * m + 2, :, :].rearrange("p t k n -> p (t k n)"),
                                   A[m], ACT.Copy).then_inc(kt_copied, 1)
                seq.wait(5)
                seq.inc(act.activation(STAT[:, 2, 0:1], EPS[:, 0:1], ACT.Sqrt))
                hsplit(n, QK_AT + 3, 1, loaded(h, QK_AT, last))
                for m in range(4):
                    act.wait_ge(o_out, h * 4 + (m + 1))
                    act.activation(junk[m], A[m], ACT.Square, accum_out=STAT[:, 0, m:m + 1]).then_inc(o_sq, 1)
                act.wait_ge(o_sq, h * 4 + 4)
                act.activation(STAT[:, 1, :], STAT[:, 0, :], ACT.Sqrt, scale=1.0 / HV, bias=EPS[:, 0:1]).then_inc(o_std, 1)
                if not last:
                    hsplit(n, out_at(last), 2, loaded(h, out_at(last)))
                for m in range(4):
                    act.wait_ge(o_f, h * 4 + (m + 1))
                    act.activation(OH[:, m, :], RR[:, m, :], ACT.Copy).then_inc(o_hi, 1)
                if not last:
                    qk_out(n + 12, B)
                    hsplit(n, out_at(last) + 2, 2, loaded(h, out_at(last)))

            with act.Fori(0, HEADS - 1) as h:
                head(h, False)
            head(HEADS - 1, True)

            for t in range(TT):
                act.wait_ge(y2_add, 8 * HEADS + 4 + t + 1)
                rms_tile(YO2[:, t, :], t, XN2[:, t, :], sq5, std5)

        @block.vector
        def _(dve):
            seq = Order(dve, dve_seq)
            state = {"chunk": 0, "via": 0}

            def split(count=4):
                for n in range(state["chunk"], min(state["chunk"] + count, N_STATIC)):
                    s = n % RING
                    dve.wait_ge(w_hi, n + 1)
                    dve.tensor_tensor(WL[:, s, :, :], WR[:, s, :, :], WH[:, s, :, :].bitcast(F32),
                                      ALU.subtract).then_inc(w_lo, 1)
                state["chunk"] = min(state["chunk"] + count, N_STATIC)

            def done(job):
                dve.wait_ge(weights_used if job in UNITS else side_done,
                            used_after(job) if job in UNITS else side_after(job))

            def tile_done(job, t, n0):
                if t < TT - 1:
                    dve.wait_ge(tiles_done, n0 + t + 1)
                else:
                    dve.wait_ge(weights_used, used_after(job))

            def rstd_tile(t):
                seq.inc(dve.reciprocal(STAT[:, 3, t:t + 1], STAT[:, 1, t:t + 1]))
                seq.wait()

            def turned(job, kt0, vec, version):
                for m in range(4):
                    kt = kt0 + m
                    dve.wait_ge(h_hi, 8 * version + kt + 1)
                    dve.scalar_tensor_tensor(HL[:, kt, :], bank(job, m), col(vec, kt), HH[:, kt, :].bitcast(F32),
                                             ALU.mult, ALU.subtract).then_inc(h_lo, 1)

            def hsplit(n, j0, count):
                for j in range(j0, j0 + count):
                    s = j % RING
                    dve.wait_ge(w_hi, n + (j + 1))
                    dve.tensor_tensor(WL[:, s, :, :], WR[:, s, :, :], WH[:, s, :, :].bitcast(F32),
                                      ALU.subtract).then_inc(w_lo, 1)

            def y_low(version, src, kts):
                for kt in kts:
                    dve.wait_ge(y_hi, 8 * version + kt + 1)
                    dve.tensor_tensor(YL[:, kt, :], src(kt), YH[:, kt, :].bitcast(F32), ALU.subtract).then_inc(y_lo, 1)

            def h_low(version, src, kts):
                for kt in kts:
                    dve.wait_ge(h_hi, 8 * version + kt + 1)
                    dve.tensor_tensor(HL[:, kt, :], src(kt), HH[:, kt, :].bitcast(F32), ALU.subtract).then_inc(h_lo, 1)

            def times_tmp(dsts, src=TMP):
                for i, (job, m, d) in enumerate(dsts):
                    dve.wait_ge(banks_act, act_after(job, m + 1))
                    dve.tensor_tensor(d, d, src[:, state["via"] % 2, :], ALU.mult).then_inc(tmp_free, 1)
                    state["via"] += 1

            for t in range(TT):
                dve.wait_ge(std0, t + 1)
                rstd_tile(t)
                dve.tensor_scalar(XN0[:, t, :], X[:, t, :], STAT[:, 3, t:t + 1], None, ALU.mult).then_inc(xn0, 1)
            dve.wait_ge(banks_act, act_after("params"))
            turned("h_t.0", 0, "norm_g", 0)
            split(2)
            turned("h_t.1", 4, "norm_g", 0)
            split(2)
            dve.wait_ge(lam_den, 1)
            dve.reciprocal(LS[:, 18, :], LS[:, 17, :]).then_inc(lam_rec, 1)
            split()
            split()
            split()
            for t in range(TT):
                dve.wait_ge(banks_act, act_after("a_v.1", t + 1))
                for u in range(2):
                    seq.inc(dve.bn_stats(BNS[:, t, u, :], V[:, t, u * NC:(u + 1) * NC]))
                seq.wait()
                dve.bn_aggr(BNA[:, t, :], BNS[:, t, :, :]).then_inc(v_std, 1)
            split()
            dve.wait_ge(v_std, 5)
            seq.inc(dve.reciprocal(STAT[:, 3, :], STAT[:, 2, :]))
            seq.wait()
            dve.wait_ge(ln_in, 32)
            n = [seq.inc(dve.tensor_scalar(V[:, t, :], V[:, t, :], BNA[:, t, 0:1], STAT[:, 3, t:t + 1],
                                           ALU.subtract, ALU.mult)) for t in range(TT)]
            for t in range(TT):
                seq.wait(n[t])
                n[t] = seq.inc(dve.tensor_tensor(V[:, t, :], V[:, t, :], LNROWS[:, 0, :], ALU.mult))
            split()
            for t in range(TT):
                seq.wait(n[t])
                dve.tensor_tensor(V[:, t, :], V[:, t, :], LNROWS[:, 1, :], ALU.add).then_inc(v_done, 1)
            times_tmp([("a_z.0", m, U[:, m, :]) for m in range(4)])
            split()
            times_tmp([("a_z.1", m, U[:, 4 + m, :]) for m in range(4)])
            dve.wait_ge(pool_t, 1)
            dve.wait_ge(consts, 4)
            for i in range(4):
                done(f"w_t.{i}")
                for ri in range(2):
                    dve.tensor_copy(WTS[64:P, ri, 8 * i:8 * i + 8, :],
                                    bank(f"w_t.{i}", 2 * ri + 1)[64:P, :].rearrange("p (r n) -> p r n", r=8)).then_inc(banks_dve, 1)
            split()
            split()
            for i in range(2):
                dve.wait_ge(banks_act, act_after(f"k.{i}"))
                tm = TM[:, 16 * i:16 * i + 16, :].rearrange("p r (t q) -> p r t q", q=S5_GROUP)
                for lag in range(T4):
                    if lag:
                        seq.wait()
                    for t in range(lag, T4):
                        o = dve.scalar_tensor_tensor(tm[:, :, t, :], KS[:, :, lag, :], MJ[:, t - lag:t - lag + 1],
                                                     tm[:, :, t, :], ALU.mult, ALU.add)
                        if lag == T4 - 1:
                            o.then_inc(lagged, 1)
                        else:
                            seq.inc(o)
            dve.wait_ge(bs_in, 16)
            dve.wait_ge(tmp_free, 8)

            def sgu_out(i):
                done(f"sgu.{i}")
                for m in range(4):
                    g = 4 * i + m
                    dve.tensor_tensor(TMP[:, m % 2, :].rearrange("p (n i) -> p n i", i=P),
                                      bank(f"sgu.{i}", m).rearrange("p (n i) -> p n i", i=P),
                                      SGB[:, g, :].unsqueeze(1).to_broadcast([P, TT, P]), ALU.add).then_inc(banks_dve, 1)
                    dve.wait_ge(banks_dve, dve_after(f"sgu.{i}", m + 1))
                    dve.tensor_tensor(U[:, g, :], U[:, g, :], TMP[:, m % 2, :], ALU.mult).then_inc(ya_ready, 1)

            sgu_out(0)
            sgu_out(1)
            dve.wait_ge(ya_ready, 8)
            y_low(0, lambda kt: U[:, kt, :], range(8))
            split()
            split()
            dve.wait_ge(pads, 2)
            dve.wait_ge(consts, 4 + PPAD)

            def windows(k):
                w = POOL_WINDOWS[k]
                for kt in (2 * k, 2 * k + 1):
                    dve.wait_ge(banks_act, act_after(f"b_p.{kt // 4}", kt % 4 + 1))
                    src, step = CH[:, kt, :], 1
                    slot = 0
                    while step < w:
                        seq.inc(dve.tensor_tensor(WIN[:, slot, PPAD:], src[:, PPAD:], src[:, PPAD - step:PPAD - step + SEQ], ALU.add))
                        src, slot, step = WIN[:, slot, :], slot ^ 1, 2 * step
                        seq.wait()
                    seq.inc(dve.tensor_tensor(WIN[:, 2, PPAD:PPAD + w], src[:, PPAD:PPAD + w], INVC[:, 0:w], ALU.mult))
                    seq.inc(dve.scalar_tensor_tensor(U[:, kt, w:], src[:, PPAD + w:], 1.0 / w, CH[:, kt, PPAD + w:],
                                                     ALU.mult, ALU.subtract))
                    seq.wait()
                    o = dve.tensor_tensor(U[:, kt, 0:w], WIN[:, 2, PPAD:PPAD + w], CH[:, kt, PPAD:PPAD + w], ALU.subtract)
                    if kt % 2:
                        o.then_inc(d_ready, 1)
                    else:
                        seq.inc(o)

            windows(0)
            windows(1)
            split()
            done("w_a.0")
            for m in range(4):
                dve.tensor_tensor(M[:, m, :], bank("w_a.0", m), G[:, m, :], ALU.mult).then_inc(banks_dve, 1)
            split()
            windows(2)
            done("w_a.1")
            for m in range(4):
                dve.tensor_tensor(M[:, 4 + m, :], bank("w_a.1", m), G[:, 4 + m, :], ALU.mult).then_inc(banks_dve, 1)
            windows(3)
            split()
            split()
            for i in range(2):
                done(f"pool.{i}")
                for m in range(4):
                    kt = 4 * i + m
                    if kt >= 2:
                        dve.wait_ge(yb_ready, kt - 1)
                    dve.tensor_scalar(TMP[:, m % 2, :], bank(f"pool.{i}", m), col("pool_b", kt), col("pool_scale", kt),
                                      ALU.add, ALU.mult).then_inc(banks_dve, 1)
                    dve.wait_ge(banks_dve, dve_after(f"pool.{i}", m + 1))
                    if m == 0:
                        dve.wait_ge(banks_act, act_after(f"b_z.{i}"))
                    dve.tensor_tensor(CH[:, kt, PPAD:], CH[:, kt, PPAD:], TMP[:, m % 2, :], ALU.mult).then_inc(yb_ready, 1)
            dve.wait_ge(yb_ready, 8)
            y_low(1, lambda kt: CH[:, kt, PPAD:], range(8))
            split()
            split()
            split()
            split()

            def merge(job, u, version=None):
                done(job)
                for m in range(4):
                    kt = 4 * u + m
                    dve.tensor_tensor(TMP[:, m % 2, :], bank(job, m), G[:, kt, :], ALU.mult).then_inc(banks_dve, 1)
                    dve.wait_ge(banks_dve, dve_after(job, m + 1))
                    dve.tensor_tensor(M[:, kt, :], M[:, kt, :], TMP[:, m % 2, :], ALU.add).then_inc(m_acc, 1)
                    if version and m:
                        h_low(version, lambda kt: M[:, kt, :], [kt - 1])
                if version:
                    h_low(version, lambda kt: M[:, kt, :], [4 * u + 3])

            split()
            dve.wait_ge(banks_act, act_after("g1.1"))
            dve.wait_ge(banks_dve, dve_after("w_a.1"))
            merge("w_b.0", 0)
            split()
            merge("w_b.1", 1)
            for u in range(2):
                split()
                done(f"c_c.{u}")
                dve.wait_ge(banks_act, act_after(f"c_h.{u}"))
                for m in range(4):
                    kt = 4 * u + m
                    dve.tensor_tensor(CH[:, kt, PPAD:], bank(f"c_c.{u}", m), CH[:, kt, PPAD:], ALU.mult).then_inc(banks_dve, 1)
                dve.wait_ge(side_done, side_after("pool.1"))
                for m in range(4):
                    kt = 4 * u + m
                    dve.wait_ge(banks_dve, dve_after(f"c_c.{u}", m + 1))
                    seq.inc(dve.tensor_scalar(U[:, kt, :], CH[:, kt, PPAD:], col("conv_w2", kt), col("conv_b", kt), ALU.mult, ALU.add))
                for k, s in ((1, 1), (0, 2)):
                    first = seq.n - 3
                    for m in range(4):
                        kt = 4 * u + m
                        seq.wait(first + m)
                        seq.inc(dve.scalar_tensor_tensor(U[:, kt, :], CH[:, kt, PPAD - s:PPAD - s + SEQ], col(f"conv_w{k}", kt),
                                                         U[:, kt, :], ALU.mult, ALU.add))
            split()
            split()
            split()
            seq.wait()
            for u in range(2):
                done(f"c_b.{u}")
                for m in range(4):
                    kt = 4 * u + m
                    dve.tensor_tensor(U[:, kt, :], bank(f"c_b.{u}", m), U[:, kt, :], ALU.mult).then_inc(banks_dve, 1)
                split()
            for u in range(2):
                dve.wait_ge(banks_dve, dve_after(f"c_b.{u}"))
                times_tmp([(f"c_z.{u}", m, U[:, 4 * u + m, :]) for m in range(4)])
                y_low(2, lambda kt: U[:, kt, :], range(4 * u, 4 * u + 4))
                split()
            dve.wait_ge(banks_act, act_after("g2.1"))
            dve.wait_ge(m_acc, 8)
            merge("w_c.0", 0, 1)
            split()
            merge("w_c.1", 1, 1)
            split(3)
            dve.wait_ge(x_again, 16)
            done("w_out.0")
            for t in range(TT):
                dve.tensor_tensor(X[:, t, 0:NC], bank("w_out.0", t), X[:, t, 0:NC], ALU.add).then_inc(banks_dve, 1)
            split(1)
            dve.wait_ge(frow_in, 16)

            def x1_norm(t):
                dve.wait_ge(std2, t + 1)
                rstd_tile(t)
                dve.tensor_scalar(XN1[:, t, :], X[:, t, :], STAT[:, 3, t:t + 1], None, ALU.mult).then_inc(xn1, 1)

            for t in range(TT):
                tile_done("w_out.1", t, 0)
                dve.tensor_tensor(X[:, t, NC:D], bank("w_out.1", t), X[:, t, NC:D], ALU.add).then_inc(banks_dve, 1)
                if t:
                    x1_norm(t - 1)
                dve.wait_ge(std1, t + 1)
                rstd_tile(t)
                dve.scalar_tensor_tensor(X[:, t, :], X[:, t, :], STAT[:, 3, t:t + 1], FROW[:, :], ALU.mult, ALU.mult).then_inc(x1_done, 1)
            split(1)
            x1_norm(TT - 1)
            split(1)
            turned("u_t.0", 0, "norm_pre0", 2)
            split(2)
            turned("u_t.1", 4, "norm_pre0", 2)

            split()
            split()
            times_tmp([("b_gate.0", m, CP[:, m, CPAD:]) for m in range(4)], GATEV)
            dve.wait_ge(cpads, 1)

            def taps():
                for kt0 in range(0, KT, 2):
                    for k in range(CONV_K):
                        for s in range(2):
                            yield kt0 + s, k, s

            todo = list(taps())
            conv = {"i": 0}

            def step_ops():
                sv = S[:, :, PP:PAIRS, :].rearrange("p r g (s j) -> p r g s j", j=SEG_CH)
                w1, w2 = SEGV[:, 0], SEGV[:, 1]
                shape = [P, 2, PAIRS - PP, SEG]
                dve.wait_ge(states, 1)
                dve.wait_ge(banks_act, act_after("s5_z.3"))
                last = None
                for j in range(SEG_CH - 1):
                    now, nxt = sv[:, :, :, :, j], sv[:, :, :, :, j + 1]
                    if last:
                        seq.wait(last)
                    seq.inc(dve.tensor_tensor(w1, LAM[:, 0:1, PP:].unsqueeze(3).to_broadcast(shape), now, ALU.mult))
                    first = seq.n
                    yield
                    if last:
                        seq.wait(last)
                    seq.inc(dve.tensor_tensor(w2, LAM[:, 1:3, PP:].unsqueeze(3).to_broadcast(shape), now, ALU.mult))
                    second = seq.n
                    yield
                    seq.wait(first)
                    seq.inc(dve.tensor_tensor(nxt, nxt, w1, ALU.add))
                    third = seq.n
                    yield
                    seq.wait(max(second, third))
                    seq.inc(dve.tensor_tensor(nxt[:, 1:2], nxt[:, 1:2], w2[:, 0:1], ALU.add))
                    yield
                    seq.wait(max(second, third) if j < SEG_CH - 2 else None)
                    o = dve.tensor_tensor(nxt[:, 0:1], nxt[:, 0:1], w2[:, 1:2], ALU.add)
                    if j < SEG_CH - 2:
                        last = seq.inc(o)
                    else:
                        o.then_inc(dve_states, 1)
                    yield

            def convolve(n, steps=None):
                for kt, k, s in todo[conv["i"]:conv["i"] + n]:
                    w = PRM[:, 8 * (VEC_CONV + k) + kt:8 * (VEC_CONV + k) + kt + 1]
                    if k == 0:
                        if kt >= 2:
                            dve.wait_ge(conv_done, kt - 1)
                        conv[s] = seq.inc(dve.tensor_scalar(TMP[:, s, :], CP[:, kt, 0:SEQ], w, col("conv_b_2", kt), ALU.mult, ALU.add))
                    else:
                        seq.wait(conv[s])
                        last = k == CONV_K - 1
                        o = dve.scalar_tensor_tensor(CP[:, kt, CPAD:] if last else TMP[:, s, :], CP[:, kt, k:k + SEQ], w,
                                                     TMP[:, s, :], ALU.mult, ALU.add)
                        if last:
                            o.then_inc(conv_done, 1)
                        else:
                            conv[s] = seq.inc(o)
                    conv["i"] += 1
                    if steps:
                        next(steps, None)

            dve.wait_ge(tmp_free, 20)
            dve.wait_ge(m_acc, 16)
            def split_convolve(n, steps=None):
                for q in range(4):
                    convolve(n // 4, steps)
                    split(1)

            split_convolve(24)
            split_convolve(24)
            convolve(44)
            steps = step_ops()
            split_convolve(20, steps)
            split_convolve(12, steps)
            times_tmp([("b_gate.1", m, CP[:, 4 + m, CPAD:]) for m in range(4)], GATEV)
            dve.wait_ge(tmp_free, 24)
            split_convolve(20, steps)
            split_convolve(24, steps)
            for _ in steps:
                pass
            split_convolve(8)
            dve.wait_ge(carried, 1)
            for n, (b, ri) in enumerate(FIX_DVE):
                for q in range(2):
                    fix, into, by, end, op = correction(b, ri, q, 1)
                    seq.wait()
                    seq.inc(dve.tensor_tensor(fix, by, end, ALU.mult))
                    seq.wait()
                    o = dve.tensor_tensor(into, into, fix, op)
                    if q and n in (FIX_HALF - 1, len(FIX_DVE) - 1):
                        o.then_inc(fixed_dve, 1)
                        dve.wait_ge(fixed_dve, 1 + (n > FIX_HALF))
                    else:
                        seq.inc(o)
            split()
            convolve(24)

            for i in range(2):
                for m in range(4):
                    kt = 4 * i + m
                    dve.wait_ge(banks_act, act_after(f"y_t.{i}", m + 1))
                    dve.wait_ge(y_hi, 24 + kt + 1)
                    dve.tensor_tensor(YL[:, kt, :], YA[:, kt, :], YH[:, kt, :].bitcast(F32), ALU.subtract).then_inc(y_lo, 1)
                    convolve(1)
            dve.memset(ONES[:, :], 1.0 / D).then_inc(ones_in, 1)
            seq.wait()
            split_convolve(24)
            convolve(len(todo))
            for u in range(2):
                if u:
                    split()
                    h_low(3, lambda kt: YA[:, kt, :], range(4))
                dve.wait_ge(ya_gated, 4 * u + 4)
                times_tmp([(f"glu.{u}", m, YA[:, 4 * u + m, :]) for m in range(4)], GLUV)
            h_low(3, lambda kt: YA[:, kt, :], range(4, 8))
            done("mean")
            dve.tensor_copy(MU[:, :], bank("mean", 0)).then_inc(banks_dve, 1)
            dve.wait_ge(banks_dve, dve_after("mean"))
            dve.wait_ge(conv_done, 8)
            for kt in range(KT):
                dve.tensor_tensor(CP[:, kt, CPAD:], CP[:, kt, CPAD:], MU[:, :], ALU.subtract).then_inc(z_cent, 1)
            split()
            dve.wait_ge(banks_act, act_after("var"))
            seq.inc(dve.reciprocal(RS[:, :], RS[:, :]))
            seq.wait()
            dve.wait_ge(z_sq, 8)
            for kt in range(KT):
                dve.tensor_tensor(CP[:, kt, CPAD:], CP[:, kt, CPAD:], RS[:, :], ALU.mult).then_inc(z_norm, 1)
            y_low(4, lambda kt: CP[:, kt, CPAD:], range(8))
            split()
            split()
            for u in range(2):
                if u:
                    split()
                done(f"pw.{u}")
                if u == 0:
                    dve.wait_ge(banks_act, act_after("b_z2.1"))
                for m in range(4):
                    kt = 4 * u + m
                    dve.scalar_tensor_tensor(BZ[:, kt, :], bank(f"pw.{u}", m), col("b_pw", kt), BZ[:, kt, :],
                                             ALU.add, ALU.mult).then_inc(banks_dve, 1)
                h_low(4, lambda kt: BZ[:, kt, :], range(4 * u, 4 * u + 4))
            split(3)
            dve.wait_ge(ya_gated, 8)
            dve.memset(LWH[:, :, :].bitcast(F32), 0.0).then_inc(lw_zero, 1)
            dve.memset(LWL[:, :, :].bitcast(F32), 0.0).then_inc(lw_zero, 1)
            dve.wait_ge(banks_act, act_after("ev_a.1"))
            done("ev_b.0")
            for t in range(TT):
                dve.tensor_tensor(YO[:, t, 0:NC], bank("ev_b.0", t), YO[:, t, 0:NC], ALU.add).then_inc(banks_dve, 1)
            split(1)
            dve.wait_ge(prow0_in, 16)
            dve.wait_ge(x1_in, 16)

            def x2_norm(t):
                dve.wait_ge(std4, t + 1)
                rstd_tile(t)
                dve.tensor_scalar(XN2[:, t, :], X1[:, t, :], STAT[:, 3, t:t + 1], None, ALU.mult).then_inc(xn2, 1)

            for t in range(TT):
                tile_done("ev_b.1", t, TT - 1)
                dve.tensor_tensor(YO[:, t, NC:D], bank("ev_b.1", t), YO[:, t, NC:D], ALU.add).then_inc(banks_dve, 1)
                if t:
                    x2_norm(t - 1)
                dve.wait_ge(std3, t + 1)
                rstd_tile(t)
                seq.inc(dve.scalar_tensor_tensor(YO[:, t, :], YO[:, t, :], STAT[:, 3, t:t + 1], PROW0[:, :], ALU.mult, ALU.mult))
                seq.wait()
                dve.tensor_tensor(X1[:, t, :], X1[:, t, :], YO[:, t, :], ALU.add).then_inc(x2_done, 1)
            hsplit(N_STATIC, 0, 1)
            x2_norm(TT - 1)
            hsplit(N_STATIC, 1, 1)
            turned("u2_t.0", 0, "norm_pre1", 5)
            hsplit(N_STATIC, 2, 1)
            turned("u2_t.1", 4, "norm_pre1", 5)
            hsplit(N_STATIC, 3, 1)
            dve.wait_ge(lw_hi, 1)
            dve.tensor_tensor(LWL[:, :, 0:LOWRANK], LWR[:, :, :], LWH[:, :, 0:LOWRANK].bitcast(F32), ALU.subtract).then_inc(lw_lo, 1)

            dve.wait_ge(gla_consts, 1)
            A, B = [PS[:, m, :] for m in range(4)], [PS[:, 4 + m, :] for m in range(4)]

            hsplit(head_base(0), V_AT, 2)
            seq0 = seq.n

            def chunks4(v):
                return v.rearrange("p k (t c i) -> p k t c i", c=2, i=CHUNK)

            def head(h, last):
                n = head_base(h)
                seq.base, seq.n = h * HSEQ_DVE + seq0, 0
                hsplit(n, V_AT + 2, 2)
                for m in range(2):
                    dve.wait_ge(e_abs, h * 2 + (m + 1))
                    dve.scalar_tensor_tensor(ET[:, m, :], B[m], 0.0, ET[:, m, :], ALU.min, ALU.subtract).then_inc(g_read, 1)
                dve.wait_ge(g_read, h * 2 + 2)
                dve.tensor_tensor_scan(BC[:, :, :].rearrange("p k t -> p (k t)"), SMASK[:, :],
                                       ET[:, :, :].rearrange("p k t -> p (k t)"), 0.0, ALU.mult, ALU.add).then_inc(g_scan, 1)
                dve.wait_ge(e_q, h + 1)
                dve.wait_ge(qk_copied, h * 4 + 4)
                dve.scalar_tensor_tensor(QD[:, :, :], QK[:, 0:2, :], float(HK) ** -0.5, ET[:, :, :], ALU.mult, ALU.mult).then_inc(qd_done, 1)
                dve.wait_ge(e_ke, h + 1)
                dve.tensor_tensor(KE[:, :, :], QK[:, 2:4, :], ET[:, :, :], ALU.mult).then_inc(ke_done, 1)
                dve.wait_ge(g_scan, h * 2 + 1)
                b4 = BC[:, :, :].rearrange("p k (c t) -> p (k c) t", t=CHUNK)
                dve.tensor_tensor(KX[:, :, :].rearrange("p k (c t) -> p (k c) t", t=CHUNK),
                                  b4[:, :, CHUNK - 1:CHUNK].to_broadcast([P, 2 * GCH, CHUNK]), b4, ALU.subtract).then_inc(g_scan, 1)
                dve.wait_ge(dec_in, h + 1)
                dec = DEC[:, :, :].rearrange("p k (t c) -> p k t c", c=2)
                seq.inc(dve.tensor_tensor(DD[:, :, :], dec[:, :, :, 0], dec[:, :, :, 1], ALU.mult))
                dve.wait_ge(qd_done, h + 1)
                for k in range(2):
                    qd, qx = [v[:, k, :].rearrange("p (t c i) -> p t c i", c=2, i=CHUNK) for v in (QD, QX)]
                    seq.inc(dve.tensor_copy(qx[:, :, 0, :], qd[:, :, 0, :]))
                    seq.inc(dve.tensor_tensor(qx[:, :, 1, :], qd[:, :, 1, :],
                                              dec[:, k, :, 0:1].to_broadcast([P, TT, CHUNK]), ALU.mult))
                seq.wait(5)
                dve.memset(BNA[:, 0, 0:1], 0.0).then_inc(qx_done, 1)
                dve.wait_ge(e_d, h + 1)
                for k in range(2):
                    kr, et, kx = [v.rearrange("p (t c i) -> p t c i", c=2, i=CHUNK) for v in (QK[:, 2 + k, :], ET[:, k, :], KX[:, k, :])]
                    seq.inc(dve.tensor_tensor(KD1[:, k, :, :], kr[:, :, 0, :], et[:, :, 0, :], ALU.mult))
                    seq.inc(dve.tensor_tensor(kx[:, :, 1, :], kr[:, :, 1, :], et[:, :, 1, :], ALU.mult))
                for k in range(2):
                    seq.wait(6 + 2 * k)
                    kx = KX[:, k, :].rearrange("p (t c i) -> p t c i", c=2, i=CHUNK)
                    seq.inc(dve.tensor_tensor(kx[:, :, 0, :], KD1[:, k, :, :],
                                              dec[:, k, :, 1:2].to_broadcast([P, TT, CHUNK]), ALU.mult))
                seq.wait(11)
                dve.memset(BNA[:, 0, 1:2], 0.0).then_inc(kx_done, 1)
                hsplit(n, R_AT, 4)
                hsplit(n, QK_AT, 3)

                def scale_rr(m):
                    dve.tensor_scalar(RR[:, m, :], RR[:, m, :], col("gla_norm_g", m), None, ALU.mult).then_inc(rr_in, 1)

                dve.wait_ge(sc_out, h + 1)
                dve.wait_ge(r_copied, h * 4 + 1)
                scale_rr(0)
                for t in range(TT):
                    dve.copy_predicated(ATS[:, t, :], CMASK[:, :].bitcast(U32), A[2][:, t * P:(t + 1) * P]).then_inc(ats_copied, 1)
                dve.wait_ge(ats_copied, h * 5 + 4)
                dve.tensor_copy(ATS[0:CHUNK, :, CHUNK:P],
                                A[3][0:CHUNK, 0:TT * CHUNK].rearrange("p (t i) -> p t i", i=CHUNK)).then_inc(ats_copied, 1)
                for m in range(1, 4):
                    dve.wait_ge(r_copied, h * 4 + (m + 1))
                    scale_rr(m)
                hsplit(n, QK_AT + 3, 1)
                for t in range(TT - 1):
                    dve.wait_ge(d_out, h * 3 + (t + 1))
                    delta = PS[:, 4 + 2 * (t % 2):6 + 2 * (t % 2), :]
                    if t == 0:
                        dve.tensor_copy(ST[:, 0, :, :], delta).then_inc(st_done, 1)
                        continue
                    dve.wait_ge(st_done, h * HST + (2 * t - 1))
                    if t == 2:
                        dve.wait_ge(o_out, h * 4 + 2)
                    for k in range(2):
                        dve.scalar_tensor_tensor(ST[:, t % 2, k, :], ST[:, (t - 1) % 2, k, :], DD[:, k, t:t + 1], delta[:, k, :],
                                                 ALU.mult, ALU.add).then_inc(st_done, 1)
                dve.wait_ge(o_std, h + 1)
                seq.inc(dve.reciprocal(STAT[:, 3, :], STAT[:, 1, :]))
                seq.wait()
                for m in range(TT):
                    dve.tensor_scalar(ON[:, m, :], A[m], STAT[:, 3, m:m + 1], None, ALU.mult).then_inc(on_done, 1)
                if not last:
                    hsplit(n, out_at(last), 2)
                dve.wait_ge(rr_in, h * 4 + 4)
                for m in range(4):
                    dve.wait_ge(ot_out, h * 4 + (m + 1))
                    dve.tensor_tensor(RR[:, m, :], A[m], RR[:, m, :], ALU.mult).then_inc(o_f, 1)
                for m in range(4):
                    dve.wait_ge(o_hi, h * 4 + (m + 1))
                    dve.tensor_tensor(OL[:, m, :], RR[:, m, :], OH[:, m, :].bitcast(F32), ALU.subtract).then_inc(o_lo, 1)
                if not last:
                    hsplit(n, out_at(last) + 2, 2)
                dve.wait_ge(y2_zero, 1)
                dve.wait_ge(y2_add, h * 8 + 8)
                for u in range(2):
                    if u and not last:
                        hsplit(n, HEAD_CHUNKS + V_AT, 2)
                    dve.wait_ge(weights_used, n + (out_at(last) + 2 * (u + 1)))
                    for t in range(TT):
                        dve.tensor_tensor(YO2[:, t, u * NC:(u + 1) * NC], (B, A)[u][t], YO2[:, t, u * NC:(u + 1) * NC],
                                          ALU.add).then_inc(y2_add, 1)
                assert seq.n == HSEQ_DVE

            with dve.Fori(0, HEADS - 1) as h:
                head(h, False)
            head(HEADS - 1, True)
            seq.base, seq.n = 0, seq0 + HEADS * HSEQ_DVE

            dve.wait_ge(prow1_in, 16)
            for t in range(TT):
                dve.wait_ge(std5, t + 1)
                rstd_tile(t)
                seq.inc(dve.scalar_tensor_tensor(YO2[:, t, :], YO2[:, t, :], STAT[:, 3, t:t + 1], PROW1[:, :], ALU.mult, ALU.mult))
                seq.wait()
                dve.tensor_tensor(YO2[:, t, :], X1[:, t, :], YO2[:, t, :], ALU.add).then_inc(fin, 1)

        @block.tensor
        def _(pe):
            state = {"n": 0}

            def free(name):
                i = NAMES.index(name)
                if i < 2:
                    return
                prev = JOBS[i - 2]
                if _sum(3, i - 1):
                    pe.wait_ge(banks_act, _sum(3, i - 1))
                if _sum(4, i - 1):
                    pe.wait_ge(banks_dve, _sum(4, i - 1))
                if prev[5]:
                    pe.wait_ge(h_lo if prev[5][0] == "h" else y_lo, prev[5][1])

            halves = ((0, 0), (0, 1), (1, 0))

            def unit(n0, out_banks, acts, kt_ready, rows, tok=None, slot0=0, per=4, chunks=None, bank_ready=None,
                     by_tile=False):
                if by_tile:
                    for m in range(4):
                        for q in range(4):
                            if m == 0:
                                pe.wait_ge(w_lo, n0 + (q + 1))
                            for kk in range(2):
                                kt = 2 * q + kk
                                if m == 0:
                                    kt_ready(kt)
                                for i, (wi, ai) in enumerate(halves):
                                    mm = pe.matmul(out_banks[m], tok(acts(kt)[ai], m), (WH, WL)[wi][:, q, kk, :],
                                                   start=(kt == 0 and i == 0), stop=(kt == KT - 1 and i == 2))
                            if m == 3:
                                mm.then_inc(weights_used, 1)
                            elif q == 3:
                                mm.then_inc(tiles_done, 1)
                    return
                for q in chunks or range(per):
                    s = (slot0 + q) % RING
                    pe.wait_ge(w_lo, n0 + (q + 1))
                    for kk in range(2):
                        kt = 2 * q + kk
                        kt_ready(kt)
                        for m in range(4):
                            if bank_ready and kt == 0:
                                bank_ready(m)
                            for i, (wi, ai) in enumerate(halves):
                                w, x = (WH, WL)[wi], acts(kt)[ai]
                                if rows:
                                    st, mv = tok(x, m), w[:, s, kk, :]
                                else:
                                    st, mv = w[:, s, kk, m * P:(m + 1) * P], x
                                mm = pe.matmul(out_banks[m], st, mv, start=(kt == 0 and i == 0), stop=(kt == 2 * per - 1 and i == 2))
                    mm.then_inc(weights_used, 1)

            def tile(x, m):
                return x[:, m * P:(m + 1) * P]

            def strided(x, m):
                return x.rearrange("p (c j) -> p j c", j=T4)[:, m, :]

            def acts_of(hi, lo):
                return lambda kt: (hi[:, kt, :], lo[:, kt, :])

            def ready(s, version):
                return lambda kt: pe.wait_ge(s, 8 * version + min(kt, 7) + 1)

            H, Y = acts_of(HH, HL), acts_of(YH, YL)

            def section(name, acts, r, rows=False, tok=tile, per=4, units=(0, 1), by_tile=False):
                for u in units:
                    job = f"{name}.{u}"
                    free(job)
                    unit(chunks_before(job), [bank(job, m) for m in range(4)], acts, r if u == 0 else (lambda kt: None),
                         rows, tok, per=per, by_tile=by_tile and u == 1)

            def turn(job, srcs):
                free(job)
                for m, four in enumerate(srcs):
                    for t, (src, wait) in enumerate(four):
                        if wait:
                            wait()
                        mm = pe.transpose(bank(job, m)[:, t * P:(t + 1) * P], src, ident[:, :])
                    mm.then_inc(side_done, 1)

            def turn_tokens(job, x, kt0, s):
                turn(job, [[(x[:, t, (kt0 + m) * P:(kt0 + m + 1) * P], lambda t=t: pe.wait_ge(s, t + 1)) for t in range(TT)]
                           for m in range(4)])

            pe.wait_ge(consts, 4)
            pe.wait_ge(prm_in, 16 * 14)
            for i, n in enumerate((116, P, 8 * CONV_K - P)):
                mm = pe.transpose(bank("params", i)[:, 0:n], PR[0:n, i, :], ident[0:n, 0:n])
            mm.then_inc(side_done, 1)
            turn_tokens("h_t.0", XN0, 0, xn0)
            turn_tokens("h_t.1", XN0, 4, xn0)
            section("a_v", H, ready(h_lo, 0), rows=True)
            pe.wait_ge(c_in, 16 * 32)
            free("c_t")
            for i in range(2):
                for t in range(4):
                    mm = pe.transpose(bank("c_t", i)[:, t * P:(t + 1) * P], CRAW[:, i, t, :], ident[:, :])
            mm.then_inc(side_done, 1)
            section("a_u", H, ready(h_lo, 0))
            section("a_z", H, ready(h_lo, 0))
            pe.wait_ge(pool_w, 1)
            for i in range(4):
                free(f"w_t.{i}")
                for r in range(8):
                    for m in range(4):
                        ri, g = m // 2, m % 2
                        half = slice(64 * g, 64 * g + 64)
                        mm = pe.matmul(bank(f"w_t.{i}", m)[half, r * 64:(r + 1) * 64],
                                       WST[half, ri, 8 * i + r, :, :].rearrange("p j q -> p (j q)"), ident[half, half],
                                       start=True, stop=True)
                mm.then_inc(side_done, 1)
            pe.wait_ge(sgw_masked, 1)
            free("sgu_t")
            for g in range(SGU_GROUPS):
                mm = pe.transpose(bank("sgu_t", g // 4)[:, (g % 4) * P:(g % 4 + 1) * P], SGW[:, g, :], ident[:, :])
            mm.then_inc(side_done, 1)
            section("g0", H, ready(h_lo, 0))
            pe.wait_ge(pool_g, 1)
            pe.wait_ge(pool_rep, 2)
            for i in range(2):
                free(f"k.{i}")
                for r in range(8):
                    for m in range(4):
                        oc, g = 2 * i + m // 2, m % 2
                        pr, half = 8 * oc + r, slice(64 * g, 64 * g + 64)
                        for ri, lags in enumerate((GRE, GNI)):
                            mm = pe.matmul(bank(f"k.{i}", m)[half, r * 64:(r + 1) * 64],
                                           WST[half, ri, pr, :, :].rearrange("p j q -> p (j q)"),
                                           lags[half, pr, 0:T4, :].rearrange("p l q -> p (l q)"),
                                           start=(ri == 0), stop=(ri == 1))
                mm.then_inc(side_done, 1)
            pe.wait_ge(v_done, 4)
            for i in range(2):
                free(f"sgu.{i}")
                if i == 0:
                    pe.wait_ge(banks_act, act_after("sgu_t"))
                for m in range(4):
                    g = 4 * i + m
                    for t in range(TT):
                        mm = pe.matmul(bank(f"sgu.{i}", m)[:, t * P:(t + 1) * P], V[:, t, g * P:(g + 1) * P], SGWT[:, g, :],
                                       start=True, stop=True)
                mm.then_inc(side_done, 1)
            section("b_p", H, ready(h_lo, 0))
            section("w_a", Y, ready(y_lo, 0))
            section("b_z", H, ready(h_lo, 0))
            pe.wait_ge(pw_in, 16)
            for i in range(2):
                free(f"pool.{i}")
                for m in range(4):
                    kt = 4 * i + m
                    g = kt // 2
                    pe.wait_ge(d_ready, g + 1)
                    for k in range(2):
                        mm = pe.matmul(bank(f"pool.{i}", m), PW[:, g, k, (kt % 2) * P:(kt % 2 + 1) * P], U[:, 2 * g + k, :],
                                       start=(k == 0), stop=(k == 1))
                mm.then_inc(side_done, 1)
            section("g1", H, ready(h_lo, 0))
            section("c_h", H, ready(h_lo, 0))
            section("w_b", Y, ready(y_lo, 1))
            section("c_c", H, ready(h_lo, 0))
            section("g2", H, ready(h_lo, 0))
            section("c_b", H, ready(h_lo, 0))
            section("c_z", H, ready(h_lo, 0))
            section("w_c", Y, ready(y_lo, 2))
            section("w_out", H, ready(h_lo, 1), rows=True, by_tile=True)
            turn_tokens("u_t.0", XN1, 0, xn1)
            turn_tokens("u_t.1", XN1, 4, xn1)
            section("b_val", H, ready(h_lo, 2), units=(0,))
            section("b_gate", H, ready(h_lo, 2), units=(0,))
            section("a_in", H, ready(h_lo, 2), rows=True, tok=strided)
            for u in range(2):
                pe.wait_ge(banks_act, act_after(f"a_in.{u}"))
                free(f"s5_t.{u}")
                for m in range(4):
                    for r in range(4):
                        pr = 4 * m + r
                        mm = pe.transpose(bank(f"s5_t.{u}", m)[:, r * P:(r + 1) * P],
                                          AS[:, u, 2 * pr:2 * pr + 2, :, :].rearrange("c g j q -> c (g j q)"), ident[:, :])
                mm.then_inc(side_done, 1)
            pe.wait_ge(wt_in, 32)
            for i in range(4):
                free(f"s5_z.{i}")
                pe.wait_ge(banks_act, act_after("s5_t.0" if i < 2 else "s5_t.1"))
                for m in range(4):
                    for r in range(4):
                        pr = 8 * i + 4 * (m % 2) + r
                        mm = pe.matmul(bank(f"s5_z.{i}", m)[:, r * P:(r + 1) * P], WT[m // 2][:, pr, :], UT[:, pr, :],
                                       start=True, stop=True)
                mm.then_inc(side_done, 1)
            section("b_val", H, ready(h_lo, 2), units=(1,))
            section("b_gate", H, ready(h_lo, 2), units=(1,))
            section("a_z2", H, ready(h_lo, 2))
            section("b_z2", H, ready(h_lo, 2))
            for i in range(2):
                free(f"s5_y.{i}")
                pe.wait_ge(fixed_pool, i + 1)
                pe.wait_ge(fixed_dve, i + 1)
                pe.wait_ge(t6_in, 16 * (i + 1))
                pe.wait_ge(vt_in, 16 * (i + 1))
                for r in range(PAIRS // 2):
                    pr = 16 * i + r
                    o = bank(f"s5_y.{i}", r // 4)[:, (r % 4) * P:(r % 4 + 1) * P]
                    pe.matmul(o, UT[:, pr, :], T6[i][:, r, :], start=True, stop=False)
                    pe.matmul(o, S[:, 0, pr, :], VT[i][:, 0, r, :], start=False, stop=False)
                    mm = pe.matmul(o, S[:, 1, pr, :], VT[i][:, 1, r, :], start=False, stop=True)
                    if r % 4 == 3:
                        mm.then_inc(side_done, 1)
            for i in range(2):
                turn(f"y_t.{i}", [[(YT[:, t, (4 * i + m) * P:(4 * i + m + 1) * P],
                                    lambda m=m: pe.wait_ge(banks_act, act_after(f"s5_y.{i}", m + 1))) for t in range(T4)]
                                  for m in range(4)])
            section("glu", Y, ready(y_lo, 3))
            pe.wait_ge(ones_in, 1)
            pe.wait_ge(conv_done, 8)
            free("mean")
            for kt in range(KT):
                mm = pe.matmul(bank("mean", 0), ONES[:, :], CP[:, kt, CPAD:], start=(kt == 0), stop=(kt == KT - 1))
            mm.then_inc(side_done, 1)
            section("ev_a", H, ready(h_lo, 3), rows=True, units=(0,))
            free("var")
            for kt in range(KT):
                pe.wait_ge(z_sq, kt + 1)
                mm = pe.matmul(bank("var", 0), ONES[:, :], SQ[:, kt, :], start=(kt == 0), stop=(kt == KT - 1))
                mm.then_inc(sq_used, 1)
            section("ev_a", H, ready(h_lo, 3), rows=True, units=(1,))
            section("pw", Y, ready(y_lo, 4))
            section("ev_b", H, ready(h_lo, 4), rows=True, by_tile=True)
            turn_tokens("u2_t.0", XN2, 0, xn2)
            turn_tokens("u2_t.1", XN2, 4, xn2)
            A, B = [PS[:, m, :] for m in range(4)], [PS[:, 4 + m, :] for m in range(4)]
            nowait = lambda kt: None
            unit(N_STATIC, B, H, ready(h_lo, 5), False, chunks=(0, 1, 2),
                 bank_ready=lambda m: pe.wait_ge(h_lo, 40 + m + 1))
            pe.wait_ge(lw_lo, 1)
            pe.wait_ge(h_lo, 48)
            for kt in range(KT):
                for i, (wi, ai) in enumerate(halves):
                    mm = pe.matmul(A[0], (LWH, LWL)[wi][:, kt, :], (HH, HL)[ai][:, kt, :],
                                   start=(kt == 0 and i == 0), stop=(kt == KT - 1 and i == 2))
            mm.then_inc(lr_out, 1)
            unit(N_STATIC, B, H, nowait, False, chunks=(3,))
            pe.wait_ge(banks_act, act_after("lr"))

            def head(h, last):
                n = head_base(h)
                pe.wait_ge(gu_in, h * 32 + 32)
                pe.wait_ge(y2_add, h * 8 + 4)
                pe.wait_ge(qk_copied, h * 4 + 2)
                for m in range(2):
                    mm = pe.matmul(B[m], GU[0:LOWRANK + 1, m * P:(m + 1) * P], LR[0:LOWRANK + 1, :], start=True, stop=True)
                mm.then_inc(g_out, 1)
                pe.wait_ge(qk_copied, h * 4 + 4)
                unit(n + V_AT, A, H, nowait, True, tile, bank_ready=lambda m: pe.wait_ge(y2_add, h * 8 + (4 + m + 1)))
                pe.wait_ge(g_read, h * 2 + 2)
                unit(n + R_AT, B, H, nowait, False)
                pe.wait_ge(v_copied, h * 4 + 4)
                pe.wait_ge(kx_done, h + 1)
                for t in range(TT):
                    for k in range(2):
                        mm = pe.transpose(A[t // 2][:, ((t % 2) * 2 + k) * P:((t % 2) * 2 + k + 1) * P],
                                          KX[:, k, t * P:(t + 1) * P], ident[:, :])
                mm.then_inc(kt_out, 1)
                for t in range(TT):
                    for k in range(2):
                        pe.matmul(A[2][:, t * P:(t + 1) * P], KE[:, k, t * P:(t + 1) * P], QD[:, k, t * P:(t + 1) * P],
                                  start=(k == 0), stop=(k == 1))
                for t in range(TT):
                    for k in range(2):
                        mm = pe.matmul(A[3][0:CHUNK, t * CHUNK:(t + 1) * CHUNK], KD1[:, k, t, :],
                                       QD[:, k, t * P + CHUNK:(t + 1) * P], start=(k == 0), stop=(k == 1))
                mm.then_inc(sc_out, 1)

                def delta(t):
                    for k in range(2):
                        mm = pe.matmul(B[2 * (t % 2) + k], KTK[:, t, k, :], V2[:, t, :], start=True, stop=True)
                    mm.then_inc(d_out, 1)

                pe.wait_ge(r_copied, h * 4 + 4)
                pe.wait_ge(kt_copied, h * 2 + 2)
                delta(0)
                delta(1)
                pe.wait_ge(ats_copied, h * 5 + 5)
                for t in range(TT):
                    mm = pe.matmul(A[t], ATS[:, t, :], V2[:, t, :], start=True, stop=(t == 0), skip_group_check=True)
                    if t == 0:
                        mm.then_inc(o_out, 1)
                pe.wait_ge(st_done, h * HST + 1)
                delta(2)
                pe.wait_ge(qx_done, h + 1)
                for t in range(1, TT):
                    pe.wait_ge(st_done, h * HST + (2 * t - 1))
                    for k in range(2):
                        mm = pe.matmul(A[t], QX[:, k, t * P:(t + 1) * P], ST[:, (t - 1) % 2, k, :],
                                       start=False, stop=(k == 1), skip_group_check=True)
                    mm.then_inc(o_out, 1)
                if not last:
                    pe.wait_ge(st_done, h * HST + HST)
                    unit(n + QK_AT, B, H, nowait, False, chunks=(0, 1))
                pe.wait_ge(on_done, h * 4 + 4)
                for m in range(4):
                    for t in range(TT):
                        mm = pe.transpose(A[m][:, t * P:(t + 1) * P], ON[:, t, m * P:(m + 1) * P], ident[:, :])
                    mm.then_inc(ot_out, 1)
                if not last:
                    unit(n + QK_AT, B, H, nowait, False, chunks=(2, 3))
                O = acts_of(OH, OL)
                o_ready = lambda kt: pe.wait_ge(o_lo, h * 4 + (kt + 1))
                free_b = None if last else lambda m: pe.wait_ge(qk_copied, h * 4 + (4 + m + 1))
                if last:
                    pe.wait_ge(st_done, h * HST + HST)
                unit(n + out_at(last), B, O, o_ready, True, tile, slot0=0, per=2, bank_ready=free_b)
                pe.wait_ge(o_f, h * 4 + 4)
                unit(n + (out_at(last) + 2), A, O, nowait, True, tile, slot0=2, per=2)

            with pe.Fori(0, HEADS - 1) as h:
                head(h, False)
            head(HEADS - 1, True)


def kernel(**inputs):
    import numpy as _np
    import concourse.bacc as _bacc
    from concourse import mybir as _mybir
    from concourse.bass_utils import run_bass_kernel_spmd as _run

    nc = _bacc.Bacc("TRN2", target_bir_lowering=False, num_devices=1)
    arrays, args = {}, {}
    for name in inputs:
        v = _np.ascontiguousarray(inputs[name])
        arrays[f"in_{name}_dram"] = v
        args[name] = nc.dram_tensor(f"in_{name}_dram", v.shape, _mybir.dt.from_np(v.dtype), kind="ExternalInput").ap()
    out = nc.dram_tensor("out_0_dram", (1, SEQ, D), _mybir.dt.float32, kind="ExternalOutput").ap()
    three_branch_s5_gla_kernel(nc, args, out)
    r = _run(nc, [arrays], core_ids=[0])
    return r.results[0]["out_0_dram"]
```
